# Optimizing a Trainium2 kernel written in Bass

```python
import jax, jax.numpy as jnp
from jax import lax
import numpy as np
import math

D_MODEL = 1024
BATCH = 1
SEQ = 256
DEPTH = 2

HEAD_DIM = 64
A_Q_HEADS = 8
A_KV_HEADS = 2
A_BLOCK = 128
WINDOW = 128
ROPE_THETA = 10000.0
B_HEADS = 8
GRID_W = 64
NA_MAX_KH = 8
NA_KW = 16
NA_QBLOCK_W = 16
NA_SPAN_W = 2 * NA_KW
A_Q_DIM = A_Q_HEADS * HEAD_DIM
A_KV_DIM = A_KV_HEADS * HEAD_DIM
B_DIM = B_HEADS * HEAD_DIM
ATTN_IN = A_Q_DIM + 2 * A_KV_DIM + 3 * B_DIM
ATTN_OUT = A_Q_DIM + B_DIM
SSM_D_INNER = 2 * D_MODEL
SSM_HEAD_DIM = 64
SSM_HEADS = SSM_D_INNER // SSM_HEAD_DIM
SSM_GROUPS = 8
SSM_STATE = 128
SSM_CONV = 5
SSM_CHUNK = 128
SSM_CONV_DIM = SSM_D_INNER + 2 * SSM_GROUPS * SSM_STATE
SSM_IN = SSM_D_INNER + SSM_CONV_DIM + 2 * SSM_HEADS
D_FF = 4 * D_MODEL
DN_ALPHA = (2 * DEPTH) ** 0.25
DN_BETA = (8 * DEPTH) ** -0.25
LN_EPS = 1e-5
RMS_EPS = 1e-5
NEG_INF = -1e30
N_ATTN_LAYERS = (DEPTH + 1) // 2
N_SSM_LAYERS = DEPTH // 2


def layer_norm(x, g, b):
    xf = x.astype(jnp.float32)
    mu = jnp.mean(xf, -1, keepdims=True)
    var = jnp.mean(jnp.square(xf - mu), -1, keepdims=True)
    return ((xf - mu) * lax.rsqrt(var + LN_EPS)).astype(x.dtype) * g + b

def rope(x, pos):
    half = HEAD_DIM // 2
    inv = ROPE_THETA ** (-jnp.arange(half, dtype=jnp.float32) / half)
    ang = pos.astype(jnp.float32)[:, None] * inv[None, :]
    cos = jnp.cos(ang)[None, :, None, :].astype(x.dtype)
    sin = jnp.sin(ang)[None, :, None, :].astype(x.dtype)
    x1, x2 = x[..., :half], x[..., half:]
    return jnp.concatenate([x1 * cos - x2 * sin, x2 * cos + x1 * sin], axis=-1)

def windowed_gqa_sink(q, k, v, sink):
    bsz, t = q.shape[:2]
    nb = t // A_BLOCK
    rep = A_Q_HEADS // A_KV_HEADS
    qb = q.reshape(bsz, nb, A_BLOCK, A_KV_HEADS, rep, HEAD_DIM)

    def band(u):
        ub = u.reshape(bsz, nb, A_BLOCK, A_KV_HEADS, HEAD_DIM)
        up = jnp.pad(ub, ((0, 0), (1, 1), (0, 0), (0, 0), (0, 0)))
        return jnp.concatenate([up[:, :-2], up[:, 1:-1], up[:, 2:]], axis=2)

    kb, vb = band(k), band(v)
    s = jnp.einsum('bnqgrd,bnkgd->bngrqk', qb, kb).astype(jnp.float32) * (HEAD_DIM ** -0.5)
    qi = np.arange(A_BLOCK)[:, None] + A_BLOCK
    ki = np.arange(3 * A_BLOCK)[None, :]
    kabs = (np.arange(nb)[:, None, None] - 1) * A_BLOCK + ki[None]
    valid = (np.abs(qi - ki) <= WINDOW)[None] & (kabs >= 0) & (kabs < t)
    s = jnp.where(jnp.asarray(valid)[None, :, None, None], s, NEG_INF)
    sink_l = jnp.broadcast_to(sink.astype(jnp.float32).reshape(A_KV_HEADS, rep)[None, None, :, :, None, None],
                              s.shape[:-1] + (1,))
    p = jax.nn.softmax(jnp.concatenate([s, sink_l], axis=-1), axis=-1)[..., :-1]
    o = jnp.einsum('bngrqk,bnkgd->bnqgrd', p.astype(v.dtype), vb)
    return o.reshape(bsz, t, A_Q_DIM)

def _na_static():
    ncb = GRID_W // NA_QBLOCK_W
    starts = [min(max(j * NA_QBLOCK_W - NA_KW // 2, 0), GRID_W - NA_SPAN_W) for j in range(ncb)]
    c = np.arange(GRID_W).reshape(ncb, NA_QBLOCK_W)
    cs = np.clip(c - NA_KW // 2, 0, GRID_W - NA_KW)
    kc = np.array(starts)[:, None] + np.arange(NA_SPAN_W)[None, :]
    mask = (kc[:, None, :] >= cs[:, :, None]) & (kc[:, None, :] < cs[:, :, None] + NA_KW)
    dc = np.clip(kc[:, None, :] - c[:, :, None] + NA_KW - 1, 0, 2 * NA_KW - 2)
    return starts, mask, dc

def neighborhood_attention(q, k, v, rpb):
    bsz, t = q.shape[:2]
    rows = t // GRID_W
    kh = min(NA_MAX_KH, rows)
    ncb = GRID_W // NA_QBLOCK_W
    starts, mask, dc = _na_static()
    qg = q.reshape(bsz, rows, ncb, NA_QBLOCK_W, B_HEADS, HEAD_DIM)
    kg = k.reshape(bsz, rows, GRID_W, B_HEADS, HEAD_DIM)
    vg = v.reshape(bsz, rows, GRID_W, B_HEADS, HEAD_DIM)
    mask_j = jnp.asarray(mask)[:, :, None, :]
    scale = HEAD_DIM ** -0.5

    def row_step(r):
        rs = jnp.clip(r - kh // 2, 0, rows - kh)
        k_rows = lax.dynamic_slice_in_dim(kg, rs, kh, axis=1)
        v_rows = lax.dynamic_slice_in_dim(vg, rs, kh, axis=1)
        k_blk = jnp.stack([k_rows[:, :, s0:s0 + NA_SPAN_W] for s0 in starts], axis=1)
        v_blk = jnp.stack([v_rows[:, :, s0:s0 + NA_SPAN_W] for s0 in starts], axis=1)
        q_r = lax.dynamic_index_in_dim(qg, r, axis=1, keepdims=False)
        s = jnp.einsum('bjqhd,bjakhd->bhjqak', q_r, k_blk).astype(jnp.float32) * scale
        dr = rs + jnp.arange(kh) - r + NA_MAX_KH - 1
        bias = rpb[:, dr][:, :, dc].transpose(0, 2, 3, 1, 4)
        s = jnp.where(mask_j, s + bias.astype(jnp.float32), NEG_INF)
        p = jax.nn.softmax(s.reshape(s.shape[:-2] + (kh * NA_SPAN_W,)), axis=-1).reshape(s.shape)
        o = jnp.einsum('bhjqak,bjakhd->bjqhd', p.astype(v.dtype), v_blk)
        return o.reshape(bsz, GRID_W, B_DIM)

    out = lax.map(row_step, jnp.arange(rows))
    return out.transpose(1, 0, 2, 3).reshape(bsz, t, B_DIM)

def attention_mixer(x, w_in, sink, rpb, w_out):
    bsz, t, _ = x.shape
    h = x @ w_in
    qa, ka, va, qb, kb, vb = jnp.split(
        h, [A_Q_DIM, A_Q_DIM + A_KV_DIM, A_Q_DIM + 2 * A_KV_DIM,
            A_Q_DIM + 2 * A_KV_DIM + B_DIM, A_Q_DIM + 2 * A_KV_DIM + 2 * B_DIM], axis=-1)
    pos = jnp.arange(t)
    qa = rope(qa.reshape(bsz, t, A_Q_HEADS, HEAD_DIM), pos)
    ka = rope(ka.reshape(bsz, t, A_KV_HEADS, HEAD_DIM), pos)
    va = va.reshape(bsz, t, A_KV_HEADS, HEAD_DIM)
    oa = windowed_gqa_sink(qa, ka, va, sink)
    shp = (bsz, t, B_HEADS, HEAD_DIM)
    ob = neighborhood_attention(qb.reshape(shp), kb.reshape(shp), vb.reshape(shp), rpb)
    return jnp.concatenate([oa, ob], axis=-1) @ w_out

def depthwise_conv_centred(u, w, b):
    c = u.shape[-1]
    pad = SSM_CONV // 2
    out = lax.conv_general_dilated(u, w[:, None, :].astype(u.dtype), window_strides=(1,),
                                   padding=[(pad, pad)], dimension_numbers=('NWC', 'WIO', 'NWC'),
                                   feature_group_count=c)
    return out + b

def ssd_chunked(x, dt, a_neg, bm, cm):
    bsz, t = x.shape[:2]
    nc, L, G, R = t // SSM_CHUNK, SSM_CHUNK, SSM_GROUPS, SSM_HEADS // SSM_GROUPS
    x = x.astype(jnp.float32)
    dt = dt.astype(jnp.float32)
    xc = (x * dt[..., None]).reshape(bsz, nc, L, G, R, SSM_HEAD_DIM)
    a = (dt * a_neg.astype(jnp.float32)).reshape(bsz, nc, L, G, R).transpose(0, 1, 3, 4, 2)
    acum = jnp.cumsum(a, axis=-1)
    bc = bm.astype(jnp.float32).reshape(bsz, nc, L, G, SSM_STATE)
    cc = cm.astype(jnp.float32).reshape(bsz, nc, L, G, SSM_STATE)
    tri = jnp.tril(jnp.ones((L, L), dtype=bool))
    lmat = jnp.exp(jnp.where(tri, acum[..., :, None] - acum[..., None, :], -jnp.inf))
    cb = jnp.einsum('bclgn,bcsgn->bcgls', cc, bc)
    y_diag = jnp.einsum('bcgrls,bcsgrp->bclgrp', cb[:, :, :, None] * lmat, xc)
    decay_states = jnp.exp(acum[..., -1:] - acum)
    states = jnp.einsum('bcsgn,bcgrs,bcsgrp->bcgrpn', bc, decay_states, xc)
    chunk_decay = jnp.exp(acum[..., -1])

    def step(h, inp):
        st, dec = inp
        return h * dec[..., None, None] + st, h

    h0 = jnp.zeros((bsz, G, R, SSM_HEAD_DIM, SSM_STATE), jnp.float32)
    _, prev = lax.scan(step, h0, (jnp.moveaxis(states, 1, 0), jnp.moveaxis(chunk_decay, 1, 0)))
    prev = jnp.moveaxis(prev, 0, 1)
    y_off = jnp.einsum('bclgn,bcgrpn,bcgrl->bclgrp', cc, prev, jnp.exp(acum))
    return (y_diag + y_off).reshape(bsz, t, SSM_HEADS, SSM_HEAD_DIM)

def mamba2_bidir_mixer(x, w_in, conv_w, conv_b, dt_bias, a_log, d_skip, norm_w, w_out):
    bsz, t, _ = x.shape
    zxbcdt = x @ w_in
    z, xbc, dt = jnp.split(zxbcdt, [SSM_D_INNER, SSM_D_INNER + SSM_CONV_DIM], axis=-1)
    xbc = jax.nn.silu(depthwise_conv_centred(xbc, conv_w, conv_b))
    xs, bm, cm = jnp.split(xbc, [SSM_D_INNER, SSM_D_INNER + SSM_GROUPS * SSM_STATE], axis=-1)
    xs = xs.reshape(bsz, t, SSM_HEADS, SSM_HEAD_DIM)
    bm = bm.reshape(bsz, t, SSM_GROUPS, SSM_STATE)
    cm = cm.reshape(bsz, t, SSM_GROUPS, SSM_STATE)
    dt = jax.nn.softplus((dt + dt_bias).astype(jnp.float32))
    dt_f, dt_b = dt[..., :SSM_HEADS], dt[..., SSM_HEADS:]
    a_neg = -jnp.exp(a_log.astype(jnp.float32))
    y_f = ssd_chunked(xs, dt_f, a_neg[0], bm, cm)
    flip = lambda u: jnp.flip(u, axis=1)
    y_b = flip(ssd_chunked(flip(xs), flip(dt_b), a_neg[1], flip(bm), flip(cm)))
    y = (y_f + y_b).astype(x.dtype) + xs * d_skip[:, None]
    y = y.reshape(bsz, t, SSM_D_INNER) * jax.nn.silu(z)
    yg = y.astype(jnp.float32).reshape(bsz, t, SSM_GROUPS, SSM_D_INNER // SSM_GROUPS)
    yg = yg * lax.rsqrt(jnp.mean(jnp.square(yg), -1, keepdims=True) + RMS_EPS)
    y = yg.reshape(bsz, t, SSM_D_INNER).astype(x.dtype) * norm_w
    return y @ w_out

def squared_relu_mlp(x, w1, w2):
    return jnp.square(jax.nn.relu(x @ w1)) @ w2

def first_inputs(seed: int = 0) -> dict:
    key = jax.random.key(seed)
    ks = jax.random.split(key, 20)
    f32 = jnp.float32
    nrm = lambda k, shp, sc: jax.random.normal(k, shp, f32) * sc
    dt0 = jnp.exp(jax.random.uniform(ks[9], (N_SSM_LAYERS, 2 * SSM_HEADS), f32,
                                     jnp.log(1e-3), jnp.log(1e-1)))
    return {
        "x": nrm(ks[0], (BATCH, SEQ, D_MODEL), 1.0),
        "attn_w_in": nrm(ks[1], (N_ATTN_LAYERS, D_MODEL, ATTN_IN), D_MODEL ** -0.5),
        "attn_sink": nrm(ks[2], (N_ATTN_LAYERS, A_Q_HEADS), 1.0),
        "attn_rpb": nrm(ks[3], (N_ATTN_LAYERS, B_HEADS, 2 * NA_MAX_KH - 1, 2 * NA_KW - 1), 0.1),
        "attn_w_out": nrm(ks[4], (N_ATTN_LAYERS, ATTN_OUT, D_MODEL), ATTN_OUT ** -0.5 * DN_BETA),
        "ssm_w_in": nrm(ks[5], (N_SSM_LAYERS, D_MODEL, SSM_IN), D_MODEL ** -0.5),
        "ssm_conv_w": nrm(ks[6], (N_SSM_LAYERS, SSM_CONV, SSM_CONV_DIM), SSM_CONV ** -0.5),
        "ssm_conv_b": nrm(ks[7], (N_SSM_LAYERS, SSM_CONV_DIM), 0.02),
        "ssm_dt_bias": dt0 + jnp.log(-jnp.expm1(-dt0)),
        "ssm_A_log": jnp.log(jax.random.uniform(ks[10], (N_SSM_LAYERS, 2, SSM_HEADS), f32, 1.0, 16.0)),
        "ssm_D": 1.0 + nrm(ks[11], (N_SSM_LAYERS, SSM_HEADS), 0.05),
        "ssm_norm_w": 1.0 + nrm(ks[12], (N_SSM_LAYERS, SSM_D_INNER), 0.05),
        "ssm_w_out": nrm(ks[13], (N_SSM_LAYERS, SSM_D_INNER, D_MODEL), SSM_D_INNER ** -0.5 * DN_BETA),
        "mlp_w1": nrm(ks[14], (DEPTH, D_MODEL, D_FF), D_MODEL ** -0.5),
        "mlp_w2": nrm(ks[15], (DEPTH, D_FF, D_MODEL), D_FF ** -0.5 * DN_BETA),
        "ln1_g": 1.0 + nrm(ks[16], (DEPTH, D_MODEL), 0.05),
        "ln1_b": nrm(ks[17], (DEPTH, D_MODEL), 0.02),
        "ln2_g": 1.0 + nrm(ks[18], (DEPTH, D_MODEL), 0.05),
        "ln2_b": nrm(ks[19], (DEPTH, D_MODEL), 0.02),
    }

def first_block(x, attn_w_in, attn_sink, attn_rpb, attn_w_out, ssm_w_in, ssm_conv_w, ssm_conv_b,
              ssm_dt_bias, ssm_A_log, ssm_D, ssm_norm_w, ssm_w_out, mlp_w1, mlp_w2,
              ln1_g, ln1_b, ln2_g, ln2_b):
    for i in range(DEPTH):
        j = i // 2
        if i % 2 == 0:
            mix = attention_mixer(x, attn_w_in[j], attn_sink[j], attn_rpb[j], attn_w_out[j])
        else:
            mix = mamba2_bidir_mixer(x, ssm_w_in[j], ssm_conv_w[j], ssm_conv_b[j], ssm_dt_bias[j],
                                     ssm_A_log[j], ssm_D[j], ssm_norm_w[j], ssm_w_out[j])
        x = layer_norm(DN_ALPHA * x + mix, ln1_g[i], ln1_b[i])
        x = layer_norm(DN_ALPHA * x + squared_relu_mlp(x, mlp_w1[i], mlp_w2[i]), ln2_g[i], ln2_b[i])
    return x


EPS = 1e-6
BLOCK_Q = 128
RET_HEADS = 4
RET_DK = 64
RET_DV = 128
RET_CHUNK = 128
FOX_HEADS = 4
FOX_DH = 128
MLA_HEADS = 4
MLA_Q_RANK = 256
MLA_KV_RANK = 128
MLA_NOPE = 128
MLA_ROPE = 64
MLA_V = 128
N_BRANCH = 3
BRANCH_W = 512
N_GROUPS = 4
EXP_PER_GROUP = 8
N_EXPERTS = N_GROUPS * EXP_PER_GROUP
TOP_K = 2
D_EXPERT = 512
MOE_BLOCK = 128

IN_SIZES = (RET_HEADS * RET_DK, RET_HEADS * RET_DK, RET_HEADS * RET_DV, RET_HEADS * RET_DV,
            FOX_HEADS * FOX_DH, FOX_HEADS * FOX_DH, FOX_HEADS * FOX_DH, FOX_HEADS,
            MLA_Q_RANK, MLA_KV_RANK, MLA_ROPE)
IN_OFFSETS = tuple(sum(IN_SIZES[:i + 1]) for i in range(len(IN_SIZES) - 1))
D_IN = sum(IN_SIZES)


def rms_norm(x, g):
    xf = x.astype(jnp.float32)
    y = xf * lax.rsqrt(jnp.mean(xf * xf, axis=-1, keepdims=True) + EPS)
    return (y * g.astype(jnp.float32)).astype(x.dtype)

def modulate(h, shift, scale):
    return h * (1 + scale[:, None, :]) + shift[:, None, :]

def rope_2(x, positions):
    d = x.shape[-1]
    inv = ROPE_THETA ** (-jnp.arange(0, d, 2, dtype=jnp.float32) / d)
    ang = positions.astype(jnp.float32)[..., None] * inv
    cos = jnp.cos(ang)[:, :, None, :]
    sin = jnp.sin(ang)[:, :, None, :]
    xf = x.astype(jnp.float32)
    x1, x2 = xf[..., : d // 2], xf[..., d // 2:]
    return jnp.concatenate([x1 * cos - x2 * sin, x2 * cos + x1 * sin], axis=-1).astype(x.dtype)

def retention(q, k, v, g):
    B, S, H, dk = q.shape
    dv = v.shape[-1]
    C = RET_CHUNK
    N = S // C
    dt = q.dtype
    f32 = jnp.float32
    log_gamma = jnp.log1p(-jnp.exp2(-5.0 - jnp.arange(H, dtype=f32)))
    idx = jnp.arange(C, dtype=f32)
    rel = idx[:, None] - idx[None, :]
    dmask = jnp.where(rel >= 0, jnp.exp(log_gamma[:, None, None] * jnp.maximum(rel, 0.0)), 0.0)
    decay_in = jnp.exp(log_gamma[:, None] * (idx + 1.0))
    decay_out = jnp.exp(log_gamma[:, None] * (C - 1.0 - idx))
    decay_chunk = jnp.exp(log_gamma * C)
    qc = q.astype(f32).reshape(B, N, C, H, dk)
    kc = (k.astype(f32) * dk ** -0.5).reshape(B, N, C, H, dk)
    vc = v.astype(f32).reshape(B, N, C, H, dv)
    scores = jnp.einsum('bnchd,bnmhd->bhncm', qc, kc) * dmask[None, :, None]
    inner = jnp.einsum('bhncm,bnmhe->bnche', scores, vc)
    kv = jnp.einsum('bnmhd,hm,bnmhe->nbhde', kc, decay_out, vc)

    def step(state, kv_n):
        return state * decay_chunk[None, :, None, None] + kv_n, state

    _, s_prev = lax.scan(step, jnp.zeros((B, H, dk, dv), f32), kv)
    cross = jnp.einsum('bnchd,hc,nbhde->bnche', qc, decay_in, s_prev)
    o = (inner + cross).reshape(B, S, H, dv)
    mu = jnp.mean(o, axis=-1, keepdims=True)
    var = jnp.mean(jnp.square(o - mu), axis=-1, keepdims=True)
    o = ((o - mu) * lax.rsqrt(var + EPS)).reshape(B, S, H * dv)
    return (jax.nn.silu(g.astype(f32)) * o).astype(dt)

def blocked_causal_attention(q, k, v, log_f_cum=None):
    B, S, H, d = q.shape
    dv = v.shape[-1]
    NQ = S // BLOCK_Q
    scale = d ** -0.5
    kpos = jnp.arange(S)
    qb = q.reshape(B, NQ, BLOCK_Q, H, d).transpose(1, 0, 2, 3, 4)
    blk_ids = jnp.arange(NQ)
    use_forget = log_f_cum is not None
    if use_forget:
        fk = log_f_cum.transpose(0, 2, 1)
        fq = log_f_cum.reshape(B, NQ, BLOCK_Q, H).transpose(1, 0, 3, 2)
        xs = (qb, blk_ids, fq)
    else:
        xs = (qb, blk_ids)

    def body(args):
        qblk, bi = args[0], args[1]
        s = jnp.einsum('bqhd,bkhd->bhqk', qblk, k).astype(jnp.float32) * scale
        if use_forget:
            s = s + args[2][..., None] - fk[:, :, None, :]
        qpos = bi * BLOCK_Q + jnp.arange(BLOCK_Q)
        s = jnp.where(kpos[None, :] <= qpos[:, None], s, -jnp.inf)
        p = jax.nn.softmax(s, axis=-1)
        return jnp.einsum('bhqk,bkhe->bqhe', p.astype(v.dtype), v)

    out = lax.map(body, xs)
    return out.transpose(1, 0, 2, 3, 4).reshape(B, S, H * dv)

def token_mixer(h, positions, w_in, fox_fb, mla_q_norm_g, mla_wq_up, mla_kv_norm_g, mla_wkv_up,
                gate_w, gate_b, branch_w, out_w):
    B, S, D = h.shape
    proj = h @ w_in
    rq, rk, rv, rg, fq, fk, fv, ff, mq, mkv, mkr = jnp.split(proj, IN_OFFSETS, axis=-1)
    rq = rope_2(rq.reshape(B, S, RET_HEADS, RET_DK), positions)
    rk = rope_2(rk.reshape(B, S, RET_HEADS, RET_DK), positions)
    ya = retention(rq, rk, rv.reshape(B, S, RET_HEADS, RET_DV), rg)
    log_f = jax.nn.log_sigmoid((ff + fox_fb).astype(jnp.float32))
    f_cum = jnp.cumsum(log_f, axis=1)
    yb = blocked_causal_attention(fq.reshape(B, S, FOX_HEADS, FOX_DH),
                                  fk.reshape(B, S, FOX_HEADS, FOX_DH),
                                  fv.reshape(B, S, FOX_HEADS, FOX_DH), f_cum)
    qh = (rms_norm(mq, mla_q_norm_g) @ mla_wq_up).reshape(B, S, MLA_HEADS, MLA_NOPE + MLA_ROPE)
    q_nope, q_pe = qh[..., :MLA_NOPE], rope_2(qh[..., MLA_NOPE:], positions)
    kvh = (rms_norm(mkv, mla_kv_norm_g) @ mla_wkv_up).reshape(B, S, MLA_HEADS, MLA_NOPE + MLA_V)
    k_nope, v_c = kvh[..., :MLA_NOPE], kvh[..., MLA_NOPE:]
    k_pe = jnp.broadcast_to(rope_2(mkr[:, :, None, :], positions), (B, S, MLA_HEADS, MLA_ROPE))
    yc = blocked_causal_attention(jnp.concatenate([q_nope, q_pe], axis=-1),
                                  jnp.concatenate([k_nope, k_pe], axis=-1), v_c)
    gates = jax.nn.sigmoid((h @ gate_w + gate_b).astype(jnp.float32)).astype(h.dtype)
    gates = gates.reshape(B, S, N_BRANCH, D)
    merged = gates[:, :, 0] * (ya @ branch_w[0])
    merged = merged + gates[:, :, 1] * (yb @ branch_w[1])
    merged = merged + gates[:, :, 2] * (yc @ branch_w[2])
    return merged @ out_w

def hier_moe(h, w_grp, b_grp, w_exp, b_exp, w1, w3, w2):
    B, S, D = h.shape
    T = B * S
    f32 = jnp.float32
    t = h.reshape(T, D)
    tf = t.astype(f32)
    grp_p = jax.nn.softmax(tf @ w_grp.astype(f32) + b_grp.astype(f32), axis=-1)
    g_idx = jnp.argmax(grp_p, axis=-1)
    g_w = jnp.max(grp_p, axis=-1)
    exp_logits = (tf @ w_exp.astype(f32) + b_exp.astype(f32)).reshape(T, N_GROUPS, EXP_PER_GROUP)
    in_grp = jnp.take_along_axis(exp_logits, g_idx[:, None, None], axis=1)[:, 0]
    top_p, top_i = lax.top_k(jax.nn.softmax(in_grp, axis=-1), TOP_K)
    top_p = top_p / jnp.sum(top_p, axis=-1, keepdims=True)
    eid = (g_idx[:, None] * EXP_PER_GROUP + top_i).reshape(-1).astype(jnp.int32)
    wts = (g_w[:, None] * top_p).reshape(-1)
    tok = jnp.repeat(jnp.arange(T, dtype=jnp.int32), TOP_K)
    A = T * TOP_K
    order = jnp.argsort(eid)
    se, stok, sw = eid[order], tok[order], wts[order]
    counts = jnp.bincount(eid, length=N_EXPERTS)
    starts = jnp.cumsum(counts) - counts
    pcounts = (counts + MOE_BLOCK - 1) // MOE_BLOCK * MOE_BLOCK
    pends = jnp.cumsum(pcounts)
    pstarts = pends - pcounts
    dest = pstarts[se] + jnp.arange(A) - starts[se]
    n_blocks = -(-A // MOE_BLOCK) + N_EXPERTS
    P = n_blocks * MOE_BLOCK
    buf_tok = jnp.zeros((P,), jnp.int32).at[dest].set(stok)
    buf_w = jnp.zeros((P,), f32).at[dest].set(sw)
    blk_e = jnp.minimum(jnp.searchsorted(pends, jnp.arange(n_blocks) * MOE_BLOCK, side='right'),
                        N_EXPERTS - 1)

    def expert_block(args):
        tok_b, w_b, e = args
        xb = t[tok_b]
        hid = jax.nn.silu(xb @ w1[e]) * (xb @ w3[e])
        return (hid @ w2[e]) * w_b[:, None].astype(t.dtype)

    ys = lax.map(expert_block, (buf_tok.reshape(n_blocks, MOE_BLOCK),
                                buf_w.reshape(n_blocks, MOE_BLOCK), blk_e))
    out = jnp.zeros((T, D), t.dtype).at[buf_tok].add(ys.reshape(P, D))
    return out.reshape(B, S, D)

def second_inputs(seed: int = 0) -> dict:
    key = jax.random.key(seed)
    ks = jax.random.split(key, 26)
    L, D = DEPTH, D_MODEL
    f32 = jnp.float32

    def nrm(k, shape, fan_in, mult=1.0):
        return jax.random.normal(k, shape, f32) * (mult * fan_in ** -0.5)

    def gain(k, shape):
        return 1.0 + 0.05 * jax.random.normal(k, shape, f32)

    def small(k, shape, s=0.02):
        return s * jax.random.normal(k, shape, f32)

    positions = (jnp.arange(SEQ, dtype=jnp.int32)[None, :]
                 + jax.random.randint(ks[2], (BATCH, 1), 0, 1024, dtype=jnp.int32))
    return {
        "x": jax.random.normal(ks[0], (BATCH, SEQ, D), f32),
        "c": jax.random.normal(ks[1], (BATCH, D), f32),
        "positions": positions,
        "ada_w": nrm(ks[3], (L, D, 6 * D), D, 0.5),
        "ada_b": small(ks[4], (L, 6 * D)),
        "norm1_g": gain(ks[5], (L, D)),
        "norm2_g": gain(ks[6], (L, D)),
        "w_in": nrm(ks[7], (L, D, D_IN), D),
        "fox_fb": 1.0 + 0.5 * jax.random.normal(ks[8], (L, FOX_HEADS), f32),
        "mla_q_norm_g": gain(ks[9], (L, MLA_Q_RANK)),
        "mla_wq_up": nrm(ks[10], (L, MLA_Q_RANK, MLA_HEADS * (MLA_NOPE + MLA_ROPE)), MLA_Q_RANK),
        "mla_kv_norm_g": gain(ks[11], (L, MLA_KV_RANK)),
        "mla_wkv_up": nrm(ks[12], (L, MLA_KV_RANK, MLA_HEADS * (MLA_NOPE + MLA_V)), MLA_KV_RANK),
        "gate_w": nrm(ks[13], (L, D, N_BRANCH * D), D),
        "gate_b": small(ks[14], (L, N_BRANCH * D)),
        "branch_w": nrm(ks[15], (L, N_BRANCH, BRANCH_W, D), BRANCH_W),
        "out_w": nrm(ks[16], (L, D, D), D),
        "router_grp_w": nrm(ks[17], (L, D, N_GROUPS), D),
        "router_grp_b": small(ks[18], (L, N_GROUPS), 0.01),
        "router_exp_w": nrm(ks[19], (L, D, N_EXPERTS), D),
        "router_exp_b": small(ks[20], (L, N_EXPERTS), 0.01),
        "exp_w1": nrm(ks[21], (L, N_EXPERTS, D, D_EXPERT), D),
        "exp_w3": nrm(ks[22], (L, N_EXPERTS, D, D_EXPERT), D),
        "exp_w2": nrm(ks[23], (L, N_EXPERTS, D_EXPERT, D), D_EXPERT),
        "final_g": gain(ks[24], (D,)),
    }

def second_block(x, c, positions, ada_w, ada_b, norm1_g, norm2_g, w_in, fox_fb, mla_q_norm_g,
              mla_wq_up, mla_kv_norm_g, mla_wkv_up, gate_w, gate_b, branch_w, out_w,
              router_grp_w, router_grp_b, router_exp_w, router_exp_b, exp_w1, exp_w3, exp_w2,
              final_g):
    c_act = jax.nn.silu(c)
    for l in range(DEPTH):
        mod = c_act @ ada_w[l] + ada_b[l]
        sh1, sc1, gt1, sh2, sc2, gt2 = jnp.split(mod, 6, axis=-1)
        h = modulate(rms_norm(x, norm1_g[l]), sh1, sc1)
        mix = token_mixer(h, positions, w_in[l], fox_fb[l], mla_q_norm_g[l], mla_wq_up[l],
                          mla_kv_norm_g[l], mla_wkv_up[l], gate_w[l], gate_b[l], branch_w[l], out_w[l])
        x = x + gt1[:, None, :] * mix
        h = modulate(rms_norm(x, norm2_g[l]), sh2, sc2)
        ffn = hier_moe(h, router_grp_w[l], router_grp_b[l], router_exp_w[l], router_exp_b[l],
                       exp_w1[l], exp_w3[l], exp_w2[l])
        x = x + gt2[:, None, :] * ffn
    return rms_norm(x, final_g)


def setup_inputs(seed=0):
    out = dict(first_inputs(seed))
    for name, value in second_inputs(seed + 1).items():
        if name != "x":
            out[name + "_2"] = value
    return out


def reference(
    x, attn_w_in, attn_sink, attn_rpb, attn_w_out, ssm_w_in, ssm_conv_w, ssm_conv_b,
    ssm_dt_bias, ssm_A_log, ssm_D, ssm_norm_w, ssm_w_out, mlp_w1, mlp_w2, ln1_g, ln1_b, ln2_g,
    ln2_b, c_2, positions_2, ada_w_2, ada_b_2, norm1_g_2, norm2_g_2, w_in_2, fox_fb_2,
    mla_q_norm_g_2, mla_wq_up_2, mla_kv_norm_g_2, mla_wkv_up_2, gate_w_2, gate_b_2, branch_w_2,
    out_w_2, router_grp_w_2, router_grp_b_2, router_exp_w_2, router_exp_b_2, exp_w1_2, exp_w3_2,
    exp_w2_2, final_g_2,
):
    x = first_block(
        x, attn_w_in, attn_sink, attn_rpb, attn_w_out, ssm_w_in, ssm_conv_w, ssm_conv_b,
        ssm_dt_bias, ssm_A_log, ssm_D, ssm_norm_w, ssm_w_out, mlp_w1, mlp_w2, ln1_g, ln1_b,
        ln2_g, ln2_b,
    )
    return second_block(
        x, c_2, positions_2, ada_w_2, ada_b_2, norm1_g_2, norm2_g_2, w_in_2, fox_fb_2,
        mla_q_norm_g_2, mla_wq_up_2, mla_kv_norm_g_2, mla_wkv_up_2, gate_w_2, gate_b_2,
        branch_w_2, out_w_2, router_grp_w_2, router_grp_b_2, router_exp_w_2, router_exp_b_2,
        exp_w1_2, exp_w3_2, exp_w2_2, final_g_2,
    )


_drawn_inputs = setup_inputs


def setup_inputs(seed=0):
    import zlib

    import numpy as np

    out = dict(_drawn_inputs(seed))
    spreads = {}
    factors = {'attn_sink': 8.0,
     'attn_rpb': 5.934,
     'ssm_conv_b': 3.34,
     'ssm_D': 3.925,
     'mla_q_norm_g_2': 8.0,
     'mla_kv_norm_g_2': 5.379,
     'gate_b_2': 8.0,
     'router_grp_b_2': 5.941,
     'router_exp_b_2': 8.0}
    for name, (base, spread) in spreads.items():
        noise = np.random.default_rng([zlib.crc32(name.encode()), seed]).standard_normal(out[name].shape)
        drawn = base * np.exp(spread * noise) if base else spread * noise
        out[name] = __import__('jax').numpy.asarray(drawn.astype(out[name].dtype))
    for name, factor in factors.items():
        out[name] = (out[name] * factor).astype(out[name].dtype)
    return out
```

```python
from contextlib import ExitStack

import numpy as np
import concourse.bass as bass
from concourse import mybir

F32 = mybir.dt.float32
I32 = mybir.dt.int32
ALU = mybir.AluOpType
ACT = mybir.ActivationFunctionType
AX = mybir.AxisListType.X

P = 128
T = 256
D = 1024
NEG = -1e30
NRING = 4
SLAB = 4096
NE = 32
ALPHA = float(4 ** 0.25)


class Queues:

    def __init__(self, nc, ctx):
        self.nc, self.ctx = nc, ctx
        self.q = {"pe": [], "act": [], "dve": [], "pool": [], "sp": []}
        self.sem = {e: ctx.enter_context(nc.semaphore("s_" + e)) for e in ("pe", "act", "dve", "pool")}
        self.cnt = {e: 0 for e in self.sem}
        self.seen = {}

    def emit(self, e, fn, waits, inc=True):
        for w in flat(waits):
            key = (e, w[0])
            if self.seen.get(key, 0) < w[2]:
                self.seen[key] = w[2]
                self.q[e].append(("wait", w[1], w[2]))
        rec = ["op", fn, None, 0]
        self.q[e].append(rec)
        if inc:
            return self.done(e)
        return None

    def done(self, e):
        rec = self.q[e][-1]
        assert rec[0] == "op"
        if rec[2] is None:
            self.cnt[e] += 1
            rec[2], rec[3] = self.sem[e], 1
        return (e, self.sem[e], self.cnt[e])

    def all_done(self):
        out = []
        for e in ("pe", "act", "dve", "pool"):
            if self.q[e]:
                out.append(self.done(e))
        return out

    def run(self, e, eng):
        for rec in self.q[e]:
            if rec[0] == "wait":
                eng.wait_ge(rec[1], rec[2])
            else:
                ins = rec[1](eng)
                if rec[2] is not None:
                    ins.then_inc(rec[2], rec[3])


def flat(ws):
    out = []
    for w in ws:
        if w is None:
            continue
        if isinstance(w, tuple) and len(w) == 3 and isinstance(w[0], (str, int)):
            out.append(w)
        else:
            out.extend(flat(w))
    return out


class Rot:

    def __init__(self, bufs):
        self.bufs = bufs
        self.free = [[] for _ in bufs]
        self.held = [False] * len(bufs)
        self.i = -1

    def take(self):
        for _ in range(len(self.bufs)):
            self.i = (self.i + 1) % len(self.bufs)
            if not self.held[self.i]:
                self.held[self.i] = True
                return self.i, self.bufs[self.i], list(self.free[self.i])
        raise AssertionError("no free buffer")

    def give(self, i, *toks):
        self.free[i] = flat(toks)
        self.held[i] = False


class Arena:
    def __init__(self, ap, size):
        self.ap, self.size, self.pos, self.base = ap, size, 0, 0

    def get(self, *shape):
        n = 1
        for s in shape:
            n *= s
        a = self.ap[:, self.pos:self.pos + n]
        self.pos += n
        assert self.pos <= self.size, (self.pos, self.size)
        if len(shape) == 2:
            a = a.rearrange("p (a b) -> p a b", a=shape[0])
        if len(shape) == 3:
            a = a.rearrange("p (a b c) -> p a b c", a=shape[0], b=shape[1])
        return a


def build(nc, d, out, consts):
    with ExitStack() as ctx:
        Q = Queues(nc, ctx)

        def sb(name, shape, dt=F32):
            return ctx.enter_context(nc.sbuf_tensor(name, shape, dt))

        psb = [ctx.enter_context(nc.psum_tensor(f"ps{i}", [P, 512], F32)) for i in range(8)]
        bank = Rot([p[:, :] for p in psb])
        ringt = sb("ring", [P, NRING * SLAB])
        ring = Rot([ringt[:, i * SLAB:(i + 1) * SLAB] for i in range(NRING)])
        rsem = [ctx.enter_context(nc.semaphore(f"s_ring{i}")) for i in range(NRING)]
        ruse = [0] * NRING
        X = sb("X", [P, 2, D])[:, :, :]
        XT = sb("XT", [P, 8, T])[:, :, :]
        GB = sb("GB", [P, 2, D])[:, :, :]
        small = sb("small", [P, 512])[:, :]
        C = {}
        LATE = ("cm", "dmask", "rope2c", "rope2s")
        for name, arr in consts.items():
            if name in LATE:
                continue
            C[name] = sb("c_" + name, [P, arr])[:, :]
        ASZ = 27904
        arena = Arena(sb("arena", [P, ASZ])[:, :], ASZ)
        posi = sb("posi", [P, 2], I32)[:, :]
        NPD = 12
        psem = [ctx.enter_context(nc.semaphore(f"s_pd{i}")) for i in range(NPD)]
        puse = [0] * NPD
        pn = [0]
        osem = ctx.enter_context(nc.semaphore("s_out"))

        def mm(o, lhsT, rhs, start, stop, *w):
            Q.emit("pe", lambda e: e.matmul(o, lhsT=lhsT, rhs=rhs, start=start, stop=stop, skip_group_check=True), w, False)

        def tr(o, i, *w):
            n = i.shape[0]
            Q.emit("pe", lambda e: e.transpose(o, i, C["ident"][0:n, 0:n]), w, False)

        def pe_done():
            return Q.done("pe")

        def act(o, i, func, *w, bias=0.0, scale=1.0, acc=None):
            if acc is None:
                return Q.emit("act", lambda e: e.activation(o, i, func, bias=bias, scale=scale), w)
            return Q.emit("act", lambda e: e.activation(o, i, func, bias=bias, scale=scale, accum_out=acc), w)

        def ts(o, i, s1, s2, op0, op1, *w, e="dve"):
            if s2 is None:
                return Q.emit(e, lambda g: g.tensor_scalar(o, i, s1, None, op0), w)
            return Q.emit(e, lambda g: g.tensor_scalar(o, i, s1, s2, op0, op1), w)

        def stt(o, i0, s, i1, op0, op1, *w):
            return Q.emit("dve", lambda g: g.scalar_tensor_tensor(out=o, in0=i0, scalar=s, in1=i1, op0=op0, op1=op1), w)

        def tt(o, a, b, op, *w, e="dve"):
            return Q.emit(e, lambda g: g.tensor_tensor(o, a, b, op), w)

        def cp(o, i, *w, e="dve"):
            if e == "act":
                return Q.emit(e, lambda g: g.copy(o, i), w)
            return Q.emit(e, lambda g: g.tensor_copy(o, i), w)

        def red(o, i, op, *w):
            return Q.emit("dve", lambda g: g.tensor_reduce(o, i, AX, op), w)

        def recip(o, i, *w):
            return Q.emit("dve", lambda g: g.reciprocal(o, i), w)

        def mset(o, v, *w, e="pool"):
            return Q.emit(e, lambda g: g.memset(o, v), w)

        def pdma(o, i, *w):
            k = pn[0] % NPD
            pn[0] += 1
            prev = (f"pd{k}", psem[k], 16 * puse[k])
            puse[k] += 1
            for x in flat([w, prev] if puse[k] > 1 else [w]):
                key = ("pool", x[0])
                if Q.seen.get(key, 0) < x[2]:
                    Q.seen[key] = x[2]
                    Q.q["pool"].append(("wait", x[1], x[2]))
            sem = psem[k]
            Q.q["pool"].append(["dma", lambda e: e.dma_start(o, i).then_inc(sem, 16), None, 0])
            return (f"pd{k}", psem[k], 16 * puse[k])

        def load(src, kc, n):
            i, buf, free = ring.take()
            for x in flat(free):
                key = ("sp", x[0])
                if Q.seen.get(key, 0) < x[2]:
                    Q.seen[key] = x[2]
                    Q.q["sp"].append(("wait", x[1], x[2]))
            ruse[i] += 1
            dst = buf[:, 0:kc * n]
            sem = rsem[i]
            Q.q["sp"].append(["dma", lambda e: e.dma_start(dst, src).then_inc(sem, 16), None, 0])
            view = dst.rearrange("p (c n) -> p c n", c=kc)
            return i, view, ("r%d" % i, rsem[i], 16 * ruse[i])

        def slab(name, off, kc, n):
            src = d[name][off:off + P * kc * n].rearrange("(p f) -> p f", p=P)
            return load(src, kc, n)

        def gemm_t(xt, w, tok, n, evac, kcs=8, *extra):
            for t in range(2):
                b, ps, fr = bank.take()
                for c in range(kcs):
                    mm(ps[:, 0:n], xt[:, c, t * P:(t + 1) * P], w[:, c, 0:n], c == 0, c == kcs - 1, fr, tok, extra)
                bank.give(b, evac(t, ps[:, 0:n], pe_done()))

        def gemm_f(xt, w, tok, nf, evac, kcs=8, *extra):
            for f in range(0, nf, 2):
                b, ps, fr = bank.take()
                for j in range(2):
                    for c in range(kcs):
                        mm(ps[:, j * T:(j + 1) * T], w[:, c, (f + j) * P:(f + j + 1) * P], xt[:, c, :],
                           c == 0, c == kcs - 1, fr, tok, extra)
                bank.give(b, evac(f // 2, ps[:, :].rearrange("p (a b) -> p a b", a=2), pe_done()))

        flip = [0]

        def copy_any(o, i, *w):
            flip[0] ^= 1
            return cp(o, i, *w, e="act" if flip[0] else "dve")

        def transpose_to(dst, src_of, n, t, toks, extra=()):
            last = []
            for c0 in range(0, n, 4):
                m = min(4, n - c0)
                b, ps, fr = bank.take()
                for j in range(m):
                    tr(ps[:, j * P:(j + 1) * P], src_of(c0 + j), fr, toks, extra)
                k = copy_any(dst[:, c0:c0 + m, t * P:(t + 1) * P],
                             ps[:, 0:m * P].rearrange("p (a b) -> p a b", a=m), pe_done(), extra)
                bank.give(b, k)
                last.append(k)
            return last

        def rsqrt_small(o, i, mul, eps, *w):
            k = ts(o, i, mul, eps, ALU.mult, ALU.add, *w)
            n = o.shape[-1]
            return tt(o, o, C["half"][:, 0:n], ALU.pow, k, e="pool")

        def barrier():
            toks = Q.all_done()
            for e in ("pe", "act", "dve", "pool"):
                for x in toks:
                    key = (e, x[0])
                    if Q.seen.get(key, 0) < x[2]:
                        Q.seen[key] = x[2]
                        Q.q[e].append(("wait", x[1], x[2]))
            arena.pos = arena.base
            return toks

        def all_done():
            out_ = []
            for e in ("pe", "act", "dve", "pool"):
                for rec in reversed(Q.q[e]):
                    if rec[0] == "op":
                        if rec[2] is None:
                            Q.cnt[e] += 1
                            rec[2], rec[3] = Q.sem[e], 1
                        break
                if Q.cnt[e]:
                    out_.append((e, Q.sem[e], Q.cnt[e]))
            return out_
        Q.all_done = all_done

        def to_xt(toks):
            xv = X.rearrange("p t (q c) -> p t q c", c=8)
            out_ = []
            for t in range(2):
                out_ += transpose_to(XT, lambda c, t=t: xv[:, t, :, c], 8, t, toks)
            return out_

        def layer_norm(toks, ptok):
            st = small[:, 0:24].rearrange("p (t a b) -> p t a b", t=2, a=2)
            mv = small[:, 24:28].rearrange("p (t a) -> p t a", t=2)
            rs = small[:, 28:30]
            ks = []
            for t in range(2):
                kk = []
                for h in range(2):
                    o, i = st[:, t, h, :], X[:, t, h * 512:(h + 1) * 512]
                    kk.append(Q.emit("dve", lambda e, o=o, i=i: e.bn_stats(o, i), [toks]))
                o, i = mv[:, t, :], st[:, t, :, :]
                ks.append(Q.emit("dve", lambda e, o=o, i=i: e.bn_aggr(o, i), kk))
            k = rsqrt_small(rs, mv[:, :, 1], 1.0, 1e-5, ks)
            out_ = []
            xv = X.rearrange("p t (q c) -> p t q c", c=8)
            for t in range(2):
                a = ts(X[:, t, :], X[:, t, :], mv[:, t, 0:1], rs[:, t:t + 1], ALU.subtract, ALU.mult, k)
                a = tt(X[:, t, :], X[:, t, :], GB[:, 0, :], ALU.mult, a, ptok)
                a = tt(X[:, t, :], X[:, t, :], GB[:, 1, :], ALU.add, a)
                out_ += transpose_to(XT, lambda c, t=t: xv[:, t, :, c], 8, t, a)
            return out_

        def bcast(src):
            return src.partition_broadcast(P)

        def mlp(l, xtok):
            arena.pos = 0
            hT = arena.get(32, T)
            hk = []
            for s in range(8):
                r, w, tok = slab("mlp_w1", (l * 8 + s) * P * SLAB, 8, 512)

                def ev(fp, ps, k, s=s):
                    h = hT[:, 4 * s + 2 * fp:4 * s + 2 * fp + 2, :]
                    a = act(h, ps, ACT.Relu, k)
                    hk.append(tt(h, h, h, ALU.mult, a))
                    return a
                gemm_f(XT, w, tok, 4, ev, 8, xtok)
                ring.give(r, pe_done())
            bs = [bank.take() for _ in range(4)]
            for s in range(8):
                r, w, tok = slab("mlp_w2", (l * 8 + s) * P * SLAB, 4, 1024)
                for t in range(2):
                    for n in range(2):
                        b, ps, fr = bs[t * 2 + n]
                        for c in range(4):
                            mm(ps, hT[:, 4 * s + c, t * P:(t + 1) * P], w[:, c, n * 512:(n + 1) * 512],
                               s == 0 and c == 0, s == 7 and c == 3, fr, tok, hk[2 * s:2 * s + 2])
                ring.give(r, pe_done())
            k = pe_done()
            out_ = []
            for t in range(2):
                for n in range(2):
                    b, ps, fr = bs[t * 2 + n]
                    x = X[:, t, n * 512:(n + 1) * 512]
                    a = stt(x, x, ALPHA, ps, ALU.mult, ALU.add, k)
                    bank.give(b, a)
                    out_.append(a)
            return out_

        def residual_gemm(name, lay, lt, ltok, evac, off0=0):
            ns, kc, n = lay
            if kc == 8:
                for s in range(ns):
                    r, w, tok = slab(name, off0 + s * P * SLAB, 8, 512)
                    gemm_t(lt, w, tok, 512, lambda t, ps, k, s=s: evac(t, s, ps, k), 8, ltok)
                    ring.give(r, pe_done())
            else:
                bs = [bank.take() for _ in range(4)]
                for s in range(ns):
                    r, w, tok = slab(name, off0 + s * P * SLAB, 4, 1024)
                    for t in range(2):
                        for n_ in range(2):
                            b, ps, fr = bs[t * 2 + n_]
                            for c in range(4):
                                mm(ps, lt[:, 4 * s + c, t * P:(t + 1) * P], w[:, c, n_ * 512:(n_ + 1) * 512],
                                   s == 0 and c == 0, s == ns - 1 and c == 3, fr, tok, ltok)
                    ring.give(r, pe_done())
                k = pe_done()
                for t in range(2):
                    for n_ in range(2):
                        b, ps, fr = bs[t * 2 + n_]
                        bank.give(b, evac(t, n_, ps, k))

        def rope(ps, nh, ctab, stab, outs, tmp, tmpfree, *w):
            n = nh * 64
            a = tmp[:, 0:n].rearrange("p (h x) -> p h x", h=nh)
            b = tmp[:, n:2 * n].rearrange("p (h x) -> p h x", h=nh)
            cb = ctab.unsqueeze(1).to_broadcast([P, nh, 64])
            s1 = stab[:, 0:32].unsqueeze(1).to_broadcast([P, nh, 32])
            s2 = stab[:, 32:64].unsqueeze(1).to_broadcast([P, nh, 32])
            k1 = tt(a, ps, cb, ALU.mult, tmpfree, *w)
            k2 = tt(b[:, :, 0:32], ps[:, :, 32:64], s1, ALU.mult, tmpfree, *w)
            k3 = tt(b[:, :, 32:64], ps[:, :, 0:32], s2, ALU.mult, tmpfree, *w)
            ks = [tt(o, a, b, ALU.add, k1, k2, k3) for o in outs]
            return [k1, k2, k3], ks

        def attention(n, heads, sc, pr, ptb, st):
            S = {}

            def scores(h):
                H = heads(h)
                b, ps, fr = bank.take()
                H["mm"](ps, fr)
                k = pe_done()
                i, s, sf = sc.take()
                n_ = H["width"]
                a = stt(s[:, 0:n_], ps[:, 0:n_], H["scale"], H["bias"], ALU.mult, ALU.add, k, sf, H.get("btok"))
                bank.give(b, a)
                q, sm, smf = st.take()
                rs = []
                for t in range(2):
                    o0, o1 = H["cols"][t]
                    rs.append(red(sm[:, t:t + 1], s[:, o0:o1], ALU.max, a, smf))
                sink = H.get("sink")
                if sink is not None:
                    x = sm[:, 0:2]
                    rs = [ts(x, x, sink, None, ALU.max, None, rs)]
                ng = ts(sm[:, 2:4], sm[:, 0:2], -1.0, None, ALU.mult, None, rs)
                es = []
                j, p_, pf = pr.take()
                for t in range(2):
                    o0, o1 = H["cols"][t]
                    es.append(act(p_[:, o0:o1], s[:, o0:o1], ACT.Exp, ng, pf, bias=sm[:, 2 + t:3 + t],
                                  acc=sm[:, 4 + t:5 + t]))
                    if sink is not None:
                        es.append(act(sm[:, 6 + t:7 + t], sink, ACT.Exp, ng, bias=sm[:, 2 + t:3 + t]))
                sc.give(i, es)
                if sink is not None:
                    es.append(tt(sm[:, 4:6], sm[:, 4:6], sm[:, 6:8], ALU.add, es))
                rc = recip(sm[:, 8:10], sm[:, 4:6], es)
                nk = []
                for t in range(2):
                    o0, o1 = H["cols"][t]
                    nk.append(ts(p_[:, o0:o1], p_[:, o0:o1], sm[:, 8 + t:9 + t], None, ALU.mult, None, rc))
                st.give(q, nk, es)
                S[h] = (H, j, p_, nk)

            def turn(h):
                H, j, p_, nk = S[h]
                b, ps, fr = bank.take()
                for (t, kc, c0) in H["blocks"]:
                    tr(ps[:, kc * T + t * P:kc * T + (t + 1) * P], p_[:, c0:c0 + P], fr, nk)
                k = pe_done()
                pr.give(j, k)
                m, pt, pf = ptb.take()
                if len(H["blocks"]) == 4:
                    kk = cp(pt, ps, k, pf, e="act")
                else:
                    kk = [cp(pt[:, 0:T], ps[:, 0:T], k, pf, e="act"), cp(pt[:, T + P:], ps[:, T + P:], k, pf, e="act")]
                bank.give(b, kk)
                S[h] = (H, m, pt, kk)

            def apply(h):
                H, m, pt, kk = S.pop(h)
                ptb.give(m, H["pv"](pt, kk))

            for i in range(n + 2):
                if i < n:
                    scores(i)
                if 1 <= i <= n:
                    turn(i - 1)
                if i >= 2:
                    apply(i - 2)

        def att_bufs():
            sc = Rot([arena.get(512) for _ in range(2)])
            pr = Rot([arena.get(512) for _ in range(3)])
            ptb = Rot([arena.get(512) for _ in range(2)])
            st = Rot([arena.get(16) for _ in range(3)])
            return sc, pr, ptb, st

        ct = {}
        for name in consts:
            if name not in ("half", "ones") + LATE:
                ct[name] = pdma(C[name], d["const_" + name])
        ct["half"] = mset(C["half"], -0.5)
        onesk = mset(C["ones"], 1.0)
        xl = pdma(X, d["x"].rearrange("(t p) f -> p t f", p=P))
        ctoks = list(ct.values()) + [onesk]
        gk = [pdma(GB[:, j, :], bcast(d[nm][0:1, :])) for j, nm in ((0, "ln1_g"), (1, "ln1_b"))]
        xtok = to_xt([xl, ctoks])

        arena.pos = 0
        qT = arena.get(4, T)
        kT = arena.get(2, T)
        qbT = arena.get(4, T)
        kbT = arena.get(4, T)
        vA = arena.get(2, P)
        vB = arena.get(2, 512)
        OT = arena.get(8, T)
        qtok = arena.get(2, 512)
        kdup = arena.get(2, 256)
        sinkb = arena.get(8)
        rot_tmp = arena.get(1024)
        sk = pdma(sinkb, bcast(d["attn_sink"][0:1, :]))
        ro = [[]]
        qk = [None, None]
        kk = [None, None]

        r, w, tok = slab("attn_w_in", 0, 8, 512)

        def ev(t, ps, k):
            reads, ks = rope(ps.rearrange("p (h x) -> p h x", h=8), 8, C["ropec"][:, t * 64:t * 64 + 64],
                             C["ropes"][:, t * 64:t * 64 + 64],
                             [qtok[:, t, :].rearrange("p (h x) -> p h x", h=8)], rot_tmp, ro[0], k, ctoks)
            ro[0] = ks
            qk[t] = ks
            return reads
        gemm_t(XT, w, tok, 512, ev, 8, xtok)
        ring.give(r, pe_done())
        r, w, tok = slab("attn_w_in", P * 4096, 8, 256)
        vk = []

        def ev(t, ps, k):
            kv = kdup[:, t, :].rearrange("p (g c x) -> p g c x", g=2, c=2)
            reads, ks = rope(ps[:, 0:128].rearrange("p (h x) -> p h x", h=2), 2, C["ropec"][:, t * 64:t * 64 + 64],
                             C["ropes"][:, t * 64:t * 64 + 64], [kv[:, :, 0, :], kv[:, :, 1, :]], rot_tmp, ro[0], k)
            ro[0] = ks
            kk[t] = ks
            a = cp(vA[:, t, :], ps[:, 128:256], k, reads, e="act")
            vk.append(a)
            return [reads, a]
        gemm_t(XT, w, tok, 256, ev, 8)
        ring.give(r, pe_done())
        r, w, tok = slab("attn_w_in", P * 6144, 8, 512)
        bk = []

        def ev(fp, ps, k):
            a = copy_any(qbT[:, 2 * fp:2 * fp + 2, :], ps, k)
            bk.append(a)
            return a
        gemm_f(XT, w, tok, 4, ev)
        ring.give(r, pe_done())
        r, w, tok = slab("attn_w_in", P * (6144 + 4096), 8, 512)

        def ev(fp, ps, k):
            a = copy_any(kbT[:, 2 * fp:2 * fp + 2, :], ps, k)
            bk.append(a)
            return a
        gemm_f(XT, w, tok, 4, ev)
        ring.give(r, pe_done())
        r, w, tok = slab("attn_w_in", P * (6144 + 8192), 8, 512)

        def ev(t, ps, k):
            a = copy_any(vB[:, t, :], ps, k)
            vk.append(a)
            return a
        gemm_t(XT, w, tok, 512, ev)
        ring.give(r, pe_done())
        tk = []
        for t in range(2):
            tk += transpose_to(qT, lambda c, t=t: qtok[:, t, c * P:(c + 1) * P], 4, t, qk[t])
            tk += transpose_to(kT, lambda c, t=t: kdup[:, t, c * P:(c + 1) * P], 2, t, kk[t])

        sc, pr, ptb, st = att_bufs()
        rb, wb, btok = load(d["attn_bias"].rearrange("(p f) -> p f", p=P), 8, 512)
        obank = {}
        otk = []

        def heads(h):
            if h < 8:
                qa, ka, va = qT[:, h // 2, :], kT[:, h // 4, :], vA[:, :, 64 * (h // 4):64 * (h // 4) + 64]
            else:
                g = h - 8
                qa, ka, va = qbT[:, g // 2, :], kbT[:, g // 2, :], vB[:, :, 64 * g:64 * g + 64]
            p0 = 64 * (h % 2)

            def m(ps, fr):
                for t in range(2):
                    mm(ps[:, t * T:(t + 1) * T], qa[p0:p0 + 64, t * P:(t + 1) * P], ka[p0:p0 + 64, :], True, True,
                       fr, tk, bk)

            def pv(pt, k):
                if h % 2 == 0:
                    obank[0] = bank.take()
                b, ps, fr = obank[0]
                for kc in range(2):
                    mm(ps[p0:p0 + 64, 0:T], va[:, kc, :], pt[:, kc * T:(kc + 1) * T], kc == 0, kc == 1, fr, k, vk)
                kd = pe_done()
                if h % 2 == 1:
                    a = copy_any(OT[:, h // 2, :], ps[:, 0:T], kd)
                    otk.append(a)
                    bank.give(b, a)
                return kd
            H = dict(mm=m, pv=pv, width=512, scale=0.125, cols=[(0, 256), (256, 512)],
                     blocks=[(t, kc, t * T + kc * P) for kc in range(2) for t in range(2)])
            if h < 8:
                H["bias"], H["sink"] = C["maska"], sinkb[:, h:h + 1]
                H["btok"] = sk
            else:
                H["bias"], H["btok"] = wb[:, h - 8, :], btok
            return H
        attention(16, heads, sc, pr, ptb, st)
        ring.give(rb, Q.done("dve"))

        rk = []

        def ev(t, n, ps, k):
            x = X[:, t, n * 512:(n + 1) * 512]
            a = stt(x, x, ALPHA, ps, ALU.mult, ALU.add, k)
            rk.append(a)
            return a
        residual_gemm("attn_w_out", (2, 8, 512), OT, otk, ev)
        xtok = layer_norm(rk, gk)

        def next_gb(a, b, ia, ib, toks):
            return [pdma(GB[:, 0, :], bcast(d[a][ia:ia + 1, :]), toks),
                    pdma(GB[:, 1, :], bcast(d[b][ib:ib + 1, :]), toks)]

        gk = next_gb("ln2_g", "ln2_b", 0, 0, Q.done("dve"))
        barrier()
        rk = mlp(0, xtok)
        xtok = layer_norm(rk, gk)
        gk = next_gb("ln1_g", "ln1_b", 1, 1, Q.done("dve"))

        barrier()
        zT = arena.get(16, T)
        xcT = arena.get(32, T)
        xF = arena.get(2, 2048)
        xB = arena.get(2, 2048)
        pos0 = arena.pos
        prm = arena.get(32, 6)
        dd = arena.get(32)
        dtt = arena.get(2, 64)
        aa = arena.get(2, 64)
        dtb = arena.get(64)
        ang = arena.get(64)
        ups = Rot([arena.get(2, 260) for _ in range(2)])
        cvs = Rot([arena.get(2, T) for _ in range(2)])
        k1 = pdma(prm, d["ssm_conv"].rearrange("p (a b) -> p a b", a=32))
        k2 = pdma(dd, d["ssm_dn"])
        k3 = pdma(dtb, bcast(d["ssm_dt_bias"][0:1, :]))
        k4 = pdma(ang, bcast(d["ssm_A_log"][0:1, :]))
        zz = [mset(u[:, :, 0:2], 0.0) for u in ups.bufs] + [mset(u[:, :, 258:260], 0.0) for u in ups.bufs]
        r, w, tok = slab("ssm_w_dt", 0, 8, 64)
        dk = []

        def ev(t, ps, k):
            a = tt(dtt[:, t, :], ps, dtb, ALU.add, k, k3)
            dk.append(a)
            return a
        gemm_t(XT, w, tok, 64, ev, 8, xtok)
        ring.give(r, pe_done())
        k = ts(aa, dtt, -1.0, None, ALU.mult, None, dk)
        k = tt(aa, aa, dtt, ALU.min, k)
        k = act(aa, aa, ACT.Exp, k)
        k = act(aa, aa, ACT.Ln, k, bias=1.0)
        k = stt(dtt, dtt, 0.0, aa, ALU.max, ALU.add, k)
        ka = act(ang, ang, ACT.Exp, k4)
        ka = ts(ang, ang, -1.0, None, ALU.mult, None, ka)
        ak = tt(aa, dtt, ang.unsqueeze(1).to_broadcast([P, 2, 64]), ALU.mult, k, ka)
        zk = []
        for s in range(4):
            r, w, tok = slab("ssm_w_in", s * P * SLAB, 8, 512)

            def ev(fp, ps, k, s=s):
                a = act(zT[:, 4 * s + 2 * fp:4 * s + 2 * fp + 2, :], ps, ACT.Silu, k)
                zk.append(a)
                return a
            gemm_f(XT, w, tok, 4, ev)
            ring.give(r, pe_done())
        xk = {}
        for s in range(8):
            r, w, tok = slab("ssm_w_in", (4 + s) * P * SLAB, 8, 512)

            def ev(fp, ps, k, s=s):
                f0 = 4 * s + 2 * fp
                i, u, uf = ups.take()
                a = cp(u[:, :, 2:258], ps, k, uf, zz, e="act")
                j, v, vf = cvs.take()
                lk = []
                for q in range(2):
                    f = f0 + q
                    kk_ = act(v[:, q, :], u[:, q, 0:T], ACT.Identity, a, vf, k1,
                              scale=prm[:, f, 0:1], bias=prm[:, f, 5:6])
                    for c in range(1, 5):
                        kk_ = stt(v[:, q, :], u[:, q, c:c + T], prm[:, f, c:c + 1], v[:, q, :], ALU.mult, ALU.add, kk_)
                    lk.append(kk_)
                ups.give(i, lk)
                o = act(xcT[:, f0:f0 + 2, :], v, ACT.Silu, lk)
                cvs.give(j, o)
                xk[f0] = xk[f0 + 1] = o
                return a
            gemm_f(XT, w, tok, 4, ev)
            ring.give(r, pe_done())
        xs_k = []
        for t in range(2):
            for g in range(4):
                b, ps, fr = bank.take()
                for j in range(4):
                    f = 4 * g + j
                    tr(ps[:, j * P:(j + 1) * P], xcT[:, f, t * P:(t + 1) * P], fr, xk[f])
                kd = pe_done()
                pv_ = ps.rearrange("p (h x) -> p h x", h=8)
                for o, dr in ((xF, 0), (xB, 1)):
                    ov = o[:, t, g * 512:(g + 1) * 512].rearrange("p (h x) -> p h x", h=8)
                    dv_ = dtt[:, t, dr * 32 + g * 8:dr * 32 + g * 8 + 8].unsqueeze(2).to_broadcast([P, 8, 64])
                    kl = tt(ov, pv_, dv_, ALU.mult, kd, ak)
                    xs_k.append(kl)
                bank.give(b, kl)
        arena.pos = pos0 + 192 + 32 + 128 + 128 + 64 + 64
        barrier_pos = arena.pos
        pre = all_done()
        cbr = Rot([arena.get(768) for _ in range(2)])
        lmr = Rot([arena.get(2, 3, P) for _ in range(2)])
        emr = Rot([arena.get(768) for _ in range(3)])
        cb_of = {}

        def cb_group(g):
            b, ps, fr = bank.take()
            BT, CT = xcT[:, 16 + g, :], xcT[:, 24 + g, :]
            for s in range(2):
                mm(ps[:, s * T:(s + 1) * T], BT[:, s * P:(s + 1) * P], CT, True, True, fr, xk[16 + g], xk[24 + g])
            kd = pe_done()
            i, cb, cf = cbr.take()
            ks = [tt(cb[:, 0:T], ps[:, 0:T], C["leo"], ALU.mult, kd, cf, pre),
                  tt(cb[:, T:T + P], ps[:, T + P:], C["leo"][:, 0:P], ALU.mult, kd),
                  tt(cb[:, 384:512], ps[:, 0:P], C["oge"][:, P:], ALU.mult, kd),
                  tt(cb[:, 512:768], ps[:, T:], C["oge"], ALU.mult, kd)]
            bank.give(b, ks)
            cb_of[g] = (i, cb, ks)

        LE, GE = C["leo"][:, 0:P], C["oge"][:, P:]
        E_of = {}

        def decay(h):
            g = h // 4
            i, L, lf = lmr.take()
            cf_, cb_ = slice(h, h + 1), slice(32 + h, 33 + h)
            k_ = [ts(L[:, 0, 0, :], C["gt"], aa[:, 0, cf_], None, ALU.mult, None, lf, ak, pre),
                  ts(L[:, 0, 1, :], C["gt"], aa[:, 1, cf_], None, ALU.mult, None),
                  ts(L[:, 0, 2, :], C["ones"], aa[:, 1, cf_], None, ALU.mult, None),
                  ts(L[:, 1, 0, :], C["lt"], aa[:, 0, cb_], None, ALU.mult, None),
                  ts(L[:, 1, 1, :], C["lt"], aa[:, 1, cb_], None, ALU.mult, None),
                  ts(L[:, 1, 2, :], C["ones"], aa[:, 0, cb_], None, ALU.mult, None)]
            j, E, ef = emr.take()
            ek = []
            b, ps, fr = bank.take()
            mm(ps[:, 0:T], L[:, 0, 0, :], C["leo"], True, False, fr, k_)
            mm(ps[:, P:T], L[:, 0, 2, :], LE, False, True)
            mm(ps[:, T:T + P], L[:, 0, 1, :], LE, True, True)
            a = act(E[:, 0:384], ps[:, 0:384], ACT.Exp, pe_done(), ef, pre)
            bank.give(b, a)
            ek.append(a)
            b, ps, fr = bank.take()
            mm(ps[:, 0:P], L[:, 1, 0, :], GE, True, True, fr)
            mm(ps[:, P:384], L[:, 1, 1, :], C["oge"], True, False)
            mm(ps[:, P:T], L[:, 1, 2, :], GE, False, True)
            kd = pe_done()
            lmr.give(i, kd)
            a = act(E[:, 384:768], ps[:, 0:384], ACT.Exp, kd)
            bank.give(b, a)
            ek.append(a)
            ci, cb, cks = cb_of[g]
            mk = tt(E, E, cb, ALU.mult, ek, cks)
            if h % 4 == 3:
                cbr.give(ci, mk)
            E_of[h] = (j, E, mk)

        yk = []
        ybk = {}

        def ssm_out(h):
            j, E, mk = E_of.pop(h)
            p0 = 64 * (h % 2)
            if h % 2 == 0:
                ybk[0] = bank.take()
            b, ps, fr = ybk[0]
            o = ps[p0:p0 + 64, :]
            hs = slice(h * 64, h * 64 + 64)
            mm(o[:, 0:T], xF[:, 0, hs], E[:, 0:T], True, False, fr, mk, xs_k)
            mm(o[:, P:T], xF[:, 1, hs], E[:, T:384], False, False)
            mm(o[:, 0:P], xB[:, 0, hs], E[:, 384:512], False, False)
            mm(o[:, 0:T], xB[:, 1, hs], E[:, 512:768], False, True)
            kd = pe_done()
            emr.give(j, kd)
            if h % 2 == 1:
                f = h // 2
                a = stt(xcT[:, f, :], xcT[:, f, :], dd[:, f:f + 1], ps[:, 0:T], ALU.mult, ALU.add, kd, k2)
                bank.give(b, a)
                yk.append(tt(zT[:, f, :], xcT[:, f, :], zT[:, f, :], ALU.mult, a, zk))

        for i in range(34):
            if i < 32:
                if i % 4 == 0:
                    cb_group(i // 4)
                decay(i)
            if i >= 2:
                ssm_out(i - 2)
        arena.pos = barrier_pos
        sq = Rot([arena.get(2, T) for _ in range(2)])
        rsg = xF.rearrange("p a b -> p (a b)")[:, 0:2048].rearrange("p (g x) -> p g x", g=8)
        pre = all_done()
        gkk = []
        for g in range(0, 8, 2):
            b, ps, fr = bank.take()
            for q in range(2):
                i, s_, sf = sq.take()
                z2 = zT[:, 2 * (g + q):2 * (g + q) + 2, :]
                a = tt(s_, z2, z2, ALU.mult, sf, pre)
                for c in range(2):
                    mm(ps[:, q * T:(q + 1) * T], C["ones"], s_[:, c, :], c == 0, c == 1, fr, a)
                sq.give(i, pe_done())
            v = rsg[:, g:g + 2, :].rearrange("p g x -> p (g x)")
            a = ts(v, ps, 1.0 / 256, 1e-5, ALU.mult, ALU.add, pe_done())
            bank.give(b, a)
            gkk.append(act(v, v, ACT.Sqrt, a))
        a = recip(xF.rearrange("p a b -> p (a b)")[:, 0:2048], xF.rearrange("p a b -> p (a b)")[:, 0:2048], gkk)
        yk = []
        for f in range(16):
            yk.append(stt(zT[:, f, :], zT[:, f, :], dd[:, 16 + f:17 + f], rsg[:, f // 2, :], ALU.mult, ALU.mult, a))
        rk = []

        def ev(t, n, ps, k):
            x = X[:, t, n * 512:(n + 1) * 512]
            a = stt(x, x, ALPHA, ps, ALU.mult, ALU.add, k)
            rk.append(a)
            return a
        residual_gemm("ssm_w_out", (4, 4, 1024), zT, yk, ev)
        xtok = layer_norm(rk, gk)
        gk = next_gb("ln2_g", "ln2_b", 1, 1, Q.done("dve"))
        barrier()
        rk = mlp(1, xtok)
        xtok = layer_norm(rk, gk)

        barrier()
        for name in LATE:
            C[name] = arena.get(consts[name])
        ctoks = [pdma(C[name], d["const_" + name]) for name in ("cm", "dmask")]
        arena.base = arena.pos
        ctab = C["rope2c"]
        stab = C["rope2s"]
        posf = small[:, 40:42]
        kp = pdma(posi, d["positions"])
        k = cp(posf, posi, kp)
        A = arena.get(2, 32)
        Bk = arena.get(2, 32)
        for t in range(2):
            k = ts(A[:, t, :], C["inv"], posf[:, t:t + 1], None, ALU.mult, None, k)
        MAGIC = 12582912.0
        k = ts(Bk, A, float(1.0 / (2 * np.pi)), MAGIC, ALU.mult, ALU.add, k)
        k = ts(Bk, Bk, MAGIC, None, ALU.subtract, None, k)
        for cst in (6.28125, 0.0019350051879882812, 3.019916050995584e-07):
            k = stt(A, Bk, -cst, A, ALU.mult, ALU.add, k)
        PI = 3.1415925
        k = ts(A, A, PI, -PI, ALU.min, ALU.max, k)
        sv = stab.rearrange("p (t x) -> p t x", t=2)
        cv = ctab.rearrange("p (t x) -> p t x", t=2)
        k5 = act(sv[:, :, 32:64], A, ACT.Sin, k)
        k6 = ts(sv[:, :, 0:32], sv[:, :, 32:64], -1.0, None, ALU.mult, None, k5)
        k = ts(A, A, float(np.pi / 2), None, ALU.add, None, k5)
        k = ts(Bk, A, float(np.pi), float(-2 * np.pi), ALU.is_gt, ALU.mult, k)
        k = tt(A, A, Bk, ALU.add, k)
        k = ts(A, A, PI, -PI, ALU.min, ALU.max, k)
        k7 = act(cv[:, :, 0:32], A, ACT.Sin, k)
        k8 = cp(cv[:, :, 32:64], cv[:, :, 0:32], k7)
        ropek = [k6, k7, k8]
        ck = pdma(small[:, 44:52], d["c"].rearrange("(p c) -> p c", c=8))
        csil = small[:, 52:60]
        ck = act(csil, small[:, 44:52], ACT.Silu, ck)

        def rms(src, nf, o, tokw, w_):
            js = arena.get(nf)
            ks = []
            pk = None
            for t in range(2):
                pk = act(js, src(t), ACT.Square, tokw, pk, acc=o[:, t:t + 1])
                ks.append(pk)
            return rsqrt_small(o, o, 1.0 / nf, 1e-6, ks, w_)

        for l in range(2):
            barrier()
            MOD = arena.get(6, D)
            mbase = arena.pos
            acc = Rot([arena.get(512) for _ in range(2)])
            abb = Rot([arena.get(512) for _ in range(2)])
            modk = []
            for s in range(12):
                r, w, tok = slab("ada_w", (l * 12 + s) * P * SLAB, 8, 512)
                i, m_, mf = acc.take()
                k = ts(m_, w[:, 0, :], csil[:, 0:1], None, ALU.mult, None, tok, mf, ck)
                for c in range(1, 8):
                    k = stt(m_, w[:, c, :], csil[:, c:c + 1], m_, ALU.mult, ALU.add, k)
                ring.give(r, k)
                j, ab, af = abb.take()
                ka = pdma(ab, bcast(d["ada_b"][l:l + 1, s * 512:(s + 1) * 512]), af)
                b, ps, fr = bank.take()
                mm(ps, C["ones"], m_, True, True, fr, k)
                kd = pe_done()
                acc.give(i, kd)
                a = tt(MOD[:, s // 2, (s % 2) * 512:(s % 2) * 512 + 512], ps, ab, ALU.add, kd, ka)
                abb.give(j, a)
                bank.give(b, a)
                modk.append(a)
            gk = next_gb("norm1_g", "norm2_g", l, l, all_done())
            g1 = stt(MOD[:, 1, :], MOD[:, 1, :], 1.0, GB[:, 0, :], ALU.add, ALU.mult, modk, gk)
            g2 = stt(MOD[:, 4, :], MOD[:, 4, :], 1.0, GB[:, 1, :], ALU.add, ALU.mult, modk, gk)

            def norm_mod(si, gi, w_):
                hh = arena.get(2, D)
                rs = small[:, 60:62]
                k = rms(lambda t: X[:, t, :], D, rs, w_, w_)
                hv = hh.rearrange("p t (q c) -> p t q c", c=8)
                out_ = []
                for t in range(2):
                    a = stt(hh[:, t, :], X[:, t, :], rs[:, t:t + 1], MOD[:, gi, :], ALU.mult, ALU.mult, k, g1, g2)
                    a = tt(hh[:, t, :], hh[:, t, :], MOD[:, si, :], ALU.add, a)
                    out_ += transpose_to(XT, lambda c, t=t: hv[:, t, :, c], 8, t, a, w_)
                return out_
            barrier()
            arena.pos = mbase
            htok = norm_mod(0, 1, rk if l == 0 else [])
            arena.pos = mbase
            barrier()
            arena.pos = mbase
            gb = arena.get(24)
            kgb = pdma(gb, d["gate_b"][l * P:(l + 1) * P, :])
            yT = [arena.get(4, T) for _ in range(3)]
            work = arena.pos
            rqk = arena.get(2, 512)
            rqT = arena.get(2, T)
            rkT = arena.get(2, T)
            rv = arena.get(2, 512)
            rg = arena.get(2, 512)
            tmp = arena.get(1024)
            ra_pos = arena.pos
            woff = l * P * (7 * 4096 - 8 * 60)
            ro[0] = []
            qk2 = [None, None]
            r, w, tok = slab("w_in2", woff, 8, 512)

            def ev(t, ps, k):
                reads, ks = rope(ps.rearrange("p (h x) -> p h x", h=8), 8, ctab[:, t * 64:t * 64 + 64],
                                 stab[:, t * 64:t * 64 + 64],
                                 [rqk[:, t, :].rearrange("p (h x) -> p h x", h=8)], tmp, ro[0], k, ropek)
                ro[0] = ks
                qk2[t] = ks
                return reads
            gemm_t(XT, w, tok, 512, ev, 8, htok)
            ring.give(r, pe_done())
            rvk, rgk = [], []
            r, w, tok = slab("w_in2", woff + P * 4096, 8, 512)

            def ev(t, ps, k):
                a = copy_any(rv[:, t, :], ps, k)
                rvk.append(a)
                return a
            gemm_t(XT, w, tok, 512, ev)
            ring.give(r, pe_done())
            r, w, tok = slab("w_in2", woff + P * 8192, 8, 512)

            def ev(t, ps, k):
                a = act(rg[:, t, :], ps, ACT.Silu, k)
                rgk.append(a)
                return a
            gemm_t(XT, w, tok, 512, ev)
            ring.give(r, pe_done())
            tk = []
            for t in range(2):
                tk += transpose_to(rqT, lambda c, t=t: rqk[:, t, c * P:(c + 1) * P], 2, t, qk2[t])
                tk += transpose_to(rkT, lambda c, t=t: rqk[:, t, 256 + c * P:256 + (c + 1) * P], 2, t, qk2[t])
            smr = Rot([arena.get(384) for _ in range(2)])
            ob = [bank.take() for _ in range(2)]
            for h in range(4):
                p0 = 64 * (h % 2)
                b, ps, fr = bank.take()
                kh, qh = rkT[p0:p0 + 64, h // 2, :], rqT[p0:p0 + 64, h // 2, :]
                mm(ps[:, 0:T], kh[:, 0:P], qh, True, True, fr, tk)
                mm(ps[:, T:384], kh[:, P:T], qh[:, P:T], True, True)
                i, s_, sf = smr.take()
                a = tt(s_, ps[:, 0:384], C["dmask"][:, h * 384:(h + 1) * 384], ALU.mult, pe_done(), sf, ctoks)
                bank.give(b, a)
                hs = slice(h * P, h * P + P)
                mm(ob[0][1][:, hs], s_[:, 0:P], rv[:, 0, hs], True, True, ob[0][2], a, rvk)
                mm(ob[1][1][:, hs], s_[:, P:T], rv[:, 0, hs], True, False, ob[1][2])
                mm(ob[1][1][:, hs], s_[:, T:384], rv[:, 1, hs], False, True)
                smr.give(i, pe_done())
            kd = pe_done()
            st8 = small[:, 64:112].rearrange("p (a b) -> p a b", a=8)
            mv8 = small[:, 112:128].rearrange("p (a b) -> p a b", a=8)
            rs8 = small[:, 128:136]
            ks = []
            for t in range(2):
                for h in range(4):
                    q = t * 4 + h
                    o, i_ = st8[:, q, :], ob[t][1][:, h * P:(h + 1) * P]
                    k = Q.emit("dve", lambda e, o=o, i_=i_: e.bn_stats(o, i_), [kd])
                    o2, i2 = mv8[:, q, :], st8[:, q, :]
                    ks.append(Q.emit("dve", lambda e, o2=o2, i2=i2: e.bn_aggr(o2, i2), [k]))
            k = rsqrt_small(rs8, mv8[:, :, 1], 1.0, 1e-6, ks)
            yak = []
            for t in range(2):
                lk = []
                for h in range(4):
                    q = t * 4 + h
                    lk.append(ts(rqk[:, t, h * P:(h + 1) * P], ob[t][1][:, h * P:(h + 1) * P], mv8[:, q, 0:1],
                                 rs8[:, q:q + 1], ALU.subtract, ALU.mult, k, tk))
                bank.give(ob[t][0], lk)
                a = tt(rqk[:, t, :], rqk[:, t, :], rg[:, t, :], ALU.mult, lk, rgk)
                yak += transpose_to(yT[0], lambda c, t=t: rqk[:, t, c * P:(c + 1) * P], 4, t, a)
            barrier()
            arena.pos = work
            fqT = arena.get(4, T)
            fkT = arena.get(4, T)
            fv = arena.get(2, 512)
            misc = arena.get(2, 452)
            lf = arena.get(2, 4)
            fbb = arena.get(4)
            bufs = att_bufs()
            fmr = Rot([arena.get(384) for _ in range(2)])
            kfb = pdma(fbb, bcast(d["fox_fb"][l:l + 1, :]))
            fk_ = []
            FS = float(128 ** -0.5)
            r, w, tok = slab("w_in2", woff + P * 3 * 4096, 8, 512)

            def ev(fp, ps, k):
                a = act(fqT[:, 2 * fp:2 * fp + 2, :], ps, ACT.Copy, k, scale=FS)
                fk_.append(a)
                return a
            gemm_f(XT, w, tok, 4, ev)
            ring.give(r, pe_done())
            r, w, tok = slab("w_in2", woff + P * 4 * 4096, 8, 512)

            def ev(fp, ps, k):
                a = copy_any(fkT[:, 2 * fp:2 * fp + 2, :], ps, k)
                fk_.append(a)
                return a
            gemm_f(XT, w, tok, 4, ev)
            ring.give(r, pe_done())
            r, w, tok = slab("w_in2", woff + P * 5 * 4096, 8, 512)
            fvk, mk_ = [], []

            def ev(t, ps, k):
                a = copy_any(fv[:, t, :], ps, k)
                fvk.append(a)
                return a
            gemm_t(XT, w, tok, 512, ev)
            ring.give(r, pe_done())
            r, w, tok = slab("w_in2", woff + P * 6 * 4096, 8, 452)

            def ev(t, ps, k):
                a = copy_any(misc[:, t, :], ps, k)
                mk_.append(a)
                return a
            gemm_t(XT, w, tok, 452, ev)
            ring.give(r, pe_done())
            lt_ = small[:, 140:148].rearrange("p (t h) -> p t h", t=2)
            k = tt(lf, misc[:, :, 0:4], fbb.unsqueeze(1).to_broadcast([P, 2, 4]), ALU.add, mk_, kfb)
            k = ts(lt_, lf, -1.0, None, ALU.mult, None, k)
            k = tt(lt_, lt_, lf, ALU.min, k)
            k = act(lt_, lt_, ACT.Exp, k)
            k = act(lt_, lt_, ACT.Ln, k, bias=1.0)
            lfk = stt(lf, lf, 0.0, lt_, ALU.min, ALU.subtract, k)
            CB = [(0, 128), (128, 384)]
            CBL = [(0, 0, 0), (1, 0, 128), (1, 1, 256)]
            ytk = [yak, [], []]

            def causal_pv(br, v, vtok):
                def make(h):
                    def pv(pt, k):
                        b, ps, fr = bank.take()
                        hs = slice(h * P, h * P + P)
                        mm(ps[:, 0:T], v[:, 0, hs], pt[:, 0:T], True, False, fr, k, vtok)
                        mm(ps[:, P:T], v[:, 1, hs], pt[:, T + P:2 * T], False, True)
                        kd = pe_done()
                        a = copy_any(yT[br][:, h, :], ps[:, 0:T], kd)
                        ytk[br].append(a)
                        bank.give(b, a)
                        return kd
                    return pv
                return make

            mkpv = causal_pv(1, fv, fvk)

            def heads(h):
                i, F, ff = fmr.take()
                a = [ts(F[:, 0:P], C["gt"], lf[:, 0, h:h + 1], None, ALU.mult, None, ff, lfk),
                     ts(F[:, P:T], C["ones"], lf[:, 1, h:h + 1], None, ALU.mult, None),
                     ts(F[:, T:384], C["gt"], lf[:, 1, h:h + 1], None, ALU.mult, None)]

                def m(ps, fr):
                    mm(ps[:, 0:P], fqT[:, h, 0:P], fkT[:, h, 0:P], True, False, fr, fk_)
                    mm(ps[:, 0:P], LE, F[:, 0:P], False, True, a)
                    mm(ps[:, P:384], fqT[:, h, P:T], fkT[:, h, :], True, False)
                    mm(ps[:, P:T], C["ones"], F[:, 0:P], False, False)
                    mm(ps[:, P:384], LE, F[:, P:384], False, True)
                    fmr.give(i, pe_done())
                return dict(mm=m, pv=mkpv(h), width=384, scale=1.0, cols=CB, blocks=CBL, bias=C["cm"], btok=ctoks)
            attention(4, heads, *bufs)
            barrier()
            arena.pos = work + 3 * 1024 + 904
            qnT = arena.get(4, T)
            knT = arena.get(4, T)
            vM = arena.get(2, 512)
            arena_keep = arena.pos
            qpT = arena.get(2, T)
            kpT = arena.get(1, T)
            lat = arena.get(2, 384)
            latT = arena.get(3, T)
            gq = arena.get(384)
            qpt = arena.get(2, T)
            kpt = arena.get(2, P)
            tmp = arena.get(512)
            kg1 = pdma(gq[:, 0:256], bcast(d["mla_q_g"][l:l + 1, :]))
            kg2 = pdma(gq[:, 256:384], bcast(d["mla_kv_g"][l:l + 1, :]))
            rs_q, rs_k = small[:, 160:162], small[:, 162:164]
            kq = rms(lambda t: misc[:, t, 4:260], 256, rs_q, [], [])
            kkv = rms(lambda t: misc[:, t, 260:388], 128, rs_k, [], [])
            lk = []
            for t in range(2):
                lk.append([stt(lat[:, t, 0:256], misc[:, t, 4:260], rs_q[:, t:t + 1], gq[:, 0:256], ALU.mult,
                               ALU.mult, kq, kg1),
                           stt(lat[:, t, 256:384], misc[:, t, 260:388], rs_k[:, t:t + 1], gq[:, 256:384], ALU.mult,
                               ALU.mult, kkv, kg2)])
            ltk = []
            kpk = [None, None]
            ro[0] = []
            for t in range(2):
                ltk += transpose_to(latT, lambda c, t=t: lat[:, t, c * P:(c + 1) * P], 3, t, lk[t])
                kv = kpt[:, t, :].rearrange("p (c x) -> p c x", c=2)
                reads, ks = rope(misc[:, t, 388:452].unsqueeze(1), 1, ctab[:, t * 64:t * 64 + 64],
                                 stab[:, t * 64:t * 64 + 64], [kv[:, 0:1, :], kv[:, 1:2, :]], tmp, ro[0])
                ro[0] = ks
                kpk[t] = ks
            r, w, tok = slab("wq_up", l * P * 1536, 2, 768)
            MS = float(192 ** -0.5)
            for h in range(0, 4, 2):
                b, ps, fr = bank.take()
                for j in range(2):
                    for c in range(2):
                        mm(ps[:, j * T:(j + 1) * T], w[:, c, (h + j) * 192:(h + j) * 192 + P], latT[:, c, :],
                           c == 0, c == 1, fr, tok, ltk)
                a = act(qnT[:, h:h + 2, :], ps.rearrange("p (a b) -> p a b", a=2), ACT.Copy, pe_done(), scale=MS)
                bank.give(b, a)
                fk_.append(a)
            wv = w.rearrange("p c (h x) -> p c h x", h=4)
            qpk = [None, None]
            for t in range(2):
                b, ps, fr = bank.take()
                for c in range(2):
                    mm(ps[:, 0:T].rearrange("p (h x) -> p h x", h=4), latT[:, c, t * P:(t + 1) * P],
                       wv[:, c, :, 128:192], c == 0, c == 1, fr, tok, ltk)
                reads, ks = rope(ps[:, 0:T].rearrange("p (h x) -> p h x", h=4), 4, ctab[:, t * 64:t * 64 + 64],
                                 stab[:, t * 64:t * 64 + 64],
                                 [qpt[:, t, :].rearrange("p (h x) -> p h x", h=4)], tmp, ro[0], pe_done())
                ks = [ts(qpt[:, t, :], qpt[:, t, :], MS, None, ALU.mult, None, ks)]
                ro[0] = ks
                qpk[t] = ks
                bank.give(b, reads)
            ring.give(r, pe_done())
            r, w, tok = slab("wkv_up", l * P * 1024, 1, 1024)
            for h in range(0, 4, 2):
                b, ps, fr = bank.take()
                for j in range(2):
                    mm(ps[:, j * T:(j + 1) * T], w[:, 0, (h + j) * 256:(h + j) * 256 + P], latT[:, 2, :],
                       True, True, fr, tok, ltk)
                a = copy_any(knT[:, h:h + 2, :], ps.rearrange("p (a b) -> p a b", a=2), pe_done())
                bank.give(b, a)
                fk_.append(a)
            wv = w.rearrange("p c (h x) -> p c h x", h=4)
            vmk = []
            for t in range(2):
                b, ps, fr = bank.take()
                mm(ps.rearrange("p (h x) -> p h x", h=4), latT[:, 2, t * P:(t + 1) * P], wv[:, 0, :, 128:256],
                   True, True, fr, tok, ltk)
                a = copy_any(vM[:, t, :], ps, pe_done())
                bank.give(b, a)
                vmk.append(a)
            ring.give(r, pe_done())
            for t in range(2):
                fk_ += transpose_to(qpT, lambda c, t=t: qpt[:, t, c * P:(c + 1) * P], 2, t, qpk[t])
                fk_ += transpose_to(kpT, lambda c, t=t: kpt[:, t, :], 1, t, kpk[t])
            mkpv = causal_pv(2, vM, vmk)
            barrier()
            arena.pos = work
            bufs = att_bufs()
            assert arena.pos <= work + 3 * 1024 + 904

            def heads(h):
                p0 = 64 * (h % 2)
                qp, kp_ = qpT[p0:p0 + 64, h // 2, :], kpT[p0:p0 + 64, 0, :]

                def m(ps, fr):
                    mm(ps[:, 0:P], qnT[:, h, 0:P], knT[:, h, 0:P], True, False, fr)
                    mm(ps[:, 0:P], qp[:, 0:P], kp_[:, 0:P], False, True)
                    mm(ps[:, P:384], qnT[:, h, P:T], knT[:, h, :], True, False)
                    mm(ps[:, P:384], qp[:, P:T], kp_, False, True)
                return dict(mm=m, pv=mkpv(h), width=384, scale=1.0, cols=CB, blocks=CBL, bias=C["cm"], btok=ctoks)
            attention(4, heads, *bufs)
            barrier()
            arena.pos = work
            gT = arena.get(8, T)
            mg = arena.get(8, T)
            tb = Rot([arena.get(2, T) for _ in range(2)])
            gprev = {}
            mgk = {}
            for br in range(3):
                gtk = {}
                for s in range(2):
                    r, w, tok = slab("gate_w", (l * 6 + br * 2 + s) * P * SLAB, 8, 512)

                    def ev(fp, ps, k, s=s, br=br):
                        f0 = 4 * s + 2 * fp
                        ks = []
                        for j in range(2):
                            ks.append(act(gT[:, f0 + j, :], ps[:, j, :], ACT.Sigmoid, k, kgb, gprev.get(f0),
                                          bias=gb[:, br * 8 + f0 + j:br * 8 + f0 + j + 1]))
                        gtk[f0] = ks
                        return ks
                    gemm_f(XT, w, tok, 4, ev)
                    ring.give(r, pe_done())
                r, w, tok = slab("branch_w", (l * 3 + br) * P * SLAB, 4, 1024)

                def ev(fp, ps, k, br=br):
                    f0 = 2 * fp
                    m_ = mg[:, f0:f0 + 2, :]
                    g_ = gT[:, f0:f0 + 2, :]
                    if br == 0:
                        a = tt(m_, ps, g_, ALU.mult, k, gtk[f0])
                        mgk[f0] = a
                        gprev[f0] = a
                        return a
                    i, t_, tf = tb.take()
                    a = tt(t_, ps, g_, ALU.mult, k, gtk[f0], tf)
                    gprev[f0] = a
                    mgk[f0] = tt(m_, m_, t_, ALU.add, a, mgk[f0])
                    tb.give(i, mgk[f0])
                    return a
                gemm_f(yT[br], w, tok, 8, ev, 4, ytk[br])
                ring.give(r, pe_done())
            ot = Rot([arena.get(512) for _ in range(2)])
            rk = []

            def gated_res(gi):
                def ev(t, n, ps, k):
                    i, o, of = ot.take()
                    a = tt(o, ps, MOD[:, gi, n * 512:(n + 1) * 512], ALU.mult, k, of)
                    x = X[:, t, n * 512:(n + 1) * 512]
                    a2 = tt(x, x, o, ALU.add, a)
                    ot.give(i, a2)
                    rk.append(a2)
                    return a
                return ev
            residual_gemm("out_w", (2, 8, 512), mg, list(mgk.values()), gated_res(2), l * 2 * P * SLAB)

            barrier()
            arena.pos = mbase
            htok = norm_mod(3, 4, rk)
            barrier()
            arena.pos = mbase
            wc = arena.get(2, 32)
            rb_ = arena.get(36)
            lg = arena.get(2, 36)
            pr_ = arena.get(2, 8)
            m1 = arena.get(2, 8)
            m2 = arena.get(2, 8)
            tm = arena.get(2, 32)
            sel = arena.get(2, 8)
            gm = arena.get(2, 4)
            s4 = arena.get(2, 16)
            krb = pdma(rb_, bcast(d["router_b"][l:l + 1, :]))
            r, w, tok = slab("router_w", l * P * 288, 8, 36)
            lk = []

            def ev(t, ps, k):
                a = tt(lg[:, t, :], ps, rb_, ALU.add, k, krb)
                lk.append(a)
                return a
            gemm_t(XT, w, tok, 36, ev, 8, htok)
            ring.give(r, pe_done())

            def bc2(x, n):
                return x.to_broadcast([P, 2, n])

            def first_max(x, n, mask, mx, w_):
                k = red(mx, x, ALU.max, w_)
                k = tt(mask, x, bc2(mx, n), ALU.is_equal, k)
                k = tt(mask, mask, C["desc"][:, 0:n].unsqueeze(1).to_broadcast([P, 2, n]), ALU.mult, k)
                k = red(s4[:, :, 15:16], mask, ALU.max, k)
                return tt(mask, mask, bc2(s4[:, :, 15:16], n), ALU.is_equal, k)

            def softmax(o, x, n, mx, w_):
                k = tt(o, x, bc2(mx, n), ALU.subtract, w_)
                k = act(o, o, ACT.Exp, k)
                k = red(s4[:, :, 14:15], o, ALU.add, k)
                k = recip(s4[:, :, 13:14], s4[:, :, 14:15], k)
                return tt(o, o, bc2(s4[:, :, 13:14], n), ALU.mult, k)

            k = red(s4[:, :, 0:1], lg[:, :, 0:4], ALU.max, lk)
            k = softmax(gm, lg[:, :, 0:4], 4, s4[:, :, 0:1], k)
            k = first_max(gm, 4, tm[:, :, 0:4], s4[:, :, 1:2], k)
            k = cp(gm, tm[:, :, 0:4], k)
            tv = tm.rearrange("p t (g e) -> p t g e", g=4)
            for t in range(2):
                k = tt(tv[:, t, :, :], lg[:, t, 4:36].rearrange("p (g e) -> p g e", g=4),
                       gm[:, t, :].unsqueeze(2).to_broadcast([P, 4, 8]), ALU.mult, k)
            k = tt(sel, tm[:, :, 0:8], tm[:, :, 8:16], ALU.add, k)
            k = tt(sel, sel, tm[:, :, 16:24], ALU.add, k)
            k = tt(sel, sel, tm[:, :, 24:32], ALU.add, k)
            k = red(s4[:, :, 2:3], sel, ALU.max, k)
            k = softmax(pr_, sel, 8, s4[:, :, 2:3], k)
            k = first_max(pr_, 8, m1, s4[:, :, 3:4], k)
            k = stt(sel, m1, -4.0, pr_, ALU.mult, ALU.add, k)
            k = first_max(sel, 8, m2, s4[:, :, 4:5], k)
            k = tt(s4[:, :, 5:6], s4[:, :, 3:4], s4[:, :, 4:5], ALU.add, k)
            k = recip(s4[:, :, 6:7], s4[:, :, 5:6], k)
            k = tt(m1, m1, bc2(s4[:, :, 3:4], 8), ALU.mult, k)
            k = tt(m2, m2, bc2(s4[:, :, 4:5], 8), ALU.mult, k)
            k = tt(m1, m1, m2, ALU.add, k)
            k = tt(m1, m1, bc2(s4[:, :, 6:7], 8), ALU.mult, k)
            k = tt(m1, m1, bc2(s4[:, :, 1:2], 8), ALU.mult, k)
            for t in range(2):
                k = tt(wc[:, t, :].rearrange("p (g e) -> p g e", g=4), gm[:, t, :].unsqueeze(2).to_broadcast([P, 4, 8]),
                       m1[:, t, :].unsqueeze(1).to_broadcast([P, 4, 8]), ALU.mult, k)
            wk = k
            av = arena.get(2, D)
            ah = Rot([arena.get(2, T) for _ in range(3)])
            hid = Rot([arena.get(4, T) for _ in range(2)])
            ak_ = {}
            for e in range(NE):
                r1, w1, t1 = slab("exp_w1", (l * NE + e) * P * SLAB, 8, 512)
                r3, w3, t3 = slab("exp_w3", (l * NE + e) * P * SLAB, 8, 512)
                r2, w2, t2 = slab("exp_w2", (l * NE + e) * P * SLAB, 4, 1024)
                hi, hd, hf = hid.take()
                hk = []
                for fp in range(2):
                    ba, pa, fa = bank.take()
                    for j in range(2):
                        f = 2 * fp + j
                        for c in range(8):
                            mm(pa[:, j * T:(j + 1) * T], w1[:, c, f:512:4], XT[:, c, :], c == 0, c == 7,
                               fa, t1, htok)
                    ka = pe_done()
                    i, s_, sf = ah.take()
                    a = act(s_, pa.rearrange("p (a b) -> p a b", a=2), ACT.Silu, ka, sf)
                    bank.give(ba, a)
                    bb, pb, fb_ = bank.take()
                    for j in range(2):
                        f = 2 * fp + j
                        for c in range(8):
                            mm(pb[:, j * T:(j + 1) * T], w3[:, c, f:512:4], XT[:, c, :], c == 0, c == 7,
                               fb_, t3)
                    a2 = tt(hd[:, 2 * fp:2 * fp + 2, :], s_, pb.rearrange("p (a b) -> p a b", a=2), ALU.mult, a,
                            pe_done(), hf)
                    ah.give(i, a2)
                    bank.give(bb, a2)
                    hk.append(a2)
                ring.give(r1, pe_done())
                ring.give(r3, pe_done())
                for t in range(2):
                    for n in range(2):
                        b, ps, fr = bank.take()
                        for c in range(4):
                            mm(ps, hd[:, c, t * P:(t + 1) * P], w2[:, c, n * 512:(n + 1) * 512], c == 0, c == 3,
                               fr, t2, hk)
                        o = av[:, t, n * 512:(n + 1) * 512]
                        if e == 0:
                            a = ts(o, ps, wc[:, t, e:e + 1], None, ALU.mult, None, pe_done(), wk)
                        else:
                            a = stt(o, ps, wc[:, t, e:e + 1], o, ALU.mult, ALU.add, pe_done(), ak_[t, n])
                        ak_[t, n] = a
                        bank.give(b, a)
                hid.give(hi, pe_done())
                ring.give(r2, pe_done())
            rk = []
            for t in range(2):
                a = tt(av[:, t, :], av[:, t, :], MOD[:, 5, :], ALU.mult, ak_[t, 0], ak_[t, 1])
                rk.append(tt(X[:, t, :], X[:, t, :], av[:, t, :], ALU.add, a))

        barrier()
        kf = pdma(GB[:, 0, :], bcast(d["final_g"][0:1, :]), all_done())
        rs = small[:, 60:62]
        k = rms(lambda t: X[:, t, :], D, rs, rk, rk)
        fk = []
        for t in range(2):
            fk.append(stt(X[:, t, :], X[:, t, :], rs[:, t:t + 1], GB[:, 0, :], ALU.mult, ALU.mult, k, kf))

        last = flat(fk)
        block = ctx.enter_context(nc.Block())

        def run(e, eng):
            for rec in Q.q[e]:
                if rec[0] == "wait":
                    eng.wait_ge(rec[1], rec[2])
                else:
                    ins = rec[1](eng)
                    if rec[2] is not None:
                        ins.then_inc(rec[2], rec[3])

        @block.sync
        def _(eng):
            run("sp", eng)
            for x in last:
                eng.wait_ge(x[1], x[2])
            eng.dma_start(out.rearrange("(t p) f -> p t f", p=P), X).then_inc(osem, 16)
            eng.wait_ge(osem, 16)

        @block.gpsimd
        def _(eng):
            run("pool", eng)

        @block.scalar
        def _(eng):
            run("act", eng)

        @block.vector
        def _(eng):
            run("dve", eng)

        @block.tensor
        def _(eng):
            run("pe", eng)


def constants():
    i = np.arange(P)[:, None]
    j = np.arange(P)[None, :]
    f = np.float32
    one = np.ones((P, P), f)
    c = {}
    c["ident"] = np.eye(P, dtype=f)
    c["ones"] = None
    c["half"] = None
    c["gt"] = (i > j).astype(f)
    c["lt"] = (i < j).astype(f)
    c["leo"] = np.concatenate([(i <= j).astype(f), one], 1)
    c["oge"] = np.concatenate([one, (i >= j).astype(f)], 1)
    k = np.arange(T)[None, :]
    c["maska"] = np.concatenate([np.where(np.abs(i + t * P - k) <= 128, 0.0, NEG) for t in range(2)], 1).astype(f)
    tri = np.where(j <= i, 0.0, NEG)
    c["cm"] = np.concatenate([tri, np.zeros((P, P)), tri], 1).astype(f)
    inv = 10000.0 ** (-np.arange(32, dtype=np.float64) / 32)
    c["inv"] = np.broadcast_to(inv.astype(f)[None], (P, 32)).copy()
    ang = (np.arange(T, dtype=f)[:, None] * inv.astype(f)[None, :]).astype(f).astype(np.float64)
    co, si = np.cos(ang), np.sin(ang)
    ct = np.concatenate([co, co], 1).reshape(2, P, 64).transpose(1, 0, 2).reshape(P, 128)
    st = np.concatenate([-si, si], 1).reshape(2, P, 64).transpose(1, 0, 2).reshape(P, 128)
    c["ropec"], c["ropes"] = ct.astype(f), st.astype(f)
    dm = []
    for h in range(4):
        lg = np.log1p(-np.exp2(-5.0 - h))
        q = np.arange(T)[None, :]
        m0 = np.where(q >= i, np.exp(lg * np.maximum(q - i, 0)), 0.0)
        q1 = np.arange(P)[None, :]
        m1 = np.where(q1 >= i, np.exp(lg * np.maximum(q1 - i, 0)), 0.0)
        dm.append(np.concatenate([m0, m1], 1) * 0.125)
    c["dmask"] = np.concatenate(dm, 1).astype(f)
    c["desc"] = np.broadcast_to((8 - np.arange(8)).astype(f)[None], (P, 8)).copy()
    return c


CONST_WIDTH = {"ident": 128, "ones": 128, "half": 8, "gt": 128, "lt": 128, "leo": 256, "oge": 256, "maska": 512,
               "cm": 384, "inv": 32, "ropec": 128, "ropes": 128, "dmask": 1536, "desc": 8, "rope2c": 128,
               "rope2s": 128}


def pc(w, cuts):
    k, n = w.shape
    v = w.reshape(P, k // P, n)
    out, a = [], 0
    for m in cuts:
        out.append(v[:, :, a:a + m].reshape(-1))
        a += m
    assert a == n
    return np.concatenate(out)


def cpw(w, cuts):
    k, n = w.shape
    return pc(np.ascontiguousarray(w.reshape(k // P, P, n).transpose(1, 0, 2)).reshape(k, n), cuts)


def cpk(w, kc):
    k, n = w.shape
    return np.ascontiguousarray(w.reshape(k // (kc * P), kc, P, n).transpose(0, 2, 1, 3)).reshape(-1)


def kernel(**inputs):
    import numpy as _np
    import concourse.bacc as _bacc
    from concourse import mybir as _mybir
    from concourse.bass_utils import run_bass_kernel_spmd as _run

    g = {k: _np.asarray(v) for k, v in inputs.items()}
    a = {}
    a["x"] = g["x"].reshape(T, D)
    a["attn_w_in"] = pc(g["attn_w_in"][0], [512, 256, 512, 512, 512])
    a["attn_sink"] = g["attn_sink"]
    q = _np.arange(T)
    r_, c_ = q // 64, q % 64
    cs = _np.clip(c_ - 8, 0, 48)
    ok = (c_[None, :] >= cs[:, None]) & (c_[None, :] < cs[:, None] + 16)
    dr = r_[None, :] - r_[:, None] + 7
    dc = _np.clip(c_[None, :] - c_[:, None] + 15, 0, 30)
    idx = _np.where(ok, dr * 31 + dc, 15 * 31)
    rp = _np.concatenate([g["attn_rpb"][0].reshape(8, 465), _np.full((8, 1), NEG, _np.float32)], 1)
    bias = rp[:, idx.reshape(-1)].reshape(8, 2, P, T)
    a["attn_bias"] = _np.ascontiguousarray(bias.transpose(2, 0, 1, 3)).reshape(-1)
    a["attn_w_out"] = cpw(g["attn_w_out"][0], [512, 512])
    a["ssm_w_in"] = pc(g["ssm_w_in"][0][:, 0:6144], [512] * 12)
    a["ssm_w_dt"] = pc(g["ssm_w_in"][0][:, 6144:], [64])
    cw = g["ssm_conv_w"][0].reshape(5, 32, P).transpose(2, 1, 0)
    cb = g["ssm_conv_b"][0].reshape(32, P).T[:, :, None]
    a["ssm_conv"] = _np.concatenate([cw, cb], 2).reshape(P, 192)
    dsk = _np.repeat(g["ssm_D"][0], 64).reshape(16, P).T
    a["ssm_dn"] = _np.concatenate([dsk, g["ssm_norm_w"][0].reshape(16, P).T], 1)
    a["ssm_dt_bias"] = g["ssm_dt_bias"]
    a["ssm_A_log"] = g["ssm_A_log"].reshape(1, 64)
    a["ssm_w_out"] = cpk(g["ssm_w_out"][0], 4)
    a["mlp_w1"] = _np.concatenate([pc(g["mlp_w1"][l], [512] * 8) for l in range(2)])
    a["mlp_w2"] = _np.concatenate([cpk(g["mlp_w2"][l], 4) for l in range(2)])
    for n in ("ln1_g", "ln1_b", "ln2_g", "ln2_b"):
        a[n] = g[n]
    a["c"] = g["c_2"].reshape(-1)
    a["positions"] = g["positions_2"].reshape(2, P).T
    a["ada_w"] = _np.concatenate([pc(g["ada_w_2"][l], [512] * 12) for l in range(2)])
    a["ada_b"] = g["ada_b_2"]
    a["norm1_g"], a["norm2_g"], a["final_g"] = g["norm1_g_2"], g["norm2_g_2"], g["final_g_2"].reshape(1, D)
    a["w_in2"] = _np.concatenate([pc(g["w_in_2"][l], [512] * 6 + [452]) for l in range(2)])
    a["fox_fb"] = g["fox_fb_2"]
    a["mla_q_g"], a["mla_kv_g"] = g["mla_q_norm_g_2"], g["mla_kv_norm_g_2"]
    a["wq_up"] = _np.concatenate([cpw(g["mla_wq_up_2"][l], [768]) for l in range(2)])
    a["wkv_up"] = _np.concatenate([cpw(g["mla_wkv_up_2"][l], [1024]) for l in range(2)])
    a["gate_w"] = _np.concatenate([pc(g["gate_w_2"][l], [512] * 6) for l in range(2)])
    a["gate_b"] = _np.concatenate([g["gate_b_2"][l].reshape(24, P).T for l in range(2)])
    a["branch_w"] = _np.concatenate([cpk(g["branch_w_2"][l, b], 4) for l in range(2) for b in range(3)])
    a["out_w"] = _np.concatenate([cpw(g["out_w_2"][l], [512, 512]) for l in range(2)])
    a["router_w"] = _np.concatenate(
        [pc(_np.concatenate([g["router_grp_w_2"][l], g["router_exp_w_2"][l]], 1), [36]) for l in range(2)])
    a["router_b"] = _np.concatenate([g["router_grp_b_2"], g["router_exp_b_2"]], 1)
    a["exp_w1"] = g["exp_w1_2"].reshape(-1)
    a["exp_w3"] = g["exp_w3_2"].reshape(-1)
    a["exp_w2"] = g["exp_w2_2"].reshape(-1)
    for n, v in constants().items():
        if v is not None:
            a["const_" + n] = v

    nc = _bacc.Bacc("TRN2", target_bir_lowering=False, num_devices=1)
    arrays, args = {}, {}
    for name, v in a.items():
        v = _np.ascontiguousarray(v)
        arrays[f"in_{name}"] = v
        args[name] = nc.dram_tensor(f"in_{name}", v.shape, _mybir.dt.from_np(v.dtype), kind="ExternalInput").ap()
    out = nc.dram_tensor("out_0", (T, D), _mybir.dt.float32, kind="ExternalOutput").ap()
    build(nc, args, out, CONST_WIDTH)
    r = _run(nc, [arrays], core_ids=[0])
    return r.results[0]["out_0"].reshape(1, T, D)
```

```python
from contextlib import ExitStack

import numpy as np
import concourse.bass as bass
from concourse import mybir

F32 = mybir.dt.float32
I32 = mybir.dt.int32
ALU = mybir.AluOpType
ACT = mybir.ActivationFunctionType
AX = mybir.AxisListType.X

P = 128
T = 256
D = 1024
NEG = -1e30
NRING = 4
SLAB = 4096
NE = 32
CAP = 64
ALPHA = float(4 ** 0.25)


class Queues:

    def __init__(self, nc, ctx, suffix=""):
        self.q = {"pe": [], "act": [], "dve": [], "pool": [], "sp": []}
        self.sem = {e: ctx.enter_context(nc.semaphore("s_" + e + suffix)) for e in ("pe", "act", "dve", "pool")}
        self.cnt = {e: 0 for e in self.sem}
        self.seen = {}

    def emit(self, e, fn, waits, inc=True):
        for w in flat(waits):
            key = (e, w[0])
            if self.seen.get(key, 0) < w[2]:
                self.seen[key] = w[2]
                self.q[e].append(("wait", w[1], w[2]))
        rec = ["op", fn, None, 0]
        self.q[e].append(rec)
        if inc:
            return self.done(e)
        return None

    def done(self, e):
        rec = self.q[e][-1]
        assert rec[0] == "op"
        if rec[2] is None:
            self.cnt[e] += 1
            rec[2], rec[3] = self.sem[e], 1
        return (e, self.sem[e], self.cnt[e])

    def all_done(self):
        out = []
        for e in ("pe", "act", "dve", "pool"):
            for rec in reversed(self.q[e]):
                if rec[0] == "op":
                    if rec[2] is None:
                        self.cnt[e] += 1
                        rec[2], rec[3] = self.sem[e], 1
                    break
            if self.cnt[e]:
                out.append((e, self.sem[e], self.cnt[e]))
        return out


def flat(ws):
    out = []
    for w in ws:
        if w is None:
            continue
        if isinstance(w, tuple) and len(w) == 3 and isinstance(w[0], (str, int)):
            out.append(w)
        else:
            out.extend(flat(w))
    return out


class Rot:

    def __init__(self, bufs):
        self.bufs = bufs
        self.free = [[] for _ in bufs]
        self.held = [False] * len(bufs)
        self.i = -1

    def take(self):
        for _ in range(len(self.bufs)):
            self.i = (self.i + 1) % len(self.bufs)
            if not self.held[self.i]:
                self.held[self.i] = True
                return self.i, self.bufs[self.i], list(self.free[self.i])
        raise AssertionError("no free buffer")

    def give(self, i, *toks):
        self.free[i] = flat(toks)
        self.held[i] = False


class Arena:
    def __init__(self, ap, size):
        self.ap, self.size, self.pos, self.base = ap, size, 0, 0

    def get(self, *shape):
        n = 1
        for s in shape:
            n *= s
        a = self.ap[:, self.pos:self.pos + n]
        self.pos += n
        assert self.pos <= self.size, (self.pos, self.size)
        if len(shape) == 2:
            a = a.rearrange("p (a b) -> p a b", a=shape[0])
        if len(shape) == 3:
            a = a.rearrange("p (a b c) -> p a b c", a=shape[0], b=shape[1])
        return a


def build(nc, d, out, consts):
    with ExitStack() as ctx:
        Q = Queues(nc, ctx)

        def sb(name, shape, dt=F32):
            return ctx.enter_context(nc.sbuf_tensor(name, shape, dt))

        psb = [ctx.enter_context(nc.psum_tensor(f"ps{i}", [P, 512], F32)) for i in range(8)]
        bank = Rot([p[:, :] for p in psb])
        ringt = sb("ring", [P, NRING * SLAB])
        ring = Rot([ringt[:, i * SLAB:(i + 1) * SLAB] for i in range(NRING)])
        rsem = [ctx.enter_context(nc.semaphore(f"s_ring{i}")) for i in range(NRING + 2)]
        ruse = [0] * (NRING + 2)
        X = sb("X", [P, 2, D])[:, :, :]
        XT = sb("XT", [P, 8, T])[:, :, :]
        GB = sb("GB", [P, 2, D])[:, :, :]
        small = sb("small", [P, 512])[:, :]
        C = {}
        LATE = ("cm", "dmask", "rope2c", "rope2s")
        for name, arr in consts.items():
            if name in LATE:
                continue
            C[name] = sb("c_" + name, [P, arr])[:, :]
        ASZ = 27180
        arena = Arena(sb("arena", [P, ASZ])[:, :], ASZ)
        posi = sb("posi", [P, 2], I32)[:, :]
        flag = sb("flag", [P, 2], I32)[:, :]
        NPD = 12
        psem = [ctx.enter_context(nc.semaphore(f"s_pd{i}")) for i in range(NPD)]
        puse = [0] * NPD
        pn = [0]
        osem = ctx.enter_context(nc.semaphore("s_out"))

        def mm(o, lhsT, rhs, start, stop, *w):
            Q.emit("pe", lambda e: e.matmul(o, lhsT=lhsT, rhs=rhs, start=start, stop=stop, skip_group_check=True), w, False)

        def tr(o, i, *w):
            n = i.shape[0]
            Q.emit("pe", lambda e: e.transpose(o, i, C["ident"][0:n, 0:n]), w, False)

        def pe_done():
            return Q.done("pe")

        def act(o, i, func, *w, bias=0.0, scale=1.0, acc=None):
            if acc is None:
                return Q.emit("act", lambda e: e.activation(o, i, func, bias=bias, scale=scale), w)
            return Q.emit("act", lambda e: e.activation(o, i, func, bias=bias, scale=scale, accum_out=acc), w)

        def ts(o, i, s1, s2, op0, op1, *w, e="dve"):
            if s2 is None:
                return Q.emit(e, lambda g: g.tensor_scalar(o, i, s1, None, op0), w)
            return Q.emit(e, lambda g: g.tensor_scalar(o, i, s1, s2, op0, op1), w)

        def stt(o, i0, s, i1, op0, op1, *w):
            return Q.emit("dve", lambda g: g.scalar_tensor_tensor(out=o, in0=i0, scalar=s, in1=i1, op0=op0, op1=op1), w)

        def tt(o, a, b, op, *w, e="dve"):
            return Q.emit(e, lambda g: g.tensor_tensor(o, a, b, op), w)

        def cp(o, i, *w, e="dve"):
            if e == "act":
                return Q.emit(e, lambda g: g.copy(o, i), w)
            return Q.emit(e, lambda g: g.tensor_copy(o, i), w)

        def red(o, i, op, *w):
            return Q.emit("dve", lambda g: g.tensor_reduce(o, i, AX, op), w)

        def recip(o, i, *w):
            return Q.emit("dve", lambda g: g.reciprocal(o, i), w)

        def mset(o, v, *w, e="pool"):
            return Q.emit(e, lambda g: g.memset(o, v), w)

        def pdma(o, i, *w):
            k = pn[0] % NPD
            pn[0] += 1
            prev = (f"pd{k}", psem[k], 16 * puse[k])
            puse[k] += 1
            for x in flat([w, prev] if puse[k] > 1 else [w]):
                key = ("pool", x[0])
                if Q.seen.get(key, 0) < x[2]:
                    Q.seen[key] = x[2]
                    Q.q["pool"].append(("wait", x[1], x[2]))
            sem = psem[k]
            Q.q["pool"].append(["dma", lambda e: e.dma_start(o, i).then_inc(sem, 16), None, 0])
            return (f"pd{k}", psem[k], 16 * puse[k])

        def load(src, kc, n):
            i, buf, free = ring.take()
            for x in flat(free):
                key = ("sp", x[0])
                if Q.seen.get(key, 0) < x[2]:
                    Q.seen[key] = x[2]
                    Q.q["sp"].append(("wait", x[1], x[2]))
            ruse[i] += 1
            dst = buf[:, 0:kc * n]
            sem = rsem[i]
            Q.q["sp"].append(["dma", lambda e: e.dma_start(dst, src).then_inc(sem, 16), None, 0])
            view = dst.rearrange("p (c n) -> p c n", c=kc)
            return i, view, ("r%d" % i, rsem[i], 16 * ruse[i])

        def slab(name, off, kc, n):
            src = d[name][off:off + P * kc * n].rearrange("(p f) -> p f", p=P)
            return load(src, kc, n)

        def gemm_t(xt, w, tok, n, evac, kcs=8, *extra):
            for t in range(2):
                b, ps, fr = bank.take()
                for c in range(kcs):
                    mm(ps[:, 0:n], xt[:, c, t * P:(t + 1) * P], w[:, c, 0:n], c == 0, c == kcs - 1, fr, tok, extra)
                bank.give(b, evac(t, ps[:, 0:n], pe_done()))

        def gemm_f(xt, w, tok, nf, evac, kcs=8, *extra):
            for f in range(0, nf, 2):
                b, ps, fr = bank.take()
                for j in range(2):
                    for c in range(kcs):
                        mm(ps[:, j * T:(j + 1) * T], w[:, c, (f + j) * P:(f + j + 1) * P], xt[:, c, :],
                           c == 0, c == kcs - 1, fr, tok, extra)
                bank.give(b, evac(f // 2, ps[:, :].rearrange("p (a b) -> p a b", a=2), pe_done()))

        flip = [0]

        def copy_any(o, i, *w):
            flip[0] ^= 1
            return cp(o, i, *w, e="act" if flip[0] else "dve")

        def transpose_to(dst, src_of, n, t, toks, extra=()):
            last = []
            for c0 in range(0, n, 4):
                m = min(4, n - c0)
                b, ps, fr = bank.take()
                for j in range(m):
                    tr(ps[:, j * P:(j + 1) * P], src_of(c0 + j), fr, toks, extra)
                k = copy_any(dst[:, c0:c0 + m, t * P:(t + 1) * P],
                             ps[:, 0:m * P].rearrange("p (a b) -> p a b", a=m), pe_done(), extra)
                bank.give(b, k)
                last.append(k)
            return last

        def rsqrt_small(o, i, mul, eps, *w):
            k = ts(o, i, mul, eps, ALU.mult, ALU.add, *w)
            n = o.shape[-1]
            return tt(o, o, C["half"][:, 0:n], ALU.pow, k, e="pool")

        def barrier():
            toks = Q.all_done()
            for e in ("pe", "act", "dve", "pool"):
                for x in toks:
                    key = (e, x[0])
                    if Q.seen.get(key, 0) < x[2]:
                        Q.seen[key] = x[2]
                        Q.q[e].append(("wait", x[1], x[2]))
            arena.pos = arena.base
            return toks

        all_done = Q.all_done

        filler = []
        after = []

        def step(n=1):
            for _ in range(n):
                while after:
                    after.pop(0)()
                if filler:
                    filler.pop(0)()

        def flush():
            while filler or after:
                step()

        def to_xt(toks):
            xv = X.rearrange("p t (q c) -> p t q c", c=8)
            out_ = []
            for t in range(2):
                out_ += transpose_to(XT, lambda c, t=t: xv[:, t, :, c], 8, t, toks)
            return out_

        def layer_norm(toks, ptok):
            st = small[:, 0:24].rearrange("p (t a b) -> p t a b", t=2, a=2)
            mv = small[:, 24:28].rearrange("p (t a) -> p t a", t=2)
            rs = small[:, 28:30]
            ks = []
            for t in range(2):
                kk = []
                for h in range(2):
                    o, i = st[:, t, h, :], X[:, t, h * 512:(h + 1) * 512]
                    kk.append(Q.emit("dve", lambda e, o=o, i=i: e.bn_stats(o, i), [toks]))
                o, i = mv[:, t, :], st[:, t, :, :]
                ks.append(Q.emit("dve", lambda e, o=o, i=i: e.bn_aggr(o, i), kk))
            k = rsqrt_small(rs, mv[:, :, 1], 1.0, 1e-5, ks)
            out_ = []
            xv = X.rearrange("p t (q c) -> p t q c", c=8)
            for t in range(2):
                a = ts(X[:, t, :], X[:, t, :], mv[:, t, 0:1], rs[:, t:t + 1], ALU.subtract, ALU.mult, k)
                a = tt(X[:, t, :], X[:, t, :], GB[:, 0, :], ALU.mult, a, ptok)
                a = tt(X[:, t, :], X[:, t, :], GB[:, 1, :], ALU.add, a)
                out_ += transpose_to(XT, lambda c, t=t: xv[:, t, :, c], 8, t, a)
            return out_

        def bcast(src):
            return src.partition_broadcast(P)

        def mlp(l, xtok):
            arena.pos = 0
            hT = arena.get(32, T)
            hk = []
            queue_ada(l)
            for s in range(8):
                r, w, tok = slab("mlp_w1", (l * 8 + s) * P * SLAB, 8, 512)

                def ev(fp, ps, k, s=s):
                    h = hT[:, 4 * s + 2 * fp:4 * s + 2 * fp + 2, :]
                    a = act(h, ps, ACT.Relu, k)
                    hk.append(tt(h, h, h, ALU.mult, a))
                    return a
                gemm_f(XT, w, tok, 4, ev, 8, xtok)
                ring.give(r, pe_done())
                step()
            bs = [bank.take() for _ in range(4)]
            for s in range(8):
                r, w, tok = slab("mlp_w2", (l * 8 + s) * P * SLAB, 4, 1024)
                if s < 6:
                    step()
                for t in range(2):
                    for n in range(2):
                        b, ps, fr = bs[t * 2 + n]
                        for c in range(4):
                            mm(ps, hT[:, 4 * s + c, t * P:(t + 1) * P], w[:, c, n * 512:(n + 1) * 512],
                               s == 0 and c == 0, s == 7 and c == 3, fr, tok, hk[2 * s:2 * s + 2])
                ring.give(r, pe_done())
            k = pe_done()
            out_ = []
            for t in range(2):
                for n in range(2):
                    b, ps, fr = bs[t * 2 + n]
                    x = X[:, t, n * 512:(n + 1) * 512]
                    a = stt(x, x, ALPHA, ps, ALU.mult, ALU.add, k)
                    bank.give(b, a)
                    out_.append(a)
            return out_

        def residual_gemm(name, lay, lt, ltok, evac, off0=0):
            ns, kc, n = lay
            if kc == 8:
                for s in range(ns):
                    r, w, tok = slab(name, off0 + s * P * SLAB, 8, 512)
                    gemm_t(lt, w, tok, 512, lambda t, ps, k, s=s: evac(t, s, ps, k), 8, ltok)
                    ring.give(r, pe_done())
            else:
                bs = [bank.take() for _ in range(4)]
                for s in range(ns):
                    r, w, tok = slab(name, off0 + s * P * SLAB, 4, 1024)
                    for t in range(2):
                        for n_ in range(2):
                            b, ps, fr = bs[t * 2 + n_]
                            for c in range(4):
                                mm(ps, lt[:, 4 * s + c, t * P:(t + 1) * P], w[:, c, n_ * 512:(n_ + 1) * 512],
                                   s == 0 and c == 0, s == ns - 1 and c == 3, fr, tok, ltok[s])
                    ring.give(r, pe_done())
                k = pe_done()
                for t in range(2):
                    for n_ in range(2):
                        b, ps, fr = bs[t * 2 + n_]
                        bank.give(b, evac(t, n_, ps, k))

        def rope(ps, nh, ctab, stab, outs, tmp, tmpfree, *w):
            n = nh * 64
            a = tmp[:, 0:n].rearrange("p (h x) -> p h x", h=nh)
            b = tmp[:, n:2 * n].rearrange("p (h x) -> p h x", h=nh)
            cb = ctab.unsqueeze(1).to_broadcast([P, nh, 64])
            s1 = stab[:, 0:32].unsqueeze(1).to_broadcast([P, nh, 32])
            s2 = stab[:, 32:64].unsqueeze(1).to_broadcast([P, nh, 32])
            k1 = tt(a, ps, cb, ALU.mult, tmpfree, *w)
            k2 = tt(b[:, :, 0:32], ps[:, :, 32:64], s1, ALU.mult, tmpfree, *w)
            k3 = tt(b[:, :, 32:64], ps[:, :, 0:32], s2, ALU.mult, tmpfree, *w)
            ks = [tt(o, a, b, ALU.add, k1, k2, k3) for o in outs]
            return [k1, k2, k3], ks

        def attention(n, heads, sc, pr, ptb, st):
            S = {}

            def scores(h):
                H = heads(h)
                b, ps, fr = bank.take()
                H["mm"](ps, fr)
                k = pe_done()
                i, s, sf = sc.take()
                n_ = H["width"]
                a = stt(s[:, 0:n_], ps[:, 0:n_], H["scale"], H["bias"], ALU.mult, ALU.add, k, sf, H.get("btok"))
                bank.give(b, a)
                q, sm, smf = st.take()
                if H["cols"][0] == (0, 256):
                    rs = [red(sm[:, 0:2], s.rearrange("p (t k) -> p t k", t=2), ALU.max, a, smf)]
                else:
                    rs = [red(sm[:, t:t + 1], s[:, o0:o1], ALU.max, a, smf) for t, (o0, o1) in enumerate(H["cols"])]
                sink = H.get("sink")
                if sink is not None:
                    x = sm[:, 0:2]
                    rs = [ts(x, x, sink, None, ALU.max, None, rs)]
                ng = ts(sm[:, 2:4], sm[:, 0:2], -1.0, None, ALU.mult, None, rs)
                es = []
                j, p_, pf = pr.take()
                for t in range(2):
                    o0, o1 = H["cols"][t]
                    es.append(act(p_[:, o0:o1], s[:, o0:o1], ACT.Exp, ng, pf, bias=sm[:, 2 + t:3 + t],
                                  acc=sm[:, 4 + t:5 + t]))
                    if sink is not None:
                        es.append(act(sm[:, 6 + t:7 + t], sink, ACT.Exp, ng, bias=sm[:, 2 + t:3 + t]))
                sc.give(i, es)
                S[h] = (H, j, p_, q, sm, es)

            def normalise(h):
                H, j, p_, q, sm, es = S[h]
                if H.get("sink") is not None:
                    es = [tt(sm[:, 4:6], sm[:, 4:6], sm[:, 6:8], ALU.add, es)]
                rc = recip(sm[:, 8:10], sm[:, 4:6], es)
                nk = []
                for t in range(2):
                    o0, o1 = H["cols"][t]
                    nk.append(ts(p_[:, o0:o1], p_[:, o0:o1], sm[:, 8 + t:9 + t], None, ALU.mult, None, rc))
                st.give(q, nk, es)
                S[h] = (H, j, p_, nk)

            def turn(h):
                H, j, p_, nk = S[h]
                b, ps, fr = bank.take()
                for (t, kc, c0) in H["blocks"]:
                    tr(ps[:, kc * T + t * P:kc * T + (t + 1) * P], p_[:, c0:c0 + P], fr, nk)
                k = pe_done()
                pr.give(j, k)
                m, pt, pf = ptb.take()
                if len(H["blocks"]) == 4:
                    kk = cp(pt, ps, k, pf, e="act")
                else:
                    kk = [cp(pt[:, 0:T], ps[:, 0:T], k, pf, e="act"), cp(pt[:, T + P:], ps[:, T + P:], k, pf, e="act")]
                bank.give(b, kk)
                S[h] = (H, m, pt, kk)

            def apply(h):
                H, m, pt, kk = S.pop(h)
                ptb.give(m, H["pv"](pt, kk))

            for i in range(n + 2):
                if i < n:
                    scores(i)
                if 1 <= i <= n:
                    normalise(i - 1)
                step()
                if 1 <= i <= n:
                    turn(i - 1)
                step()
                if i >= 2:
                    apply(i - 2)

        def att_bufs():
            sc = Rot([arena.get(512) for _ in range(2)])
            pr = Rot([arena.get(512) for _ in range(3)])
            ptb = Rot([arena.get(512) for _ in range(2)])
            st = Rot([arena.get(16) for _ in range(3)])
            return sc, pr, ptb, st

        def general_experts(l, av, wc, arena_hid, main, extra):
            G = Queues(nc, ctx, f"_g{l}")
            gsem = [ctx.enter_context(nc.semaphore(f"s_gr{l}_{j}")) for j in range(3)]
            for e in ("pe", "act", "dve", "sp"):
                for x in main:
                    G.q[e].append(("wait", x[1], x[2]))
            w1, w3, w2 = [ringt[:, j * SLAB:(j + 1) * SLAB] for j in range(3)]
            w1v, w3v = (w.rearrange("p (c n) -> p c n", c=8) for w in (w1, w3))
            w2v = w2.rearrange("p (c n) -> p c n", c=4)
            s_ = arena_hid[0][0].rearrange("p (a b) -> p a b", a=2)
            hd = arena_hid[1][0].rearrange("p a b -> p (a b)").rearrange("p (a b) -> p a b", a=4)
            ld = {}
            hdone = None
            last = {}

            def gmm(o, a, b, st, sp_, *w):
                G.emit("pe", lambda g: g.matmul(o, lhsT=a, rhs=b, start=st, stop=sp_, skip_group_check=True), w, False)

            for e in range(NE):
                toks = []
                for j, (nm, dst) in enumerate((("exp_w1", w1), ("exp_w3", w3), ("exp_w2", w2))):
                    off = (l * NE + e) * P * SLAB
                    src = d[nm][off:off + P * SLAB].rearrange("(p f) -> p f", p=P)
                    if j in ld:
                        G.q["sp"].append(("wait", ld[j][1], ld[j][2]))
                    sem = gsem[j]
                    G.q["sp"].append(["dma", lambda g, dst=dst, src=src, sem=sem: g.dma_start(dst, src).then_inc(sem, 16),
                                      None, 0])
                    toks.append((f"gr{j}", sem, 16 * (e + 1)))
                hk = []
                for fp in range(2):
                    pa, pb = psb[2 * fp][:, :], psb[2 * fp + 1][:, :]
                    for ps, wv, tk_ in ((pa, w1v, toks[0]), (pb, w3v, toks[1])):
                        for j in range(2):
                            for c in range(8):
                                gmm(ps[:, j * T:(j + 1) * T], wv[:, c, 2 * fp + j:512:4], XT[:, c, :], c == 0, c == 7,
                                    tk_, last.get(fp))
                    kd = G.done("pe")
                    if fp == 1:
                        ld[0] = ld[1] = kd
                    pav = pa.rearrange("p (a b) -> p a b", a=2)
                    pbv = pb.rearrange("p (a b) -> p a b", a=2)
                    a = G.emit("act", lambda g, pav=pav: g.activation(s_, pav, ACT.Silu), [kd, last.get(1 - fp)])
                    o = hd[:, 2 * fp:2 * fp + 2, :]
                    last[fp] = G.emit("dve", lambda g, o=o, pbv=pbv: g.tensor_tensor(o, s_, pbv, ALU.mult),
                                      [a, kd, ld.get(2)])
                    hk.append(last[fp])
                for t in range(2):
                    for n in range(2):
                        ps = psb[4 + 2 * t + n][:, :]
                        for c in range(4):
                            gmm(ps, hd[:, c, t * P:(t + 1) * P], w2v[:, c, n * 512:(n + 1) * 512], c == 0, c == 3,
                                toks[2], hk, last.get((t, n)))
                ld[2] = kd = G.done("pe")
                for t in range(2):
                    for n in range(2):
                        ps = psb[4 + 2 * t + n][:, :]
                        o = av[:, t, n * 512:(n + 1) * 512]
                        wcol = wc[:, t, e:e + 1]
                        if e == 0:
                            fn = lambda g, o=o, ps=ps, wcol=wcol: g.tensor_scalar(o, ps, wcol, None, ALU.mult)
                        else:
                            fn = lambda g, o=o, ps=ps, wcol=wcol: g.scalar_tensor_tensor(
                                out=o, in0=ps, scalar=wcol, in1=o, op0=ALU.mult, op1=ALU.add)
                        last[t, n] = G.emit("dve", fn, [kd, last.get((t, n))])
            for e in ("pe", "act", "dve", "pool", "sp"):
                for f in ("pe", "act", "dve"):
                    G.q[e].append(("wait", G.sem[f], G.cnt[f]))
            col = flag[0:1, l:l + 1]
            for e in ("pe", "act", "dve", "pool", "sp"):
                Q.q[e].append(("wait", flag_wait[0][1], flag_wait[0][2]))
                Q.q[e].append(("branch", col, G.q[e]))

        flag_wait = [None]
        modc = [sb(f"modc{l}", [P, 512])[:, :] for l in range(2)]
        modk_ = [None, None]

        def queue_ada(l):
            acc = Rot([arena.get(512) for _ in range(2)])
            ab = arena.get(512)
            hold = {}

            def piece(s):
                if s == 0:
                    hold["b"] = bank.take()
                    hold["ab"] = pdma(ab[0:12, :], d["ada_b"][l * 12:l * 12 + 12, :], ada_free)
                if s < 12:
                    r, w, tok = slab("ada_w", (l * 12 + s) * P * SLAB, 8, 512)
                    i, m_, mf = acc.take()
                    k = ts(m_, w[:, 0, :], csil[:, 0:1], None, ALU.mult, None, tok, mf, ck, ada_free)
                    for c in range(1, 8):
                        k = stt(m_, w[:, c, :], csil[:, c:c + 1], m_, ALU.mult, ALU.add, k)
                    ring.give(r, k)
                    hold[s] = (i, m_, k)
                if s >= 1:
                    i, m_, k = hold.pop(s - 1)
                    b, ps, fr = hold["b"]
                    mm(ps[0:12, :], C["e12"][:, 12 - s:24 - s], m_, s == 1, s == 12, fr, k)
                    acc.give(i, pe_done())
                if s == 12:
                    b, ps, fr = hold["b"]
                    a = tt(modc[l][0:12, :], ps[0:12, :], ab[0:12, :], ALU.add, pe_done(), hold["ab"])
                    modk_[l] = a
                    bank.give(b, a)
            ada_free = all_done()
            for s in range(13):
                filler.append(lambda s=s: piece(s))

        xsem = ctx.enter_context(nc.semaphore("s_x"))
        isem = ctx.enter_context(nc.semaphore("s_ident"))
        xsrc = d["x"].rearrange("(t p) f -> p t f", p=P)
        Q.q["sp"].append(["dma", lambda e: e.dma_start(X, xsrc).then_inc(xsem, 16), None, 0])
        Q.q["sp"].append(["dma", lambda e: e.dma_start(C["ident"], d["const_ident"]).then_inc(isem, 16), None, 0])
        xl = ("x", xsem, 16)
        ct = {"ident": ("ident", isem, 16)}
        for name in sorted(consts, key=lambda n: n not in ("ropec", "ropes")):
            if name not in ("half", "ones", "ident") + LATE:
                ct[name] = pdma(C[name], d["const_" + name])
        ct["half"] = mset(C["half"], -0.5)
        onesk = mset(C["ones"], 1.0)
        ctoks = list(ct.values()) + [onesk]
        ck = pdma(small[:, 44:52], d["c"].rearrange("(p c) -> p c", c=8))
        csil = small[:, 52:60]
        ck = act(csil, small[:, 44:52], ACT.Silu, ck)
        gk = [pdma(GB[:, j, :], bcast(d[nm][0:1, :])) for j, nm in ((0, "ln1_g"), (1, "ln1_b"))]
        xtok = to_xt([xl, ct["ident"]])

        arena.pos = 0
        qT = arena.get(4, T)
        kT = arena.get(2, T)
        qbT = arena.get(4, T)
        kbT = arena.get(4, T)
        vA = arena.get(2, P)
        vB = arena.get(2, 512)
        OT = arena.get(8, T)
        qtok = arena.get(2, 512)
        kdup = arena.get(2, 256)
        sinkb = arena.get(8)
        rot_tmp = arena.get(1024)
        sk = pdma(sinkb, bcast(d["attn_sink"][0:1, :]))
        ro = [[]]
        qk = [None, None]
        kk = [None, None]

        r, w, tok = slab("attn_w_in", 0, 8, 512)

        def ev(t, ps, k):
            reads, ks = rope(ps.rearrange("p (h x) -> p h x", h=8), 8, C["ropec"][:, t * 64:t * 64 + 64],
                             C["ropes"][:, t * 64:t * 64 + 64],
                             [qtok[:, t, :].rearrange("p (h x) -> p h x", h=8)], rot_tmp, ro[0], k, ct["ropec"],
                             ct["ropes"])
            ro[0] = ks
            qk[t] = ks
            return reads
        gemm_t(XT, w, tok, 512, ev, 8, xtok)
        ring.give(r, pe_done())
        r, w, tok = slab("attn_w_in", P * 4096, 8, 256)
        vk = []

        def ev(t, ps, k):
            kv = kdup[:, t, :].rearrange("p (g c x) -> p g c x", g=2, c=2)
            reads, ks = rope(ps[:, 0:128].rearrange("p (h x) -> p h x", h=2), 2, C["ropec"][:, t * 64:t * 64 + 64],
                             C["ropes"][:, t * 64:t * 64 + 64], [kv[:, :, 0, :], kv[:, :, 1, :]], rot_tmp, ro[0], k)
            ro[0] = ks
            kk[t] = ks
            a = cp(vA[:, t, :], ps[:, 128:256], k, reads, e="act")
            vk.append(a)
            return [reads, a]
        gemm_t(XT, w, tok, 256, ev, 8)
        ring.give(r, pe_done())
        bk = []
        bslab = {}

        def proj_b(j):
            if j in (0, 4, 8):
                bslab[0] = slab("attn_w_in", P * (6144 + 1024 * j), 8, 512)
            r, w, tok = bslab[0]
            b, ps, fr = bank.take()
            for c in range(8):
                if j < 8:
                    mm(ps[:, 0:T], w[:, c, (j % 4) * P:(j % 4 + 1) * P], XT[:, c, :], c == 0, c == 7, fr, tok)
                else:
                    mm(ps, XT[:, c, (j - 8) * P:(j - 7) * P], w[:, c, :], c == 0, c == 7, fr, tok)
            kd = pe_done()
            if j in (3, 7, 9):
                ring.give(r, kd)
            if j < 8:
                a = cp((qbT if j < 4 else kbT)[:, j % 4, :], ps[:, 0:T], kd, e="act")
                bk.append(a)
            else:
                a = cp(vB[:, j - 8, :], ps, kd, e="act")
                vk.append(a)
            bank.give(b, a)
        for j in range(10):
            filler.append(lambda j=j: proj_b(j))
        tk = []
        for t in range(2):
            tk += transpose_to(qT, lambda c, t=t: qtok[:, t, c * P:(c + 1) * P], 4, t, qk[t])
            tk += transpose_to(kT, lambda c, t=t: kdup[:, t, c * P:(c + 1) * P], 2, t, kk[t])

        sc, pr, ptb, st = att_bufs()
        obank = {}
        otk = []

        def heads(h):
            if h < 8:
                qa, ka, va = qT[:, h // 2, :], kT[:, h // 4, :], vA[:, :, 64 * (h // 4):64 * (h // 4) + 64]
            else:
                g = h - 8
                qa, ka, va = qbT[:, g // 2, :], kbT[:, g // 2, :], vB[:, :, 64 * g:64 * g + 64]
            p0 = 64 * (h % 2)

            def m(ps, fr):
                for t in range(2):
                    mm(ps[:, t * T:(t + 1) * T], qa[p0:p0 + 64, t * P:(t + 1) * P], ka[p0:p0 + 64, :], True, True,
                       fr, tk, bk)

            def pv(pt, k):
                if h % 2 == 0:
                    obank[0] = bank.take()
                b, ps, fr = obank[0]
                for kc in range(2):
                    mm(ps[p0:p0 + 64, 0:T], va[:, kc, :], pt[:, kc * T:(kc + 1) * T], kc == 0, kc == 1, fr, k, vk)
                kd = pe_done()
                if h % 2 == 1:
                    a = copy_any(OT[:, h // 2, :], ps[:, 0:T], kd)
                    otk.append(a)
                    bank.give(b, a)
                return kd
            H = dict(mm=m, pv=pv, width=512, scale=0.125, cols=[(0, 256), (256, 512)],
                     blocks=[(t, kc, t * T + kc * P) for kc in range(2) for t in range(2)])
            if h < 8:
                H["bias"], H["sink"] = C["maska"], sinkb[:, h:h + 1]
                H["btok"] = [sk, ctoks]
            else:
                H["bias"], H["btok"] = wb[:, h - 8, :], btok
            return H
        attention(8, heads, sc, pr, ptb, st)
        flush()
        rb, wb, btok = load(d["attn_bias"].rearrange("(p f) -> p f", p=P), 8, 512)
        r1, w1_, tok1 = slab("attn_w_out", 0, 4, 1024)
        mixb = []
        ots = list(otk)

        def out_a(q):
            b, ps, fr = bank.take()
            mixb.append((b, ps))
            t, n = q // 2, q % 2
            for c in range(4):
                mm(ps, OT[:, c, t * P:(t + 1) * P], w1_[:, c, n * 512:(n + 1) * 512], c == 0, False, fr, tok1, ots)
            if q == 3:
                ring.give(r1, pe_done())
        for q in range(4):
            filler.append(lambda q=q: out_a(q))
        attention(8, lambda h: heads(h + 8), sc, pr, ptb, st)
        flush()
        ring.give(rb, Q.done("dve"))

        rk = []

        def ev(t, n, ps, k):
            x = X[:, t, n * 512:(n + 1) * 512]
            a = stt(x, x, ALPHA, ps, ALU.mult, ALU.add, k)
            rk.append(a)
            return a
        r1, w2_, tok1 = slab("attn_w_out", P * SLAB, 4, 1024)
        for q, (b, ps) in enumerate(mixb):
            t, n = q // 2, q % 2
            for c in range(4):
                mm(ps, OT[:, 4 + c, t * P:(t + 1) * P], w2_[:, c, n * 512:(n + 1) * 512], False, c == 3, tok1, otk)
            bank.give(b, ev(t, n, ps, pe_done()))
        ring.give(r1, pe_done())
        xtok = layer_norm(rk, gk)

        def next_gb(a, b, ia, ib, toks):
            return [pdma(GB[:, 0, :], bcast(d[a][ia:ia + 1, :]), toks),
                    pdma(GB[:, 1, :], bcast(d[b][ib:ib + 1, :]), toks)]

        gk = next_gb("ln2_g", "ln2_b", 0, 0, Q.done("dve"))
        barrier()
        rk = mlp(0, xtok)
        xtok = layer_norm(rk, gk)
        gk = next_gb("ln1_g", "ln1_b", 1, 1, Q.done("dve"))

        barrier()
        zT = arena.get(16, T)
        xcT = arena.get(32, T)
        xF = arena.get(2, 2048)
        xB = arena.get(2, 2048)
        pos0 = arena.pos
        prm = arena.get(32, 6)
        dd = arena.get(32)
        dtt = arena.get(2, 64)
        aa = arena.get(2, 64)
        dtb = arena.get(64)
        ang = arena.get(64)
        ups = Rot([arena.get(2, 260) for _ in range(2)])
        cvs = Rot([arena.get(2, T) for _ in range(2)])
        k1 = pdma(prm, d["ssm_conv"].rearrange("p (a b) -> p a b", a=32))
        k2 = pdma(dd, d["ssm_dn"])
        k3 = pdma(dtb, bcast(d["ssm_dt_bias"][0:1, :]))
        k4 = pdma(ang, bcast(d["ssm_A_log"][0:1, :]))
        zz = [ctoks] + [mset(u[:, :, 0:2], 0.0) for u in ups.bufs] + [mset(u[:, :, 258:260], 0.0) for u in ups.bufs]
        r, w, tok = slab("ssm_w_dt", 0, 8, 64)
        dk = []

        def ev(t, ps, k):
            a = tt(dtt[:, t, :], ps, dtb, ALU.add, k, k3)
            dk.append(a)
            return a
        gemm_t(XT, w, tok, 64, ev, 8, xtok)
        ring.give(r, pe_done())
        k = ts(aa, dtt, -1.0, None, ALU.mult, None, dk)
        k = tt(aa, aa, dtt, ALU.min, k)
        k = act(aa, aa, ACT.Exp, k)
        k = act(aa, aa, ACT.Ln, k, bias=1.0)
        k = stt(dtt, dtt, 0.0, aa, ALU.max, ALU.add, k)
        ka = act(ang, ang, ACT.Exp, k4)
        ka = ts(ang, ang, -1.0, None, ALU.mult, None, ka)
        ak = tt(aa, dtt, ang.unsqueeze(1).to_broadcast([P, 2, 64]), ALU.mult, k, ka)
        zk = []
        for s in range(4):
            r, w, tok = slab("ssm_w_in", s * P * SLAB, 8, 512)

            def ev(fp, ps, k, s=s):
                a = act(zT[:, 4 * s + 2 * fp:4 * s + 2 * fp + 2, :], ps, ACT.Silu, k)
                zk.append(a)
                return a
            gemm_f(XT, w, tok, 4, ev)
            ring.give(r, pe_done())
        xk = {}
        for s in range(8):
            r, w, tok = slab("ssm_w_in", (4 + s) * P * SLAB, 8, 512)

            def ev(fp, ps, k, s=s):
                f0 = 4 * s + 2 * fp
                i, u, uf = ups.take()
                a = cp(u[:, :, 2:258], ps, k, uf, zz, e="act")
                j, v, vf = cvs.take()
                lk = []
                for q in range(2):
                    f = f0 + q
                    kk_ = act(v[:, q, :], u[:, q, 0:T], ACT.Identity, a, vf, k1,
                              scale=prm[:, f, 0:1], bias=prm[:, f, 5:6])
                    for c in range(1, 5):
                        kk_ = stt(v[:, q, :], u[:, q, c:c + T], prm[:, f, c:c + 1], v[:, q, :], ALU.mult, ALU.add, kk_)
                    lk.append(kk_)
                ups.give(i, lk)
                o = act(xcT[:, f0:f0 + 2, :], v, ACT.Silu, lk)
                cvs.give(j, o)
                xk[f0] = xk[f0 + 1] = o
                return a
            gemm_f(XT, w, tok, 4, ev)
            ring.give(r, pe_done())
        xs_k = []
        for t in range(2):
            for g in range(4):
                b, ps, fr = bank.take()
                for j in range(4):
                    f = 4 * g + j
                    tr(ps[:, j * P:(j + 1) * P], xcT[:, f, t * P:(t + 1) * P], fr, xk[f])
                kd = pe_done()
                pv_ = ps.rearrange("p (h x) -> p h x", h=8)
                for o, dr in ((xF, 0), (xB, 1)):
                    ov = o[:, t, g * 512:(g + 1) * 512].rearrange("p (h x) -> p h x", h=8)
                    dv_ = dtt[:, t, dr * 32 + g * 8:dr * 32 + g * 8 + 8].unsqueeze(2).to_broadcast([P, 8, 64])
                    kl = tt(ov, pv_, dv_, ALU.mult, kd, ak)
                    xs_k.append(kl)
                bank.give(b, kl)
        arena.pos = pos0 + 192 + 32 + 128 + 128 + 64 + 64
        barrier_pos = arena.pos
        pre = all_done()
        cbr = Rot([arena.get(768) for _ in range(2)])
        lmr = Rot([arena.get(2, 3, P) for _ in range(2)])
        emr = Rot([arena.get(768) for _ in range(3)])
        cb_of = {}

        def cb_group(g):
            b, ps, fr = bank.take()
            BT, CT = xcT[:, 16 + g, :], xcT[:, 24 + g, :]
            for s in range(2):
                mm(ps[:, s * T:(s + 1) * T], BT[:, s * P:(s + 1) * P], CT, True, True, fr, xk[16 + g], xk[24 + g])
            kd = pe_done()
            i, cb, cf = cbr.take()
            ks = [tt(cb[:, 0:T], ps[:, 0:T], C["leo"], ALU.mult, kd, cf, pre),
                  tt(cb[:, T:T + P], ps[:, T + P:], C["leo"][:, 0:P], ALU.mult, kd),
                  tt(cb[:, 384:512], ps[:, 0:P], C["oge"][:, P:], ALU.mult, kd),
                  tt(cb[:, 512:768], ps[:, T:], C["oge"], ALU.mult, kd)]
            bank.give(b, ks)
            cb_of[g] = (i, cb, ks)

        LE, GE = C["leo"][:, 0:P], C["oge"][:, P:]
        E_of = {}

        def build_l(h):
            i, L, lf = lmr.take()
            cf_, cb_ = slice(h, h + 1), slice(32 + h, 33 + h)
            k_ = [ts(L[:, 0, 0, :], C["gt"], aa[:, 0, cf_], None, ALU.mult, None, lf, ak, pre),
                  ts(L[:, 0, 2, :], C["ones"], aa[:, 1, cf_], None, ALU.mult, None),
                  ts(L[:, 0, 1, :], C["gt"], aa[:, 1, cf_], None, ALU.mult, None),
                  ts(L[:, 1, 0, :], C["lt"], aa[:, 0, cb_], None, ALU.mult, None),
                  ts(L[:, 1, 1, :], C["lt"], aa[:, 1, cb_], None, ALU.mult, None),
                  ts(L[:, 1, 2, :], C["ones"], aa[:, 0, cb_], None, ALU.mult, None)]
            L_of[h] = (i, L, k_)
        L_of = {}

        def decay(h):
            i, L, k_ = L_of.pop(h)
            j, E, ef = emr.take()
            ek = []
            b, ps, fr = bank.take()
            mm(ps[:, 0:T], L[:, 0, 0, :], C["leo"], True, False, fr, k_)
            mm(ps[:, P:T], L[:, 0, 2, :], LE, False, True)
            mm(ps[:, T:T + P], L[:, 0, 1, :], LE, True, True)
            a = act(E[:, 0:384], ps[:, 0:384], ACT.Exp, pe_done(), ef, pre)
            bank.give(b, a)
            ek.append(a)
            b, ps, fr = bank.take()
            mm(ps[:, 0:P], L[:, 1, 0, :], GE, True, True, fr)
            mm(ps[:, P:384], L[:, 1, 1, :], C["oge"], True, False)
            mm(ps[:, P:T], L[:, 1, 2, :], GE, False, True)
            kd = pe_done()
            lmr.give(i, kd)
            a = act(E[:, 384:768], ps[:, 0:384], ACT.Exp, kd)
            bank.give(b, a)
            ek.append(a)
            E_of[h] = (j, E, ek)

        def weigh(h):
            j, E, ek = E_of[h]
            ci, cb, cks = cb_of[h // 4]
            mk = tt(E, E, cb, ALU.mult, ek, cks)
            if h % 4 == 3:
                cbr.give(ci, mk)
            E_of[h] = (j, E, mk)

        yk = []
        ybk = {}

        def ssm_out(h):
            j, E, mk = E_of.pop(h)
            p0 = 64 * (h % 2)
            if h % 2 == 0:
                ybk[0] = bank.take()
            b, ps, fr = ybk[0]
            o = ps[p0:p0 + 64, :]
            hs = slice(h * 64, h * 64 + 64)
            mm(o[:, 0:T], xF[:, 0, hs], E[:, 0:T], True, False, fr, mk, xs_k)
            mm(o[:, P:T], xF[:, 1, hs], E[:, T:384], False, False)
            mm(o[:, 0:P], xB[:, 0, hs], E[:, 384:512], False, False)
            mm(o[:, 0:T], xB[:, 1, hs], E[:, 512:768], False, True)
            kd = pe_done()
            emr.give(j, kd)
            if h % 2 == 1:
                f = h // 2
                a = stt(xcT[:, f, :], xcT[:, f, :], dd[:, f:f + 1], ps[:, 0:T], ALU.mult, ALU.add, kd, k2)
                bank.give(b, a)
                yk.append(tt(zT[:, f, :], xcT[:, f, :], zT[:, f, :], ALU.mult, a, zk))

        nrm, normed = {}, [[] for _ in range(4)]

        def norm_a(g):
            z2 = zT[:, 2 * g:2 * g + 2, :]
            nrm[g] = tt(xcT[:, 2 * g:2 * g + 2, :], z2, z2, ALU.mult, yk[-2:])

        def norm_b(g):
            b, ps, fr = bank.take()
            for c in range(2):
                mm(ps[:, 0:T], C["ones"], xcT[:, 2 * g + c, :], c == 0, c == 1, fr, nrm[g])
            v = xcT[:, 2 * g, :]
            a = act(v, ps[:, 0:T], ACT.Ln, pe_done(), k_eps, scale=1.0 / 256, bias=epst)
            bank.give(b, a)
            nrm[g] = act(v, v, ACT.Exp, a, scale=-0.5)

        def norm_c(g):
            for f in (2 * g, 2 * g + 1):
                normed[g // 2].append(stt(zT[:, f, :], zT[:, f, :], dd[:, 16 + f:17 + f], xcT[:, 2 * g, :], ALU.mult,
                                          ALU.mult, nrm[g]))
        epst = small[:, 180:181]
        k_eps = mset(epst, 1e-5)
        build_l(0)
        for i in range(36):
            if i < 32:
                if i % 4 == 0:
                    cb_group(i // 4)
                if i < 31:
                    build_l(i + 1)
                decay(i)
            if 1 <= i <= 32:
                weigh(i - 1)
            if 2 <= i < 34:
                ssm_out(i - 2)
            if i >= 5 and i % 4 == 1:
                norm_a((i - 5) // 4)
            if i >= 6 and i % 4 == 2 and (i - 6) // 4 < 8:
                norm_b((i - 6) // 4)
            if i >= 7 and i % 4 == 3 and (i - 7) // 4 < 8:
                norm_c((i - 7) // 4)
        rk = []

        def ev(t, n, ps, k):
            x = X[:, t, n * 512:(n + 1) * 512]
            a = stt(x, x, ALPHA, ps, ALU.mult, ALU.add, k)
            rk.append(a)
            return a
        residual_gemm("ssm_w_out", (4, 4, 1024), zT, normed, ev)
        xtok = layer_norm(rk, gk)
        gk = next_gb("ln2_g", "ln2_b", 1, 1, Q.done("dve"))
        barrier()
        rk = mlp(1, xtok)
        xtok = layer_norm(rk, gk)

        barrier()
        for name in LATE:
            C[name] = arena.get(consts[name])
        ctoks = [pdma(C[name], d["const_" + name]) for name in ("cm", "dmask")]
        arena.base = arena.pos
        ctab = C["rope2c"]
        stab = C["rope2s"]
        posf = small[:, 40:42]
        kp = pdma(posi, d["positions"])
        k = cp(posf, posi, kp)
        A = arena.get(2, 32)
        Bk = arena.get(2, 32)
        for t in range(2):
            k = ts(A[:, t, :], C["inv"], posf[:, t:t + 1], None, ALU.mult, None, k)
        MAGIC = 12582912.0
        k = ts(Bk, A, float(1.0 / (2 * np.pi)), MAGIC, ALU.mult, ALU.add, k)
        k = ts(Bk, Bk, MAGIC, None, ALU.subtract, None, k)
        for cst in (6.28125, 0.0019350051879882812, 3.019916050995584e-07):
            k = stt(A, Bk, -cst, A, ALU.mult, ALU.add, k)
        PI = 3.1415925
        k = ts(A, A, PI, -PI, ALU.min, ALU.max, k)
        sv = stab.rearrange("p (t x) -> p t x", t=2)
        cv = ctab.rearrange("p (t x) -> p t x", t=2)
        k5 = act(sv[:, :, 32:64], A, ACT.Sin, k)
        k6 = ts(sv[:, :, 0:32], sv[:, :, 32:64], -1.0, None, ALU.mult, None, k5)
        k = ts(A, A, float(np.pi / 2), None, ALU.add, None, k5)
        k = ts(Bk, A, float(np.pi), float(-2 * np.pi), ALU.is_gt, ALU.mult, k)
        k = tt(A, A, Bk, ALU.add, k)
        k = ts(A, A, PI, -PI, ALU.min, ALU.max, k)
        k7 = act(cv[:, :, 0:32], A, ACT.Sin, k)
        k8 = cp(cv[:, :, 32:64], cv[:, :, 0:32], k7)
        ropek = [k6, k7, k8]
        hh_done = [None, None]

        def rms(src, nf, o, tokw, w_):
            js = arena.get(nf)
            ks = []
            pk = None
            for t in range(2):
                pk = act(js, src(t), ACT.Square, tokw, pk, acc=o[:, t:t + 1])
                ks.append(pk)
            return rsqrt_small(o, o, 1.0 / nf, 1e-6, ks, w_)

        for l in range(2):
            assert not filler
            barrier()
            MOD = arena.get(6, D)
            mbase = arena.pos
            gk = next_gb("norm1_g", "norm2_g", l, l, all_done())
            modk = {}

            def spread(s):
                b, ps, fr = bank.take()
                mm(ps, C["ident"][0:12, s:s + 1].to_broadcast([12, P]), modc[l][0:12, :], True, True, fr, modk_[l],
                   mod_free)
                a = cp(MOD[:, s // 2, (s % 2) * 512:(s % 2) * 512 + 512], ps, pe_done(), e="act")
                bank.give(b, a)
                modk[s] = a
            mod_free = all_done()
            for s in range(4):
                spread(s)
            for s in range(4, 12):
                filler.append(lambda s=s: spread(s))
            g1 = stt(MOD[:, 1, :], MOD[:, 1, :], 1.0, GB[:, 0, :], ALU.add, ALU.mult, list(modk.values()), gk)

            def norm_mod(si, gi, w_, hh=None):
                if hh is None:
                    hh = arena.get(2, D)
                rs = small[:, 60:62]
                k = rms(lambda t: X[:, t, :], D, rs, w_, w_)
                hv = hh.rearrange("p t (q c) -> p t q c", c=8)
                out_ = []
                for t in range(2):
                    a = stt(hh[:, t, :], X[:, t, :], rs[:, t:t + 1], MOD[:, gi, :], ALU.mult, ALU.mult, k, g1 if gi == 1 else g2)
                    a = tt(hh[:, t, :], hh[:, t, :], MOD[:, si, :], ALU.add, a)
                    hh_done[t] = a
                    out_ += transpose_to(XT, lambda c, t=t: hv[:, t, :, c], 8, t, a, w_)
                return out_
            htok = norm_mod(0, 1, [rk, list(modk.values())])
            barrier()
            arena.pos = mbase
            gb = arena.get(24)
            kgb = pdma(gb, d["gate_b"][l * P:(l + 1) * P, :], mod_free)
            xbase = arena.pos
            yT = [arena.get(4, T) for _ in range(3)]
            gT = arena.get(24, T)
            work = arena.pos
            gtk = {}
            gslab = {}

            def gate(q):
                if q % 4 == 0:
                    gslab[0] = slab("gate_w", (l * 6 + q // 4) * P * SLAB, 8, 512)
                r, w, tok = gslab[0]
                b, ps, fr = bank.take()
                for c in range(8):
                    mm(ps[:, 0:T], w[:, c, (q % 4) * P:(q % 4 + 1) * P], XT[:, c, :], c == 0, c == 7, fr, tok, htok)
                kd = pe_done()
                if q % 4 == 3:
                    ring.give(r, kd)
                a = act(gT[:, q, :], ps[:, 0:T], ACT.Exp, kd, ngb, bias=gb[:, q:q + 1], scale=-1.0)
                bank.give(b, a)

                def rest():
                    k = ts(gT[:, q, :], gT[:, q, :], 1.0, None, ALU.add, None, a)
                    gtk[q] = recip(gT[:, q, :], gT[:, q, :], k)
                after.append(rest)
            ngb = ts(gb, gb, -1.0, None, ALU.mult, None, kgb)
            for q in range(24):
                filler.append(lambda q=q: gate(q))
            rqk = arena.get(2, 512)
            rqT = arena.get(2, T)
            rkT = arena.get(2, T)
            rv = arena.get(2, 512)
            rg = arena.get(2, 512)
            tmp = arena.get(1024)
            ra_pos = arena.pos
            woff = l * P * (7 * 4096 - 8 * 60)
            ro[0] = []
            qk2 = [None, None]
            r, w, tok = slab("w_in2", woff, 8, 512)

            def ev(t, ps, k):
                reads, ks = rope(ps.rearrange("p (h x) -> p h x", h=8), 8, ctab[:, t * 64:t * 64 + 64],
                                 stab[:, t * 64:t * 64 + 64],
                                 [rqk[:, t, :].rearrange("p (h x) -> p h x", h=8)], tmp, ro[0], k, ropek)
                ro[0] = ks
                qk2[t] = ks
                return reads
            gemm_t(XT, w, tok, 512, ev, 8, htok)
            ring.give(r, pe_done())
            rvk, rgk = [], []
            r, w, tok = slab("w_in2", woff + P * 4096, 8, 512)

            def ev(t, ps, k):
                a = copy_any(rv[:, t, :], ps, k)
                rvk.append(a)
                return a
            gemm_t(XT, w, tok, 512, ev)
            ring.give(r, pe_done())
            r, w, tok = slab("w_in2", woff + P * 8192, 8, 512)

            def ev(t, ps, k):
                a = act(rg[:, t, :], ps, ACT.Silu, k)
                rgk.append(a)
                return a
            gemm_t(XT, w, tok, 512, ev)
            ring.give(r, pe_done())
            tk = []
            for t in range(2):
                tk += transpose_to(rqT, lambda c, t=t: rqk[:, t, c * P:(c + 1) * P], 2, t, qk2[t])
                tk += transpose_to(rkT, lambda c, t=t: rqk[:, t, 256 + c * P:256 + (c + 1) * P], 2, t, qk2[t])
            smr = Rot([arena.get(384) for _ in range(2)])
            ob = [bank.take() for _ in range(2)]
            for h in range(4):
                p0 = 64 * (h % 2)
                b, ps, fr = bank.take()
                kh, qh = rkT[p0:p0 + 64, h // 2, :], rqT[p0:p0 + 64, h // 2, :]
                mm(ps[:, 0:T], kh[:, 0:P], qh, True, True, fr, tk)
                mm(ps[:, T:384], kh[:, P:T], qh[:, P:T], True, True)
                i, s_, sf = smr.take()
                a = tt(s_, ps[:, 0:384], C["dmask"][:, h * 384:(h + 1) * 384], ALU.mult, pe_done(), sf, ctoks)
                bank.give(b, a)
                step()
                hs = slice(h * P, h * P + P)
                mm(ob[0][1][:, hs], s_[:, 0:P], rv[:, 0, hs], True, True, ob[0][2], a, rvk)
                mm(ob[1][1][:, hs], s_[:, P:T], rv[:, 0, hs], True, False, ob[1][2])
                mm(ob[1][1][:, hs], s_[:, T:384], rv[:, 1, hs], False, True)
                smr.give(i, pe_done())
            kd = pe_done()
            step(3)
            st8 = small[:, 64:112].rearrange("p (a b) -> p a b", a=8)
            mv8 = small[:, 112:128].rearrange("p (a b) -> p a b", a=8)
            rs8 = small[:, 128:136]
            ks = []
            for t in range(2):
                for h in range(4):
                    q = t * 4 + h
                    o, i_ = st8[:, q, :], ob[t][1][:, h * P:(h + 1) * P]
                    k = Q.emit("dve", lambda e, o=o, i_=i_: e.bn_stats(o, i_), [kd])
                    o2, i2 = mv8[:, q, :], st8[:, q, :]
                    ks.append(Q.emit("dve", lambda e, o2=o2, i2=i2: e.bn_aggr(o2, i2), [k]))
            k = rsqrt_small(rs8, mv8[:, :, 1], 1.0, 1e-6, ks)
            yak = []
            for t in range(2):
                lk = []
                for h in range(4):
                    q = t * 4 + h
                    lk.append(ts(rqk[:, t, h * P:(h + 1) * P], ob[t][1][:, h * P:(h + 1) * P], mv8[:, q, 0:1],
                                 rs8[:, q:q + 1], ALU.subtract, ALU.mult, k, tk))
                bank.give(ob[t][0], lk)
                a = tt(rqk[:, t, :], rqk[:, t, :], rg[:, t, :], ALU.mult, lk, rgk)
                yak += transpose_to(yT[0], lambda c, t=t: rqk[:, t, c * P:(c + 1) * P], 4, t, a)
            barrier()
            arena.pos = work
            misc = arena.get(2, 452)
            fqT = arena.get(4, T)
            fkT = arena.get(4, T)
            fv = arena.get(2, 512)
            lf = arena.get(2, 4)
            fbb = arena.get(4)
            bufs = att_bufs()
            fmr = Rot([arena.get(384) for _ in range(2)])
            kfb = pdma(fbb, bcast(d["fox_fb"][l:l + 1, :]))
            fk_ = []
            FS = float(128 ** -0.5)
            r, w, tok = slab("w_in2", woff + P * 3 * 4096, 8, 512)

            def ev(fp, ps, k):
                a = act(fqT[:, 2 * fp:2 * fp + 2, :], ps, ACT.Copy, k, scale=FS)
                fk_.append(a)
                return a
            gemm_f(XT, w, tok, 4, ev)
            ring.give(r, pe_done())
            r, w, tok = slab("w_in2", woff + P * 4 * 4096, 8, 512)

            def ev(fp, ps, k):
                a = copy_any(fkT[:, 2 * fp:2 * fp + 2, :], ps, k)
                fk_.append(a)
                return a
            gemm_f(XT, w, tok, 4, ev)
            ring.give(r, pe_done())
            r, w, tok = slab("w_in2", woff + P * 5 * 4096, 8, 512)
            fvk, mk_ = [], []

            def ev(t, ps, k):
                a = copy_any(fv[:, t, :], ps, k)
                fvk.append(a)
                return a
            gemm_t(XT, w, tok, 512, ev)
            ring.give(r, pe_done())
            r, w, tok = slab("w_in2", woff + P * 6 * 4096, 8, 452)

            def ev(t, ps, k):
                a = copy_any(misc[:, t, :], ps, k)
                mk_.append(a)
                return a
            gemm_t(XT, w, tok, 452, ev)
            ring.give(r, pe_done())
            lt_ = small[:, 140:148].rearrange("p (t h) -> p t h", t=2)
            k = tt(lf, misc[:, :, 0:4], fbb.unsqueeze(1).to_broadcast([P, 2, 4]), ALU.add, mk_, kfb)
            k = ts(lt_, lf, -1.0, None, ALU.mult, None, k)
            k = tt(lt_, lt_, lf, ALU.min, k)
            k = act(lt_, lt_, ACT.Exp, k)
            k = act(lt_, lt_, ACT.Ln, k, bias=1.0)
            lfk = stt(lf, lf, 0.0, lt_, ALU.min, ALU.subtract, k)
            CB = [(0, 128), (128, 384)]
            CBL = [(0, 0, 0), (1, 0, 128), (1, 1, 256)]
            ytk = [yak, [], []]

            def causal_pv(br, v, vtok):
                def make(h):
                    def pv(pt, k):
                        b, ps, fr = bank.take()
                        hs = slice(h * P, h * P + P)
                        mm(ps[:, 0:T], v[:, 0, hs], pt[:, 0:T], True, False, fr, k, vtok)
                        mm(ps[:, P:T], v[:, 1, hs], pt[:, T + P:2 * T], False, True)
                        kd = pe_done()
                        a = copy_any(yT[br][:, h, :], ps[:, 0:T], kd)
                        ytk[br].append(a)
                        bank.give(b, a)
                        return kd
                    return pv
                return make

            mkpv = causal_pv(1, fv, fvk)

            def heads(h):
                i, F, ff = fmr.take()
                a = [ts(F[:, 0:P], C["gt"], lf[:, 0, h:h + 1], None, ALU.mult, None, ff, lfk),
                     ts(F[:, P:T], C["ones"], lf[:, 1, h:h + 1], None, ALU.mult, None),
                     ts(F[:, T:384], C["gt"], lf[:, 1, h:h + 1], None, ALU.mult, None)]

                def m(ps, fr):
                    mm(ps[:, 0:P], fqT[:, h, 0:P], fkT[:, h, 0:P], True, False, fr, fk_)
                    mm(ps[:, 0:P], LE, F[:, 0:P], False, True, a)
                    mm(ps[:, P:384], fqT[:, h, P:T], fkT[:, h, :], True, False)
                    mm(ps[:, P:T], C["ones"], F[:, 0:P], False, False)
                    mm(ps[:, P:384], LE, F[:, P:384], False, True)
                    fmr.give(i, pe_done())
                return dict(mm=m, pv=mkpv(h), width=384, scale=1.0, cols=CB, blocks=CBL, bias=C["cm"], btok=ctoks)
            attention(4, heads, *bufs)
            barrier()
            arena.pos = work + 904
            qnT = arena.get(4, T)
            knT = arena.get(4, T)
            vM = arena.get(2, 512)
            qpT = arena.get(2, T)
            kpT = arena.get(1, T)
            arena_keep = arena.pos
            lat = arena.get(2, 384)
            latT = arena.get(3, T)
            gq = arena.get(384)
            qpt = arena.get(2, T)
            kpt = arena.get(2, P)
            tmp = arena.get(512)
            kg1 = pdma(gq[:, 0:256], bcast(d["mla_q_g"][l:l + 1, :]))
            kg2 = pdma(gq[:, 256:384], bcast(d["mla_kv_g"][l:l + 1, :]))
            rs_q, rs_k = small[:, 160:162], small[:, 162:164]
            kq = rms(lambda t: misc[:, t, 4:260], 256, rs_q, [], [])
            kkv = rms(lambda t: misc[:, t, 260:388], 128, rs_k, [], [])
            lk = []
            for t in range(2):
                lk.append([stt(lat[:, t, 0:256], misc[:, t, 4:260], rs_q[:, t:t + 1], gq[:, 0:256], ALU.mult,
                               ALU.mult, kq, kg1),
                           stt(lat[:, t, 256:384], misc[:, t, 260:388], rs_k[:, t:t + 1], gq[:, 256:384], ALU.mult,
                               ALU.mult, kkv, kg2)])
            ltk = []
            kpk = [None, None]
            ro[0] = []
            for t in range(2):
                ltk += transpose_to(latT, lambda c, t=t: lat[:, t, c * P:(c + 1) * P], 3, t, lk[t])
                kv = kpt[:, t, :].rearrange("p (c x) -> p c x", c=2)
                reads, ks = rope(misc[:, t, 388:452].unsqueeze(1), 1, ctab[:, t * 64:t * 64 + 64],
                                 stab[:, t * 64:t * 64 + 64], [kv[:, 0:1, :], kv[:, 1:2, :]], tmp, ro[0])
                ro[0] = ks
                kpk[t] = ks
            r, w, tok = slab("wq_up", l * P * 1536, 2, 768)
            MS = float(192 ** -0.5)
            for h in range(0, 4, 2):
                b, ps, fr = bank.take()
                for j in range(2):
                    for c in range(2):
                        mm(ps[:, j * T:(j + 1) * T], w[:, c, (h + j) * 192:(h + j) * 192 + P], latT[:, c, :],
                           c == 0, c == 1, fr, tok, ltk)
                a = act(qnT[:, h:h + 2, :], ps.rearrange("p (a b) -> p a b", a=2), ACT.Copy, pe_done(), scale=MS)
                bank.give(b, a)
                fk_.append(a)
            wv = w.rearrange("p c (h x) -> p c h x", h=4)
            qpk = [None, None]
            for t in range(2):
                b, ps, fr = bank.take()
                for c in range(2):
                    mm(ps[:, 0:T].rearrange("p (h x) -> p h x", h=4), latT[:, c, t * P:(t + 1) * P],
                       wv[:, c, :, 128:192], c == 0, c == 1, fr, tok, ltk)
                reads, ks = rope(ps[:, 0:T].rearrange("p (h x) -> p h x", h=4), 4, ctab[:, t * 64:t * 64 + 64],
                                 stab[:, t * 64:t * 64 + 64],
                                 [qpt[:, t, :].rearrange("p (h x) -> p h x", h=4)], tmp, ro[0], pe_done())
                ks = [ts(qpt[:, t, :], qpt[:, t, :], MS, None, ALU.mult, None, ks)]
                ro[0] = ks
                qpk[t] = ks
                bank.give(b, reads)
            ring.give(r, pe_done())
            r, w, tok = slab("wkv_up", l * P * 1024, 1, 1024)
            for h in range(0, 4, 2):
                b, ps, fr = bank.take()
                for j in range(2):
                    mm(ps[:, j * T:(j + 1) * T], w[:, 0, (h + j) * 256:(h + j) * 256 + P], latT[:, 2, :],
                       True, True, fr, tok, ltk)
                a = copy_any(knT[:, h:h + 2, :], ps.rearrange("p (a b) -> p a b", a=2), pe_done())
                bank.give(b, a)
                fk_.append(a)
            wv = w.rearrange("p c (h x) -> p c h x", h=4)
            vmk = []
            for t in range(2):
                b, ps, fr = bank.take()
                mm(ps.rearrange("p (h x) -> p h x", h=4), latT[:, 2, t * P:(t + 1) * P], wv[:, 0, :, 128:256],
                   True, True, fr, tok, ltk)
                a = copy_any(vM[:, t, :], ps, pe_done())
                bank.give(b, a)
                vmk.append(a)
            ring.give(r, pe_done())
            for t in range(2):
                fk_ += transpose_to(qpT, lambda c, t=t: qpt[:, t, c * P:(c + 1) * P], 2, t, qpk[t])
                fk_ += transpose_to(kpT, lambda c, t=t: kpt[:, t, :], 1, t, kpk[t])
            mkpv = causal_pv(2, vM, vmk)
            barrier()
            arena.pos = arena_keep
            bufs = att_bufs()

            def heads(h):
                p0 = 64 * (h % 2)
                qp, kp_ = qpT[p0:p0 + 64, h // 2, :], kpT[p0:p0 + 64, 0, :]

                def m(ps, fr):
                    mm(ps[:, 0:P], qnT[:, h, 0:P], knT[:, h, 0:P], True, False, fr)
                    mm(ps[:, 0:P], qp[:, 0:P], kp_[:, 0:P], False, True)
                    mm(ps[:, P:384], qnT[:, h, P:T], knT[:, h, :], True, False)
                    mm(ps[:, P:384], qp[:, P:T], kp_, False, True)
                return dict(mm=m, pv=mkpv(h), width=384, scale=1.0, cols=CB, blocks=CBL, bias=C["cm"], btok=ctoks)
            attention(4, heads, *bufs)
            barrier()
            arena.pos = work
            flush()
            g2 = stt(MOD[:, 4, :], MOD[:, 4, :], 1.0, GB[:, 1, :], ALU.add, ALU.mult, list(modk.values()), gk)
            mg = arena.get(8, T)
            tb = Rot([arena.get(2, T) for _ in range(2)])
            mgk = {}
            for br in range(3):
                r, w, tok = slab("branch_w", (l * 3 + br) * P * SLAB, 4, 1024)

                def ev(fp, ps, k, br=br):
                    f0 = 2 * fp
                    m_ = mg[:, f0:f0 + 2, :]
                    g_ = gT[:, br * 8 + f0:br * 8 + f0 + 2, :]
                    gk_ = [gtk[br * 8 + f0], gtk[br * 8 + f0 + 1]]
                    if br == 0:
                        mgk[f0] = tt(m_, ps, g_, ALU.mult, k, gk_)
                        return mgk[f0]
                    i, t_, tf = tb.take()
                    a = tt(t_, ps, g_, ALU.mult, k, gk_, tf)
                    mgk[f0] = tt(m_, m_, t_, ALU.add, a, mgk[f0])
                    tb.give(i, mgk[f0])
                    return a
                gemm_f(yT[br], w, tok, 8, ev, 4, ytk[br])
                ring.give(r, pe_done())
            ot = Rot([arena.get(512) for _ in range(2)])
            rk = []
            extra = [arena.ap[:, xbase + j * SLAB:xbase + (j + 1) * SLAB] for j in range(2)]
            assert xbase + 2 * SLAB <= work
            for x_ in extra:
                ring.bufs.append(x_)
                ring.free.append(all_done())
                ring.held.append(False)

            def gated_res(gi):
                def ev(t, n, ps, k):
                    i, o, of = ot.take()
                    a = tt(o, ps, MOD[:, gi, n * 512:(n + 1) * 512], ALU.mult, k, of)
                    x = X[:, t, n * 512:(n + 1) * 512]
                    a2 = tt(x, x, o, ALU.add, a)
                    ot.give(i, a2)
                    rk.append(a2)
                    return a
                return ev
            residual_gemm("out_w", (2, 8, 512), mg, list(mgk.values()), gated_res(2), l * 2 * P * SLAB)

            barrier()
            arena.pos = xbase + 2 * SLAB
            H2 = MOD[:, 0:2, :]
            hv = H2.rearrange("p t (q c) -> p t q c", c=8)
            htok = norm_mod(3, 4, rk, H2)
            hk_ = list(hh_done)
            moe_start = barrier()
            hn_done = moe_start
            av = MOD[:, 3:5, :]
            arena.pos = xbase + 2 * SLAB
            code = arena.get(2, 32)
            msk = arena.get(2, 32)
            wc = arena.get(2, 32)
            rb_ = arena.get(36)
            lg = arena.get(2, 36)
            pr_ = arena.get(2, 8)
            m1 = arena.get(2, 8)
            m2 = arena.get(2, 8)
            tm = arena.get(2, 32)
            sel = arena.get(2, 8)
            gm = arena.get(2, 4)
            s4 = arena.get(2, 16)
            krb = pdma(rb_, bcast(d["router_b"][l:l + 1, :]))
            r, w, tok = slab("router_w", l * P * 288, 8, 36)
            lk = []

            def ev(t, ps, k):
                a = tt(lg[:, t, :], ps, rb_, ALU.add, k, krb)
                lk.append(a)
                return a
            gemm_t(XT, w, tok, 36, ev, 8, htok)
            ring.give(r, pe_done())

            def bc2(x, n):
                return x.to_broadcast([P, 2, n])

            def first_max(x, n, mask, mx, w_):
                k = red(mx, x, ALU.max, w_)
                k = tt(mask, x, bc2(mx, n), ALU.is_equal, k)
                k = tt(mask, mask, C["desc"][:, 0:n].unsqueeze(1).to_broadcast([P, 2, n]), ALU.mult, k)
                k = red(s4[:, :, 15:16], mask, ALU.max, k)
                return tt(mask, mask, bc2(s4[:, :, 15:16], n), ALU.is_equal, k)

            def softmax(o, x, n, mx, w_):
                k = tt(o, x, bc2(mx, n), ALU.subtract, w_)
                k = act(o, o, ACT.Exp, k)
                k = red(s4[:, :, 14:15], o, ALU.add, k)
                k = recip(s4[:, :, 13:14], s4[:, :, 14:15], k)
                return tt(o, o, bc2(s4[:, :, 13:14], n), ALU.mult, k)

            k = red(s4[:, :, 0:1], lg[:, :, 0:4], ALU.max, lk)
            k = softmax(gm, lg[:, :, 0:4], 4, s4[:, :, 0:1], k)
            k = first_max(gm, 4, tm[:, :, 0:4], s4[:, :, 1:2], k)
            k = cp(gm, tm[:, :, 0:4], k)
            tv = tm.rearrange("p t (g e) -> p t g e", g=4)
            for t in range(2):
                k = tt(tv[:, t, :, :], lg[:, t, 4:36].rearrange("p (g e) -> p g e", g=4),
                       gm[:, t, :].unsqueeze(2).to_broadcast([P, 4, 8]), ALU.mult, k)
            k = tt(sel, tm[:, :, 0:8], tm[:, :, 8:16], ALU.add, k)
            k = tt(sel, sel, tm[:, :, 16:24], ALU.add, k)
            k = tt(sel, sel, tm[:, :, 24:32], ALU.add, k)
            k = red(s4[:, :, 2:3], sel, ALU.max, k)
            k = softmax(pr_, sel, 8, s4[:, :, 2:3], k)
            k = first_max(pr_, 8, m1, s4[:, :, 3:4], k)
            k = stt(sel, m1, -4.0, pr_, ALU.mult, ALU.add, k)
            k = first_max(sel, 8, m2, s4[:, :, 4:5], k)
            k = tt(s4[:, :, 5:6], s4[:, :, 3:4], s4[:, :, 4:5], ALU.add, k)
            k = recip(s4[:, :, 6:7], s4[:, :, 5:6], k)
            kk2 = tt(sel, m1, m2, ALU.add, k)
            for t in range(2):
                mk = tt(msk[:, t, :].rearrange("p (g e) -> p g e", g=4), gm[:, t, :].unsqueeze(2).to_broadcast([P, 4, 8]),
                        sel[:, t, :].unsqueeze(1).to_broadcast([P, 4, 8]), ALU.mult, kk2)
            k = tt(m1, m1, bc2(s4[:, :, 3:4], 8), ALU.mult, k)
            k = tt(m2, m2, bc2(s4[:, :, 4:5], 8), ALU.mult, k)
            k = tt(m1, m1, m2, ALU.add, k)
            k = tt(m1, m1, bc2(s4[:, :, 6:7], 8), ALU.mult, k)
            k = tt(m1, m1, bc2(s4[:, :, 1:2], 8), ALU.mult, k)
            for t in range(2):
                k = tt(wc[:, t, :].rearrange("p (g e) -> p g e", g=4), gm[:, t, :].unsqueeze(2).to_broadcast([P, 4, 8]),
                       m1[:, t, :].unsqueeze(1).to_broadcast([P, 4, 8]), ALU.mult, k)
            wk = k
            b, ps, fr = bank.take()
            mm(ps[:, 0:32], C["lt"], msk[:, 0, :], True, True, fr, mk)
            mm(ps[:, 32:64], C["ones"], msk[:, 0, :], True, False)
            mm(ps[:, 32:64], C["lt"], msk[:, 1, :], False, True)
            mm(ps[:, 64:96], C["ones"], msk[:, 0, :], True, False)
            mm(ps[:, 64:96], C["ones"], msk[:, 1, :], False, True)
            kd = pe_done()
            k = stt(code, ps[:, 0:64].rearrange("p (t e) -> p t e", t=2), 1.0, msk, ALU.add, ALU.mult, kd)
            ck_ = ts(code, code, -1.0, None, ALU.add, None, k)
            kf = red(small[:, 170:171], ps[:, 64:96], ALU.max, kd)
            bank.give(b, kf, k)
            flag_k = ts(flag[:, l:l + 1], small[:, 170:171], float(CAP), None, ALU.is_gt, None, kf)

            pselr = Rot([arena.get(2, P) for _ in range(2)])
            pwr = Rot([arena.get(2, P) for _ in range(1)])
            pwtr = Rot([arena.get(T) for _ in range(2)])
            xgr = Rot([arena.get(8, P) for _ in range(2)])
            sr_ = Rot([arena.get(512) for _ in range(2)])
            hr_ = Rot([arena.get(512) for _ in range(2)])
            htr = Rot([arena.get(4, P) for _ in range(2)])
            yr = Rot([arena.get(D) for _ in range(2)])
            G_, W_, Y_ = {}, {}, {}
            avk = {}

            def gather(i):
                q, pl, pf = pselr.take()
                k = tt(pl.rearrange("p t (e s) -> p t e s", e=2),
                       C["iota"].unsqueeze(1).unsqueeze(1).to_broadcast([P, 2, 2, CAP]),
                       code[:, :, 2 * i:2 * i + 2].unsqueeze(3).to_broadcast([P, 2, 2, CAP]), ALU.is_equal, ck_, pf)
                v, pw, wf = pwr.take()
                kw = tt(pw.rearrange("p t (e s) -> p t e s", e=2), pl.rearrange("p t (e s) -> p t e s", e=2),
                        wc[:, :, 2 * i:2 * i + 2].unsqueeze(3).to_broadcast([P, 2, 2, CAP]), ALU.mult, k, wk, wf)
                m, xg, xf = xgr.take()
                ks = []
                for c0 in (0, 4):
                    b, ps, fr = bank.take()
                    for c in range(c0, c0 + 4):
                        for t in range(2):
                            mm(ps[:, (c - c0) * P:(c - c0 + 1) * P], hv[:, t, :, c], pl[:, t, :], t == 0, t == 1,
                               fr, k, hk_)
                    a = cp(xg[:, c0:c0 + 4, :], ps.rearrange("p (a b) -> p a b", a=4), pe_done(), xf, e="act")
                    bank.give(b, a)
                    ks.append(a)
                pselr.give(q, pe_done(), kw)
                b, ps, fr = bank.take()
                for t in range(2):
                    tr(ps[:, t * P:(t + 1) * P], pw[:, t, :], fr, kw)
                kd = pe_done()
                pwr.give(v, kd)
                u, pt, pf2 = pwtr.take()
                a = cp(pt, ps[:, 0:T], kd, pf2)
                bank.give(b, a)
                G_[i] = (m, xg, ks)
                W_[i] = (u, pt, a)

            def inner(i):
                m, xg, ks = G_.pop(i)
                e0 = l * NE + 2 * i
                L1 = [slab("exp_w1", (e0 + j) * P * SLAB, 8, 512) for j in range(2)]
                L3 = [slab("exp_w3", (e0 + j) * P * SLAB, 8, 512) for j in range(2)]
                outs = []
                for L in (L1, L3):
                    b, ps, fr = bank.take()
                    for c in range(8):
                        for j in range(2):
                            mm(ps[64 * j:64 * j + 64, :], xg[:, c, 64 * j:64 * j + 64], L[j][1][:, c, :], c == 0,
                               c == 7, fr, ks, L[0][2], L[1][2] if j else None)
                    kd = pe_done()
                    ring.give(L[0][0], kd)
                    ring.give(L[1][0], kd)
                    outs.append((b, ps, kd))
                xgr.give(m, kd)
                (ba, pa, ka), (bb, pb, kb) = outs
                q, s_, sf = sr_.take()
                a = act(s_, pa, ACT.Silu, ka, sf)
                bank.give(ba, a)
                v, h_, hf = hr_.take()
                a2 = tt(h_, s_, pb, ALU.mult, a, kb, hf)
                bank.give(bb, a2)
                sr_.give(q, a2)
                return v, h_, a2

            def turn_h(H_):
                v, h_, hk2 = H_
                b, ps, fr = bank.take()
                for f in range(4):
                    tr(ps[:, f * P:(f + 1) * P], h_[:, f:512:4], fr, hk2)
                kd = pe_done()
                hr_.give(v, kd)
                q, ht, hf = htr.take()
                a = cp(ht, ps.rearrange("p (a b) -> p a b", a=4), kd, hf)
                bank.give(b, a)
                return q, ht, a

            def outer(i, HT_):
                q, ht, hk2 = HT_
                e0 = l * NE + 2 * i
                L2 = [slab("exp_w2", (e0 + j) * P * SLAB, 4, 1024) for j in range(2)]
                bs = [bank.take() for _ in range(2)]
                for f in range(4):
                    for j in range(2):
                        for n in range(2):
                            mm(bs[n][1][64 * j:64 * j + 64, :], ht[:, f, 64 * j:64 * j + 64],
                               L2[j][1][:, f, n * 512:(n + 1) * 512], f == 0, f == 3, bs[n][2], hk2, L2[0][2],
                               L2[1][2] if j else None)
                kd = pe_done()
                ring.give(L2[0][0], kd)
                ring.give(L2[1][0], kd)
                htr.give(q, kd)
                v, y, yf = yr.take()
                ks = []
                for n in range(2):
                    a = cp(y[:, n * 512:(n + 1) * 512], bs[n][1], kd, yf, e="act")
                    bank.give(bs[n][0], a)
                    ks.append(a)
                Y_[i] = (v, y, ks)

            def combine(i):
                v, y, ks = Y_.pop(i)
                u, pt, kp_ = W_.pop(i)
                for t in range(2):
                    for n in range(2):
                        b, ps, fr = bank.take()
                        mm(ps, pt[:, t * P:(t + 1) * P], y[:, n * 512:(n + 1) * 512], True, True, fr, ks, kp_)
                        o = av[:, t, n * 512:(n + 1) * 512]
                        if i == 0:
                            a = cp(o, ps, pe_done(), hn_done)
                        else:
                            a = tt(o, o, ps, ALU.add, pe_done(), avk[t, n])
                        avk[t, n] = a
                        bank.give(b, a)
                yr.give(v, pe_done())
                pwtr.give(u, pe_done())

            gather(0)
            for i in range(NE // 2):
                H_ = inner(i)
                if i >= 1:
                    combine(i - 1)
                if i + 1 < NE // 2:
                    gather(i + 1)
                HT_ = turn_h(H_)
                outer(i, HT_)
            combine(NE // 2 - 1)
            del ring.bufs[NRING:], ring.free[NRING:], ring.held[NRING:]
            barrier()
            moe_end = all_done()
            flag_wait[0] = flag_k
            general_experts(l, av, wc, arena_hid=(sr_.bufs, xgr.bufs), main=moe_end, extra=extra)
            avk = {0: moe_end}
            rk = []
            for t in range(2):
                a = tt(av[:, t, :], av[:, t, :], MOD[:, 5, :], ALU.mult)
                rk.append(tt(X[:, t, :], X[:, t, :], av[:, t, :], ALU.add, a))

        barrier()
        kf = pdma(GB[:, 0, :], bcast(d["final_g"][0:1, :]), all_done())
        rs = small[:, 60:62]
        k = rms(lambda t: X[:, t, :], D, rs, rk, rk)
        fk = []
        for t in range(2):
            fk.append(stt(X[:, t, :], X[:, t, :], rs[:, t:t + 1], GB[:, 0, :], ALU.mult, ALU.mult, k, kf))

        last = flat(fk)
        block = ctx.enter_context(nc.Block())

        def run(queue, eng, name):
            for n, rec in enumerate(queue):
                if rec[0] == "wait":
                    eng.wait_ge(rec[1], rec[2])
                elif rec[0] == "branch":
                    reg = eng.alloc_register(f"{name}_flag{n}")
                    eng.reg_load(reg, rec[1])
                    with eng.If_ne(reg, 0):
                        run(rec[2], eng, name)
                else:
                    ins = rec[1](eng)
                    if rec[2] is not None:
                        ins.then_inc(rec[2], rec[3])

        @block.sync
        def _(eng):
            run(Q.q["sp"], eng, "sp")
            for x in last:
                eng.wait_ge(x[1], x[2])
            eng.dma_start(out.rearrange("(t p) f -> p t f", p=P), X).then_inc(osem, 16)
            eng.wait_ge(osem, 16)

        @block.gpsimd
        def _(eng):
            run(Q.q["pool"], eng, "pool")

        @block.scalar
        def _(eng):
            run(Q.q["act"], eng, "act")

        @block.vector
        def _(eng):
            run(Q.q["dve"], eng, "dve")

        @block.tensor
        def _(eng):
            run(Q.q["pe"], eng, "pe")


def constants():
    i = np.arange(P)[:, None]
    j = np.arange(P)[None, :]
    f = np.float32
    one = np.ones((P, P), f)
    c = {}
    c["ident"] = np.eye(P, dtype=f)
    c["ones"] = None
    c["half"] = None
    c["gt"] = (i > j).astype(f)
    c["lt"] = (i < j).astype(f)
    c["leo"] = np.concatenate([(i <= j).astype(f), one], 1)
    c["oge"] = np.concatenate([one, (i >= j).astype(f)], 1)
    k = np.arange(T)[None, :]
    c["maska"] = np.concatenate([np.where(np.abs(i + t * P - k) <= 128, 0.0, NEG) for t in range(2)], 1).astype(f)
    tri = np.where(j <= i, 0.0, NEG)
    c["cm"] = np.concatenate([tri, np.zeros((P, P)), tri], 1).astype(f)
    inv = 10000.0 ** (-np.arange(32, dtype=np.float64) / 32)
    c["inv"] = np.broadcast_to(inv.astype(f)[None], (P, 32)).copy()
    ang = (np.arange(T, dtype=f)[:, None] * inv.astype(f)[None, :]).astype(f).astype(np.float64)
    co, si = np.cos(ang), np.sin(ang)
    ct = np.concatenate([co, co], 1).reshape(2, P, 64).transpose(1, 0, 2).reshape(P, 128)
    st = np.concatenate([-si, si], 1).reshape(2, P, 64).transpose(1, 0, 2).reshape(P, 128)
    c["ropec"], c["ropes"] = ct.astype(f), st.astype(f)
    dm = []
    for h in range(4):
        lg = np.log1p(-np.exp2(-5.0 - h))
        q = np.arange(T)[None, :]
        m0 = np.where(q >= i, np.exp(lg * np.maximum(q - i, 0)), 0.0)
        q1 = np.arange(P)[None, :]
        m1 = np.where(q1 >= i, np.exp(lg * np.maximum(q1 - i, 0)), 0.0)
        dm.append(np.concatenate([m0, m1], 1) * 0.125)
    c["dmask"] = np.concatenate(dm, 1).astype(f)
    c["iota"] = np.broadcast_to(np.arange(CAP, dtype=f)[None], (P, CAP)).copy()
    c["e12"] = np.zeros((P, 24), f)
    c["e12"][:, 11] = 1.0
    c["desc"] = np.broadcast_to((8 - np.arange(8)).astype(f)[None], (P, 8)).copy()
    return c


CONST_WIDTH = {"ident": 128, "ones": 128, "half": 8, "gt": 128, "lt": 128, "leo": 256, "oge": 256, "maska": 512,
               "cm": 384, "inv": 32, "ropec": 128, "ropes": 128, "dmask": 1536, "desc": 8, "e12": 24, "iota": CAP, "rope2c": 128,
               "rope2s": 128}


def pc(w, cuts):
    k, n = w.shape
    v = w.reshape(P, k // P, n)
    out, a = [], 0
    for m in cuts:
        out.append(v[:, :, a:a + m].reshape(-1))
        a += m
    assert a == n
    return np.concatenate(out)


def cpw(w, cuts):
    k, n = w.shape
    return pc(np.ascontiguousarray(w.reshape(k // P, P, n).transpose(1, 0, 2)).reshape(k, n), cuts)


def cpk(w, kc):
    k, n = w.shape
    return np.ascontiguousarray(w.reshape(k // (kc * P), kc, P, n).transpose(0, 2, 1, 3)).reshape(-1)


def kernel(**inputs):
    import numpy as _np
    import concourse.bacc as _bacc
    from concourse import mybir as _mybir
    from concourse.bass_utils import run_bass_kernel_spmd as _run

    g = {k: _np.asarray(v) for k, v in inputs.items()}
    a = {}
    a["x"] = g["x"].reshape(T, D)
    a["attn_w_in"] = pc(g["attn_w_in"][0], [512, 256, 512, 512, 512])
    a["attn_sink"] = g["attn_sink"]
    q = _np.arange(T)
    r_, c_ = q // 64, q % 64
    cs = _np.clip(c_ - 8, 0, 48)
    ok = (c_[None, :] >= cs[:, None]) & (c_[None, :] < cs[:, None] + 16)
    dr = r_[None, :] - r_[:, None] + 7
    dc = _np.clip(c_[None, :] - c_[:, None] + 15, 0, 30)
    idx = _np.where(ok, dr * 31 + dc, 15 * 31)
    rp = _np.concatenate([g["attn_rpb"][0].reshape(8, 465), _np.full((8, 1), NEG, _np.float32)], 1)
    bias = rp[:, idx.reshape(-1)].reshape(8, 2, P, T)
    a["attn_bias"] = _np.ascontiguousarray(bias.transpose(2, 0, 1, 3)).reshape(-1)
    a["attn_w_out"] = cpk(g["attn_w_out"][0], 4)
    a["ssm_w_in"] = pc(g["ssm_w_in"][0][:, 0:6144], [512] * 12)
    a["ssm_w_dt"] = pc(g["ssm_w_in"][0][:, 6144:], [64])
    cw = g["ssm_conv_w"][0].reshape(5, 32, P).transpose(2, 1, 0)
    cb = g["ssm_conv_b"][0].reshape(32, P).T[:, :, None]
    a["ssm_conv"] = _np.concatenate([cw, cb], 2).reshape(P, 192)
    dsk = _np.repeat(g["ssm_D"][0], 64).reshape(16, P).T
    a["ssm_dn"] = _np.concatenate([dsk, g["ssm_norm_w"][0].reshape(16, P).T], 1)
    a["ssm_dt_bias"] = g["ssm_dt_bias"]
    a["ssm_A_log"] = g["ssm_A_log"].reshape(1, 64)
    a["ssm_w_out"] = cpk(g["ssm_w_out"][0], 4)
    a["mlp_w1"] = _np.concatenate([pc(g["mlp_w1"][l], [512] * 8) for l in range(2)])
    a["mlp_w2"] = _np.concatenate([cpk(g["mlp_w2"][l], 4) for l in range(2)])
    for n in ("ln1_g", "ln1_b", "ln2_g", "ln2_b"):
        a[n] = g[n]
    a["c"] = g["c_2"].reshape(-1)
    a["positions"] = g["positions_2"].reshape(2, P).T
    a["ada_w"] = _np.concatenate([pc(g["ada_w_2"][l], [512] * 12) for l in range(2)])
    a["ada_b"] = g["ada_b_2"].reshape(24, 512)
    a["norm1_g"], a["norm2_g"], a["final_g"] = g["norm1_g_2"], g["norm2_g_2"], g["final_g_2"].reshape(1, D)
    a["w_in2"] = _np.concatenate([pc(g["w_in_2"][l], [512] * 6 + [452]) for l in range(2)])
    a["fox_fb"] = g["fox_fb_2"]
    a["mla_q_g"], a["mla_kv_g"] = g["mla_q_norm_g_2"], g["mla_kv_norm_g_2"]
    a["wq_up"] = _np.concatenate([cpw(g["mla_wq_up_2"][l], [768]) for l in range(2)])
    a["wkv_up"] = _np.concatenate([cpw(g["mla_wkv_up_2"][l], [1024]) for l in range(2)])
    a["gate_w"] = _np.concatenate([pc(g["gate_w_2"][l], [512] * 6) for l in range(2)])
    a["gate_b"] = _np.concatenate([g["gate_b_2"][l].reshape(24, P).T for l in range(2)])
    a["branch_w"] = _np.concatenate([cpk(g["branch_w_2"][l, b], 4) for l in range(2) for b in range(3)])
    a["out_w"] = _np.concatenate([cpw(g["out_w_2"][l], [512, 512]) for l in range(2)])
    a["router_w"] = _np.concatenate(
        [pc(_np.concatenate([g["router_grp_w_2"][l], g["router_exp_w_2"][l]], 1), [36]) for l in range(2)])
    a["router_b"] = _np.concatenate([g["router_grp_b_2"], g["router_exp_b_2"]], 1)
    a["exp_w1"] = g["exp_w1_2"].reshape(-1)
    a["exp_w3"] = g["exp_w3_2"].reshape(-1)
    a["exp_w2"] = g["exp_w2_2"].reshape(-1)
    for n, v in constants().items():
        if v is not None:
            a["const_" + n] = v

    nc = _bacc.Bacc("TRN2", target_bir_lowering=False, num_devices=1)
    arrays, args = {}, {}
    for name, v in a.items():
        v = _np.ascontiguousarray(v)
        arrays[f"in_{name}"] = v
        args[name] = nc.dram_tensor(f"in_{name}", v.shape, _mybir.dt.from_np(v.dtype), kind="ExternalInput").ap()
    out = nc.dram_tensor("out_0", (T, D), _mybir.dt.float32, kind="ExternalOutput").ap()
    build(nc, args, out, CONST_WIDTH)
    r = _run(nc, [arrays], core_ids=[0])
    return r.results[0]["out_0"].reshape(1, T, D)
```

```python
from contextlib import ExitStack

import numpy as np
import concourse.bass as bass
from concourse import mybir

F32 = mybir.dt.float32
I32 = mybir.dt.int32
ALU = mybir.AluOpType
ACT = mybir.ActivationFunctionType
AX = mybir.AxisListType.X

P = 128
T = 256
D = 1024
NEG = -1e30
NRING = 4
SLAB = 4096
NE = 32
CAP = 64
ALPHA = float(4 ** 0.25)


class Queues:

    def __init__(self, nc, ctx, suffix=""):
        self.q = {"pe": [], "act": [], "dve": [], "pool": [], "sp": []}
        self.sem = {e: ctx.enter_context(nc.semaphore("s_" + e + suffix)) for e in ("pe", "act", "dve", "pool")}
        self.cnt = {e: 0 for e in self.sem}
        self.seen = {}

    def emit(self, e, fn, waits, inc=True):
        for w in flat(waits):
            key = (e, w[0])
            if self.seen.get(key, 0) < w[2]:
                self.seen[key] = w[2]
                self.q[e].append(("wait", w[1], w[2]))
        rec = ["op", fn, None, 0]
        self.q[e].append(rec)
        if inc:
            return self.done(e)
        return None

    def done(self, e):
        rec = self.q[e][-1]
        assert rec[0] == "op"
        if rec[2] is None:
            self.cnt[e] += 1
            rec[2], rec[3] = self.sem[e], 1
        return (e, self.sem[e], self.cnt[e])

    def all_done(self):
        out = []
        for e in ("pe", "act", "dve", "pool"):
            for rec in reversed(self.q[e]):
                if rec[0] == "op":
                    if rec[2] is None:
                        self.cnt[e] += 1
                        rec[2], rec[3] = self.sem[e], 1
                    break
            if self.cnt[e]:
                out.append((e, self.sem[e], self.cnt[e]))
        return out


def flat(ws):
    out = []
    for w in ws:
        if w is None:
            continue
        if isinstance(w, tuple) and len(w) == 3 and isinstance(w[0], (str, int)):
            out.append(w)
        else:
            out.extend(flat(w))
    return out


class Rot:

    def __init__(self, bufs):
        self.bufs, self.free, self.held, self.stamp = [], [], [], []
        self.n = 0
        for b in bufs:
            self.add(b)

    def add(self, buf, *toks):
        self.bufs.append(buf)
        self.free.append(flat(toks))
        self.held.append(False)
        self.n += 1
        self.stamp.append(self.n)

    def cut(self, n):
        del self.bufs[n:], self.free[n:], self.held[n:], self.stamp[n:]

    def take(self):
        ready = [i for i in range(len(self.bufs)) if not self.held[i]]
        i = min(ready, key=lambda j: self.stamp[j])
        self.held[i] = True
        return i, self.bufs[i], list(self.free[i])

    def give(self, i, *toks):
        self.free[i] = flat(toks)
        self.held[i] = False
        self.n += 1
        self.stamp[i] = self.n


class Arena:
    def __init__(self, ap, size):
        self.ap, self.size, self.pos, self.base = ap, size, 0, 0

    def get(self, *shape):
        n = 1
        for s in shape:
            n *= s
        a = self.ap[:, self.pos:self.pos + n]
        self.pos += n
        assert self.pos <= self.size, (self.pos, self.size)
        if len(shape) == 2:
            a = a.rearrange("p (a b) -> p a b", a=shape[0])
        if len(shape) == 3:
            a = a.rearrange("p (a b c) -> p a b c", a=shape[0], b=shape[1])
        return a


def build(nc, d, out, consts):
    with ExitStack() as ctx:
        Q = Queues(nc, ctx)

        def sb(name, shape, dt=F32):
            return ctx.enter_context(nc.sbuf_tensor(name, shape, dt))

        psb = [ctx.enter_context(nc.psum_tensor(f"ps{i}", [P, 512], F32)) for i in range(8)]
        bank = Rot([p[:, :] for p in psb])
        ringt = sb("ring", [P, NRING * SLAB])
        ring = Rot([ringt[:, i * SLAB:(i + 1) * SLAB] for i in range(NRING)])
        rsem = [ctx.enter_context(nc.semaphore(f"s_ring{i}")) for i in range(NRING + 2)]
        ruse = [0] * (NRING + 2)
        X = sb("X", [P, 2, D])[:, :, :]
        XT = sb("XT", [P, 8, T])[:, :, :]
        GB = sb("GB", [P, 2, D])[:, :, :]
        small = sb("small", [P, 512])[:, :]
        C = {}
        LATE = ("cm", "dmask", "rope2c", "rope2s")
        for name, arr in consts.items():
            if name in LATE:
                continue
            C[name] = sb("c_" + name, [P, arr])[:, :]
        ASZ = 27180
        arena = Arena(sb("arena", [P, ASZ])[:, :], ASZ)
        posi = sb("posi", [P, 2], I32)[:, :]
        flag = sb("flag", [P, 2], I32)[:, :]
        NPD = 12
        psem = [ctx.enter_context(nc.semaphore(f"s_pd{i}")) for i in range(NPD)]
        puse = [0] * NPD
        pn = [0]
        osem = ctx.enter_context(nc.semaphore("s_out"))

        def mm(o, lhsT, rhs, start, stop, *w):
            Q.emit("pe", lambda e: e.matmul(o, lhsT=lhsT, rhs=rhs, start=start, stop=stop, skip_group_check=True), w, False)

        def tr(o, i, *w):
            n = i.shape[0]
            Q.emit("pe", lambda e: e.transpose(o, i, C["ident"][0:n, 0:n]), w, False)

        def pe_done():
            return Q.done("pe")

        def act(o, i, func, *w, bias=0.0, scale=1.0, acc=None):
            if acc is None:
                return Q.emit("act", lambda e: e.activation(o, i, func, bias=bias, scale=scale), w)
            return Q.emit("act", lambda e: e.activation(o, i, func, bias=bias, scale=scale, accum_out=acc), w)

        def ts(o, i, s1, s2, op0, op1, *w, e="dve"):
            if s2 is None:
                return Q.emit(e, lambda g: g.tensor_scalar(o, i, s1, None, op0), w)
            return Q.emit(e, lambda g: g.tensor_scalar(o, i, s1, s2, op0, op1), w)

        def stt(o, i0, s, i1, op0, op1, *w):
            return Q.emit("dve", lambda g: g.scalar_tensor_tensor(out=o, in0=i0, scalar=s, in1=i1, op0=op0, op1=op1), w)

        def tt(o, a, b, op, *w, e="dve"):
            return Q.emit(e, lambda g: g.tensor_tensor(o, a, b, op), w)

        def cp(o, i, *w, e="dve"):
            if e == "act":
                return Q.emit(e, lambda g: g.copy(o, i), w)
            return Q.emit(e, lambda g: g.tensor_copy(o, i), w)

        def red(o, i, op, *w):
            return Q.emit("dve", lambda g: g.tensor_reduce(o, i, AX, op), w)

        def recip(o, i, *w):
            return Q.emit("dve", lambda g: g.reciprocal(o, i), w)

        def mset(o, v, *w, e="pool"):
            return Q.emit(e, lambda g: g.memset(o, v), w)

        def pdma(o, i, *w):
            k = pn[0] % NPD
            pn[0] += 1
            prev = (f"pd{k}", psem[k], 16 * puse[k])
            puse[k] += 1
            for x in flat([w, prev] if puse[k] > 1 else [w]):
                key = ("pool", x[0])
                if Q.seen.get(key, 0) < x[2]:
                    Q.seen[key] = x[2]
                    Q.q["pool"].append(("wait", x[1], x[2]))
            sem = psem[k]
            Q.q["pool"].append(["dma", lambda e: e.dma_start(o, i).then_inc(sem, 16), None, 0])
            return (f"pd{k}", psem[k], 16 * puse[k])

        def load(src, kc, n):
            i, buf, free = ring.take()
            for x in flat(free):
                key = ("sp", x[0])
                if Q.seen.get(key, 0) < x[2]:
                    Q.seen[key] = x[2]
                    Q.q["sp"].append(("wait", x[1], x[2]))
            ruse[i] += 1
            dst = buf[:, 0:kc * n]
            sem = rsem[i]
            Q.q["sp"].append(["dma", lambda e: e.dma_start(dst, src).then_inc(sem, 16), None, 0])
            view = dst.rearrange("p (c n) -> p c n", c=kc)
            return i, view, ("r%d" % i, rsem[i], 16 * ruse[i])

        def slab(name, off, kc, n):
            src = d[name][off:off + P * kc * n].rearrange("(p f) -> p f", p=P)
            return load(src, kc, n)

        def gemm_t(xt, w, tok, n, evac, kcs=8, *extra, by_t=None):
            for t in range(2):
                xk_ = need(by_t, t)
                b, ps, fr = bank.take()
                for c in range(kcs):
                    mm(ps[:, 0:n], xt[:, c, t * P:(t + 1) * P], w[:, c, 0:n], c == 0, c == kcs - 1, fr, tok, extra,
                       xk_)
                bank.give(b, evac(t, ps[:, 0:n], pe_done()))

        def gemm_f(xt, w, tok, nf, evac, kcs=8, *extra):
            for f in range(0, nf, 2):
                b, ps, fr = bank.take()
                for j in range(2):
                    for c in range(kcs):
                        mm(ps[:, j * T:(j + 1) * T], w[:, c, (f + j) * P:(f + j + 1) * P], xt[:, c, :],
                           c == 0, c == kcs - 1, fr, tok, extra)
                bank.give(b, evac(f // 2, ps[:, :].rearrange("p (a b) -> p a b", a=2), pe_done()))

        def gemm_f2(xt, w, tok, evac, by_t):
            bs = [bank.take() for _ in range(2)]
            for t in range(2):
                xk_ = need(by_t, t)
                for f in range(4):
                    b, ps, fr = bs[f // 2]
                    o = (f % 2) * T + t * P
                    for c in range(8):
                        mm(ps[:, o:o + P], w[:, c, f * P:(f + 1) * P], xt[:, c, t * P:(t + 1) * P],
                           c == 0, c == 7, fr, tok, xk_)
            kd = pe_done()
            for i, (b, ps, fr) in enumerate(bs):
                bank.give(b, evac(i, ps[:, :].rearrange("p (a b) -> p a b", a=2), kd))

        flip = [0]

        def copy_any(o, i, *w):
            flip[0] ^= 1
            return cp(o, i, *w, e="act" if flip[0] else "dve")

        def transpose_to(dst, src_of, n, t, toks, extra=(), e=None):
            last = []
            for c0 in range(0, n, 4):
                m = min(4, n - c0)
                b, ps, fr = bank.take()
                for j in range(m):
                    tr(ps[:, j * P:(j + 1) * P], src_of(c0 + j), fr, toks, extra)
                o, i = dst[:, c0:c0 + m, t * P:(t + 1) * P], ps[:, 0:m * P].rearrange("p (a b) -> p a b", a=m)
                k = cp(o, i, pe_done(), extra, e=e) if e else copy_any(o, i, pe_done(), extra)
                bank.give(b, k)
                last.append(k)
            return last

        def rsqrt_small(o, i, mul, eps, *w):
            k = ts(o, i, mul, eps, ALU.mult, ALU.add, *w)
            n = o.shape[-1]
            return tt(o, o, C["half"][:, 0:n], ALU.pow, k, e="pool")

        def barrier(engines=("pe", "act", "dve", "pool")):
            toks = Q.all_done()
            for e in engines:
                for x in toks:
                    key = (e, x[0])
                    if Q.seen.get(key, 0) < x[2]:
                        Q.seen[key] = x[2]
                        Q.q[e].append(("wait", x[1], x[2]))
            arena.pos = arena.base
            return toks

        WRITERS = ("act", "dve", "pool")
        all_done = Q.all_done

        filler = []
        after = []

        def step(n=1):
            for _ in range(n):
                while after:
                    after.pop(0)()
                if filler:
                    filler.pop(0)()

        def flush():
            while filler or after:
                step()

        def ln_block(t, toks, ptok):
            st = small[:, 0:24].rearrange("p (t a b) -> p t a b", t=2, a=2)
            mv = small[:, 24:28].rearrange("p (t a) -> p t a", t=2)
            rs = small[:, 28:30]
            kk = []
            for h in range(2):
                o, i = st[:, t, h, :], X[:, t, h * 512:(h + 1) * 512]
                kk.append(Q.emit("dve", lambda e, o=o, i=i: e.bn_stats(o, i), [toks]))
            o, i = mv[:, t, :], st[:, t, :, :]
            k = Q.emit("dve", lambda e, o=o, i=i: e.bn_aggr(o, i), kk)
            k = rsqrt_small(rs[:, t:t + 1], mv[:, t, 1:2], 1.0, 1e-5, k)
            a = ts(X[:, t, :], X[:, t, :], mv[:, t, 0:1], rs[:, t:t + 1], ALU.subtract, ALU.mult, k)
            a = tt(X[:, t, :], X[:, t, :], GB[:, 0, :], ALU.mult, a, ptok)
            return tt(X[:, t, :], X[:, t, :], GB[:, 1, :], ALU.add, a)

        def turn_rows(src, toks):
            v = src.rearrange("p t (q c) -> p t q c", c=8)
            turn = [lambda t=t: transpose_to(XT, lambda c: v[:, t, :, c], 8, t, toks[t], e="act") for t in range(2)]
            return [turn[0](), turn[1]]

        def need(by_t, t):
            if by_t is None:
                return None
            if callable(by_t[t]):
                by_t[t] = by_t[t]()
            return by_t[t]

        def layer_norm(rows, ptok):
            ks = []
            for t in range(2):
                ks.append(ln_block(t, rows(t), ptok))
            return turn_rows(X, ks)

        def bcast(src):
            return src.partition_broadcast(P)

        def mlp(l, xtok):
            hT = arena.get(32, T)
            hk = []
            queue_ada(l)
            for s in range(8):
                r, w, tok = slab("mlp_w1", (l * 8 + s) * P * SLAB, 8, 512)

                def ev(fp, ps, k, s=s):
                    h = hT[:, 4 * s + 2 * fp:4 * s + 2 * fp + 2, :]
                    a = act(h, ps, ACT.Relu, k)
                    hk.append(tt(h, h, h, ALU.mult, a))
                    return a
                if s == 0:
                    gemm_f2(XT, w, tok, ev, xtok)
                else:
                    gemm_f(XT, w, tok, 4, ev)
                ring.give(r, pe_done())
                if s < 7:
                    step()
            bs = [bank.take() for _ in range(4)]
            kt = [None, None]
            for s in range(8):
                r, w, tok = slab("mlp_w2", (l * 8 + s) * P * SLAB, 4, 1024)
                if s < 7 + l:
                    step()
                for t in range(2):
                    for n in range(2):
                        b, ps, fr = bs[t * 2 + n]
                        for c in range(4):
                            mm(ps, hT[:, 4 * s + c, t * P:(t + 1) * P], w[:, c, n * 512:(n + 1) * 512],
                               s == 0 and c == 0, s == 7 and c == 3, fr, tok, hk[2 * s:2 * s + 2])
                    kt[t] = pe_done()
                ring.give(r, pe_done())
            return lambda t: add_rows(t, bs, kt)

        def add_rows(t, bs, kt):
            out_ = []
            for n in range(2):
                b, ps, fr = bs[t * 2 + n]
                x = X[:, t, n * 512:(n + 1) * 512]
                a = stt(x, x, ALPHA, ps, ALU.mult, ALU.add, kt[t])
                bank.give(b, a)
                out_.append(a)
            return out_

        def rope(ps, nh, ctab, stab, outs, tmp, tmpfree, *w):
            n = nh * 64
            a = tmp[:, 0:n].rearrange("p (h x) -> p h x", h=nh)
            b = tmp[:, n:2 * n].rearrange("p (h x) -> p h x", h=nh)
            cb = ctab.unsqueeze(1).to_broadcast([P, nh, 64])
            s1 = stab[:, 0:32].unsqueeze(1).to_broadcast([P, nh, 32])
            s2 = stab[:, 32:64].unsqueeze(1).to_broadcast([P, nh, 32])
            k1 = tt(a, ps, cb, ALU.mult, tmpfree, *w)
            k2 = tt(b[:, :, 0:32], ps[:, :, 32:64], s1, ALU.mult, tmpfree, *w)
            k3 = tt(b[:, :, 32:64], ps[:, :, 0:32], s2, ALU.mult, tmpfree, *w)
            ks = [tt(o, a, b, ALU.add, k1, k2, k3) for o in outs]
            return [k1, k2, k3], ks

        def attention(n, heads, sc, pr, ptb, st, lag=1, more=True):
            S = {}

            def scores(h):
                H = heads(h)
                b, ps, fr = bank.take()
                H["mm"](ps, fr)
                k = pe_done()
                i, s, sf = sc.take()
                n_ = H["width"]
                a = stt(s[:, 0:n_], ps[:, 0:n_], H["scale"], H["bias"], ALU.mult, ALU.add, k, sf, H.get("btok"))
                bank.give(b, a)
                q, sm, smf = st.take()
                if H["cols"][0] == (0, 256):
                    rs = [red(sm[:, 0:2], s.rearrange("p (t k) -> p t k", t=2), ALU.max, a, smf)]
                else:
                    rs = [red(sm[:, t:t + 1], s[:, o0:o1], ALU.max, a, smf) for t, (o0, o1) in enumerate(H["cols"])]
                sink = H.get("sink")
                if sink is not None:
                    x = sm[:, 0:2]
                    rs = [ts(x, x, sink, None, ALU.max, None, rs)]
                ng = ts(sm[:, 2:4], sm[:, 0:2], -1.0, None, ALU.mult, None, rs)
                es = []
                j, p_, pf = pr.take()
                for t in range(2):
                    o0, o1 = H["cols"][t]
                    es.append(act(p_[:, o0:o1], s[:, o0:o1], ACT.Exp, ng, pf, bias=sm[:, 2 + t:3 + t],
                                  acc=sm[:, 4 + t:5 + t]))
                    if sink is not None:
                        es.append(act(sm[:, 6 + t:7 + t], sink, ACT.Exp, ng, bias=sm[:, 2 + t:3 + t]))
                sc.give(i, es)
                S[h] = (H, j, p_, q, sm, es)

            def normalise(h):
                H, j, p_, q, sm, es = S[h]
                if H.get("sink") is not None:
                    es = [tt(sm[:, 4:6], sm[:, 4:6], sm[:, 6:8], ALU.add, es)]
                rc = recip(sm[:, 8:10], sm[:, 4:6], es)
                nk = []
                for t in range(2):
                    o0, o1 = H["cols"][t]
                    nk.append(ts(p_[:, o0:o1], p_[:, o0:o1], sm[:, 8 + t:9 + t], None, ALU.mult, None, rc))
                st.give(q, nk, es)
                S[h] = (H, j, p_, nk)

            def turn(h):
                H, j, p_, nk = S[h]
                b, ps, fr = bank.take()
                for (t, kc, c0) in H["blocks"]:
                    tr(ps[:, kc * T + t * P:kc * T + (t + 1) * P], p_[:, c0:c0 + P], fr, nk)
                k = pe_done()
                pr.give(j, k)
                m, pt, pf = ptb.take()
                if len(H["blocks"]) == 4:
                    kk = cp(pt, ps, k, pf, e="act")
                else:
                    kk = [cp(pt[:, 0:T], ps[:, 0:T], k, pf, e="act"), cp(pt[:, T + P:], ps[:, T + P:], k, pf, e="act")]
                bank.give(b, kk)
                S[h] = (H, m, pt, kk)

            def apply(h):
                H, m, pt, kk = S.pop(h)
                ptb.give(m, H["pv"](pt, kk))

            for i in range(n + lag + 1):
                if i < n:
                    scores(i)
                if 1 <= i <= n:
                    normalise(i - 1)
                step()
                if lag <= i < n + lag:
                    turn(i - lag)
                if more:
                    step()
                if i > lag:
                    apply(i - lag - 1)

        def att_bufs(lag=1):
            sc = Rot([arena.get(512) for _ in range(2)])
            pr = Rot([arena.get(512) for _ in range(lag + 2)])
            ptb = Rot([arena.get(512) for _ in range(2)])
            st = Rot([arena.get(16) for _ in range(3)])
            return sc, pr, ptb, st

        def general_experts(l, av, wc, arena_hid, main, extra):
            G = Queues(nc, ctx, f"_g{l}")
            gsem = [ctx.enter_context(nc.semaphore(f"s_gr{l}_{j}")) for j in range(3)]
            for e in ("pe", "act", "dve", "sp"):
                for x in main:
                    G.q[e].append(("wait", x[1], x[2]))
            w1, w3, w2 = [ringt[:, j * SLAB:(j + 1) * SLAB] for j in range(3)]
            w1v, w3v = (w.rearrange("p (c n) -> p c n", c=8) for w in (w1, w3))
            w2v = w2.rearrange("p (c n) -> p c n", c=4)
            s_ = arena_hid[0][0].rearrange("p (a b) -> p a b", a=2)
            hd = arena_hid[1][0].rearrange("p a b -> p (a b)").rearrange("p (a b) -> p a b", a=4)
            ld = {}
            hdone = None
            last = {}

            def gmm(o, a, b, st, sp_, *w):
                G.emit("pe", lambda g: g.matmul(o, lhsT=a, rhs=b, start=st, stop=sp_, skip_group_check=True), w, False)

            for e in range(NE):
                toks = []
                for j, (nm, dst) in enumerate((("exp_w1", w1), ("exp_w3", w3), ("exp_w2", w2))):
                    off = (l * NE + e) * P * SLAB
                    src = d[nm][off:off + P * SLAB].rearrange("(p f) -> p f", p=P)
                    if j in ld:
                        G.q["sp"].append(("wait", ld[j][1], ld[j][2]))
                    sem = gsem[j]
                    G.q["sp"].append(["dma", lambda g, dst=dst, src=src, sem=sem: g.dma_start(dst, src).then_inc(sem, 16),
                                      None, 0])
                    toks.append((f"gr{j}", sem, 16 * (e + 1)))
                hk = []
                for fp in range(2):
                    pa, pb = psb[2 * fp][:, :], psb[2 * fp + 1][:, :]
                    for ps, wv, tk_ in ((pa, w1v, toks[0]), (pb, w3v, toks[1])):
                        for j in range(2):
                            for c in range(8):
                                gmm(ps[:, j * T:(j + 1) * T], wv[:, c, 2 * fp + j:512:4], XT[:, c, :], c == 0, c == 7,
                                    tk_, last.get(fp))
                    kd = G.done("pe")
                    if fp == 1:
                        ld[0] = ld[1] = kd
                    pav = pa.rearrange("p (a b) -> p a b", a=2)
                    pbv = pb.rearrange("p (a b) -> p a b", a=2)
                    a = G.emit("act", lambda g, pav=pav: g.activation(s_, pav, ACT.Silu), [kd, last.get(1 - fp)])
                    o = hd[:, 2 * fp:2 * fp + 2, :]
                    last[fp] = G.emit("dve", lambda g, o=o, pbv=pbv: g.tensor_tensor(o, s_, pbv, ALU.mult),
                                      [a, kd, ld.get(2)])
                    hk.append(last[fp])
                for t in range(2):
                    for n in range(2):
                        ps = psb[4 + 2 * t + n][:, :]
                        for c in range(4):
                            gmm(ps, hd[:, c, t * P:(t + 1) * P], w2v[:, c, n * 512:(n + 1) * 512], c == 0, c == 3,
                                toks[2], hk, last.get((t, n)))
                ld[2] = kd = G.done("pe")
                for t in range(2):
                    for n in range(2):
                        ps = psb[4 + 2 * t + n][:, :]
                        o = av[:, t, n * 512:(n + 1) * 512]
                        wcol = wc[:, t, e:e + 1]
                        if e == 0:
                            fn = lambda g, o=o, ps=ps, wcol=wcol: g.tensor_scalar(o, ps, wcol, None, ALU.mult)
                        else:
                            fn = lambda g, o=o, ps=ps, wcol=wcol: g.scalar_tensor_tensor(
                                out=o, in0=ps, scalar=wcol, in1=o, op0=ALU.mult, op1=ALU.add)
                        last[t, n] = G.emit("dve", fn, [kd, last.get((t, n))])
            for e in ("pe", "act", "dve", "pool", "sp"):
                for f in ("pe", "act", "dve"):
                    G.q[e].append(("wait", G.sem[f], G.cnt[f]))
            col = flag[0:1, l:l + 1]
            for e in ("pe", "act", "dve", "pool", "sp"):
                Q.q[e].append(("wait", flag_wait[0][1], flag_wait[0][2]))
                Q.q[e].append(("branch", col, G.q[e]))

        flag_wait = [None]
        modc = [sb(f"modc{l}", [P, 512])[:, :] for l in range(2)]
        modk_ = [None, None]

        def queue_ada(l):
            acc = Rot([arena.get(512) for _ in range(2)])
            ab = arena.get(512)
            hold = {}

            def piece(s):
                if s == 0:
                    hold["b"] = bank.take()
                    hold["ab"] = pdma(ab[0:12, :], d["ada_b"][l * 12:l * 12 + 12, :], ada_free)
                if s < 12:
                    r, w, tok = slab("ada_w", (l * 12 + s) * P * SLAB, 8, 512)
                    i, m_, mf = acc.take()
                    k = ts(m_, w[:, 0, :], csil[:, 0:1], None, ALU.mult, None, tok, mf, ck, ada_free)
                    for c in range(1, 8):
                        k = stt(m_, w[:, c, :], csil[:, c:c + 1], m_, ALU.mult, ALU.add, k)
                    ring.give(r, k)
                    hold[s] = (i, m_, k)
                if s >= 1:
                    i, m_, k = hold.pop(s - 1)
                    b, ps, fr = hold["b"]
                    mm(ps[0:12, :], C["e12"][:, 12 - s:24 - s], m_, s == 1, s == 12, fr, k)
                    acc.give(i, pe_done())
                if s == 12:
                    b, ps, fr = hold["b"]
                    a = tt(modc[l][0:12, :], ps[0:12, :], ab[0:12, :], ALU.add, pe_done(), hold["ab"])
                    modk_[l] = a
                    bank.give(b, a)
            ada_free = all_done()
            for s in range(13):
                filler.append(lambda s=s: piece(s))

        xsem = ctx.enter_context(nc.semaphore("s_x"))
        isem = ctx.enter_context(nc.semaphore("s_ident"))
        xsrc = d["x"].rearrange("(t p) f -> p t f", p=P)
        Q.q["sp"].append(["dma", lambda e: e.dma_start(X, xsrc).then_inc(xsem, 16), None, 0])
        Q.q["sp"].append(["dma", lambda e: e.dma_start(C["ident"], d["const_ident"]).then_inc(isem, 16), None, 0])
        xl = ("x", xsem, 16)
        ct = {"ident": ("ident", isem, 16)}
        for name in sorted(consts, key=lambda n: n not in ("ropec", "ropes")):
            if name not in ("half", "ones", "ident") + LATE:
                ct[name] = pdma(C[name], d["const_" + name])
        ct["half"] = mset(C["half"], -0.5)
        onesk = mset(C["ones"], 1.0)
        ctoks = list(ct.values()) + [onesk]
        ck = pdma(small[:, 44:52], d["c"].rearrange("(p c) -> p c", c=8))
        csil = small[:, 52:60]
        kp = pdma(posi, d["positions"])
        gk = [pdma(GB[:, j, :], bcast(d[nm][0:1, :])) for j, nm in ((0, "ln1_g"), (1, "ln1_b"))]
        xtok = turn_rows(X, [[xl, ct["ident"]]] * 2)

        arena.pos = 0
        qT = arena.get(4, T)
        kT = arena.get(2, T)
        qbT = arena.get(4, T)
        kbT = arena.get(4, T)
        vA = arena.get(2, P)
        vB = arena.get(2, 512)
        OT = arena.get(8, T)
        qtok = arena.get(2, 512)
        kdup = arena.get(2, 256)
        sinkb = arena.get(8)
        rot_tmp = arena.get(1024)
        sk = pdma(sinkb, bcast(d["attn_sink"][0:1, :]))
        ro = [[]]
        qk = [None, None]
        kk = [None, None]

        r, w, tok = slab("attn_w_in", 0, 8, 512)

        def ev(t, ps, k):
            reads, ks = rope(ps.rearrange("p (h x) -> p h x", h=8), 8, C["ropec"][:, t * 64:t * 64 + 64],
                             C["ropes"][:, t * 64:t * 64 + 64],
                             [qtok[:, t, :].rearrange("p (h x) -> p h x", h=8)], rot_tmp, ro[0], k, ct["ropec"],
                             ct["ropes"])
            ro[0] = ks
            qk[t] = ks
            return reads
        gemm_t(XT, w, tok, 512, ev, by_t=xtok)
        ring.give(r, pe_done())
        ck = act(csil, small[:, 44:52], ACT.Silu, ck)
        r, w, tok = slab("attn_w_in", P * 4096, 8, 256)
        vk = []

        def ev(t, ps, k):
            kv = kdup[:, t, :].rearrange("p (g c x) -> p g c x", g=2, c=2)
            reads, ks = rope(ps[:, 0:128].rearrange("p (h x) -> p h x", h=2), 2, C["ropec"][:, t * 64:t * 64 + 64],
                             C["ropes"][:, t * 64:t * 64 + 64], [kv[:, :, 0, :], kv[:, :, 1, :]], rot_tmp, ro[0], k)
            ro[0] = ks
            kk[t] = ks
            a = cp(vA[:, t, :], ps[:, 128:256], k, reads, e="act")
            vk.append(a)
            return [reads, a]
        gemm_t(XT, w, tok, 256, ev, 8)
        ring.give(r, pe_done())
        bk = []
        bslab = {}

        def proj_b(j):
            if j in (0, 4, 8):
                bslab[0] = slab("attn_w_in", P * (6144 + 1024 * j), 8, 512)
            r, w, tok = bslab[0]
            b, ps, fr = bank.take()
            for c in range(8):
                if j < 8:
                    mm(ps[:, 0:T], w[:, c, (j % 4) * P:(j % 4 + 1) * P], XT[:, c, :], c == 0, c == 7, fr, tok)
                else:
                    mm(ps, XT[:, c, (j - 8) * P:(j - 7) * P], w[:, c, :], c == 0, c == 7, fr, tok)
            kd = pe_done()
            if j in (3, 7, 9):
                ring.give(r, kd)
            if j < 8:
                a = cp((qbT if j < 4 else kbT)[:, j % 4, :], ps[:, 0:T], kd, e="act")
                bk.append(a)
            else:
                a = cp(vB[:, j - 8, :], ps, kd, e="act")
                vk.append(a)
            bank.give(b, a)
        for j in range(10):
            filler.append(lambda j=j: proj_b(j))
        tk = []
        for t in range(2):
            tk += transpose_to(qT, lambda c, t=t: qtok[:, t, c * P:(c + 1) * P], 4, t, qk[t])
            tk += transpose_to(kT, lambda c, t=t: kdup[:, t, c * P:(c + 1) * P], 2, t, kk[t])

        bufs = att_bufs(2)
        obank = {}
        otk = []

        def heads(h):
            if h == 7:
                late["bias"] = load(d["attn_bias"].rearrange("(p f) -> p f", p=P), 8, 512)
            if h == 8:
                assert not filler
            if h == 11:
                late["ots"] = list(otk)
                assert len(otk) == 4
                late["w"] = slab("attn_w_out", 0, 4, 1024)
            if 11 <= h < 15:
                filler.append(lambda: out_a(h - 11))
            if h < 8:
                qa, ka, va = qT[:, h // 2, :], kT[:, h // 4, :], vA[:, :, 64 * (h // 4):64 * (h // 4) + 64]
            else:
                g = h - 8
                qa, ka, va = qbT[:, g // 2, :], kbT[:, g // 2, :], vB[:, :, 64 * g:64 * g + 64]
            p0 = 64 * (h % 2)

            def m(ps, fr):
                for t in range(2):
                    mm(ps[:, t * T:(t + 1) * T], qa[p0:p0 + 64, t * P:(t + 1) * P], ka[p0:p0 + 64, :], True, True,
                       fr, tk, bk)

            def pv(pt, k):
                if h % 2 == 0:
                    obank[0] = bank.take()
                b, ps, fr = obank[0]
                for kc in range(2):
                    mm(ps[p0:p0 + 64, 0:T], va[:, kc, :], pt[:, kc * T:(kc + 1) * T], kc == 0, kc == 1, fr, k, vk)
                kd = pe_done()
                if h % 2 == 1:
                    a = copy_any(OT[:, h // 2, :], ps[:, 0:T], kd)
                    otk.append(a)
                    bank.give(b, a)
                return kd
            H = dict(mm=m, pv=pv, width=512, scale=0.125, cols=[(0, 256), (256, 512)],
                     blocks=[(t, kc, t * T + kc * P) for kc in range(2) for t in range(2)])
            if h < 8:
                H["bias"], H["sink"] = C["maska"], sinkb[:, h:h + 1]
                H["btok"] = [sk, ctoks]
            else:
                H["bias"], H["btok"] = late["bias"][1][:, h - 8, :], late["bias"][2]
            return H
        mixb = []
        late = {}

        def out_a(q):
            r1, w1_, tok1 = late["w"]
            b, ps, fr = bank.take()
            mixb.append((b, ps))
            t, n = q // 2, q % 2
            for c in range(4):
                mm(ps, OT[:, c, t * P:(t + 1) * P], w1_[:, c, n * 512:(n + 1) * 512], c == 0, False, fr, tok1,
                   late["ots"])
            if q == 3:
                ring.give(r1, pe_done())
        attention(16, heads, *bufs, lag=2)
        flush()
        rb = late["bias"][0]
        ring.give(rb, Q.done("dve"))

        r1, w2_, tok1 = slab("attn_w_out", P * SLAB, 4, 1024)
        kt = [None, None]
        for q, (b, ps) in enumerate(mixb):
            t, n = q // 2, q % 2
            for c in range(4):
                mm(ps, OT[:, 4 + c, t * P:(t + 1) * P], w2_[:, c, n * 512:(n + 1) * 512], False, c == 3, tok1, otk)
            kt[t] = pe_done()
        ring.give(r1, pe_done())
        xtok = layer_norm(lambda t: add_rows(t, [m_ + (None,) for m_ in mixb], kt), gk)

        def next_gb(a, b, ia, ib, toks):
            return [pdma(GB[:, 0, :], bcast(d[a][ia:ia + 1, :]), toks),
                    pdma(GB[:, 1, :], bcast(d[b][ib:ib + 1, :]), toks)]

        gk = next_gb("ln2_g", "ln2_b", 0, 0, Q.done("dve"))
        barrier(WRITERS)
        xtok = layer_norm(mlp(0, xtok), gk)
        gk = next_gb("ln1_g", "ln1_b", 1, 1, Q.done("dve"))

        barrier(WRITERS)
        zT = arena.get(16, T)
        xcT = arena.get(32, T)
        xF = arena.get(2, 2048)
        xB = arena.get(2, 2048)
        pos0 = arena.pos
        prm = arena.get(32, 6)
        dd = arena.get(32)
        dtt = arena.get(2, 64)
        aa = arena.get(2, 64)
        dtb = arena.get(64)
        ang = arena.get(64)
        ups = Rot([arena.get(2, 260) for _ in range(2)])
        cvs = Rot([arena.get(2, T) for _ in range(2)])
        k1 = pdma(prm, d["ssm_conv"].rearrange("p (a b) -> p a b", a=32))
        k2 = pdma(dd, d["ssm_dn"])
        k3 = pdma(dtb, bcast(d["ssm_dt_bias"][0:1, :]))
        k4 = pdma(ang, bcast(d["ssm_A_log"][0:1, :]))
        zz = [ctoks] + [mset(u[:, :, 0:2], 0.0) for u in ups.bufs] + [mset(u[:, :, 258:260], 0.0) for u in ups.bufs]
        zk = []
        for s in range(4):
            r, w, tok = slab("ssm_w_in", s * P * SLAB, 8, 512)

            def ev(fp, ps, k, s=s):
                a = act(zT[:, 4 * s + 2 * fp:4 * s + 2 * fp + 2, :], ps, ACT.Silu, k)
                zk.append(a)
                return a
            if s == 0:
                gemm_f2(XT, w, tok, ev, xtok)
            else:
                gemm_f(XT, w, tok, 4, ev)
            ring.give(r, pe_done())
            if s == 0:
                r, w, tok = slab("ssm_w_dt", 0, 8, 64)
                dk = []

                def ev(t, ps, k):
                    a = tt(dtt[:, t, :], ps, dtb, ALU.add, k, k3)
                    dk.append(a)
                    return a
                gemm_t(XT, w, tok, 64, ev)
                ring.give(r, pe_done())
                k = ts(aa, dtt, -1.0, None, ALU.mult, None, dk)
                k = tt(aa, aa, dtt, ALU.min, k)
                k = act(aa, aa, ACT.Exp, k)
                k = act(aa, aa, ACT.Ln, k, bias=1.0)
                k = stt(dtt, dtt, 0.0, aa, ALU.max, ALU.add, k)
                ka = act(ang, ang, ACT.Exp, k4)
                ka = ts(ang, ang, -1.0, None, ALU.mult, None, ka)
                ak = tt(aa, dtt, ang.unsqueeze(1).to_broadcast([P, 2, 64]), ALU.mult, k, ka)
        xk = {}
        for s in range(8):
            r, w, tok = slab("ssm_w_in", (4 + s) * P * SLAB, 8, 512)

            def ev(fp, ps, k, s=s):
                f0 = 4 * s + 2 * fp
                i, u, uf = ups.take()
                a = cp(u[:, :, 2:258], ps, k, uf, zz, e="act")
                j, v, vf = cvs.take()
                lk = []
                for q in range(2):
                    f = f0 + q
                    kk_ = act(v[:, q, :], u[:, q, 0:T], ACT.Identity, a, vf, k1,
                              scale=prm[:, f, 0:1], bias=prm[:, f, 5:6])
                    for c in range(1, 5):
                        kk_ = stt(v[:, q, :], u[:, q, c:c + T], prm[:, f, c:c + 1], v[:, q, :], ALU.mult, ALU.add, kk_)
                    lk.append(kk_)
                ups.give(i, lk)
                o = act(xcT[:, f0:f0 + 2, :], v, ACT.Silu, lk)
                cvs.give(j, o)
                xk[f0] = xk[f0 + 1] = o
                return a
            gemm_f(XT, w, tok, 4, ev)
            ring.give(r, pe_done())
        xs_k = []
        for t in range(2):
            for g in range(4):
                b, ps, fr = bank.take()
                for j in range(4):
                    f = 4 * g + j
                    tr(ps[:, j * P:(j + 1) * P], xcT[:, f, t * P:(t + 1) * P], fr, xk[f])
                kd = pe_done()
                pv_ = ps.rearrange("p (h x) -> p h x", h=8)
                for o, dr in ((xF, 0), (xB, 1)):
                    ov = o[:, t, g * 512:(g + 1) * 512].rearrange("p (h x) -> p h x", h=8)
                    dv_ = dtt[:, t, dr * 32 + g * 8:dr * 32 + g * 8 + 8].unsqueeze(2).to_broadcast([P, 8, 64])
                    kl = tt(ov, pv_, dv_, ALU.mult, kd, ak)
                    xs_k.append(kl)
                bank.give(b, kl)
        arena.pos = pos0 + 192 + 32 + 128 + 128 + 64 + 64
        barrier_pos = arena.pos
        pre = all_done()
        cbr = Rot([arena.get(768) for _ in range(2)])
        lmr = Rot([arena.get(2, 3, P) for _ in range(2)])
        emr = Rot([arena.get(768) for _ in range(3)])
        cb_of = {}

        def cb_group(g):
            b, ps, fr = bank.take()
            BT, CT = xcT[:, 16 + g, :], xcT[:, 24 + g, :]
            for s in range(2):
                mm(ps[:, s * T:(s + 1) * T], BT[:, s * P:(s + 1) * P], CT, True, True, fr, xk[16 + g], xk[24 + g])
            kd = pe_done()
            i, cb, cf = cbr.take()
            ks = [tt(cb[:, 0:T], ps[:, 0:T], C["leo"], ALU.mult, kd, cf, pre),
                  tt(cb[:, T:T + P], ps[:, T + P:], C["leo"][:, 0:P], ALU.mult, kd),
                  tt(cb[:, 384:512], ps[:, 0:P], C["oge"][:, P:], ALU.mult, kd),
                  tt(cb[:, 512:768], ps[:, T:], C["oge"], ALU.mult, kd)]
            bank.give(b, ks)
            cb_of[g] = (i, cb, ks)

        LE, GE = C["leo"][:, 0:P], C["oge"][:, P:]
        E_of = {}

        def build_l(h):
            i, L, lf = lmr.take()
            cf_, cb_ = slice(h, h + 1), slice(32 + h, 33 + h)
            k_ = [ts(L[:, 0, 0, :], C["gt"], aa[:, 0, cf_], None, ALU.mult, None, lf, ak, pre),
                  ts(L[:, 0, 1, :], C["gt"], aa[:, 1, cf_], None, ALU.mult, None),
                  ts(L[:, 1, 0, :], C["lt"], aa[:, 0, cb_], None, ALU.mult, None),
                  ts(L[:, 1, 1, :], C["lt"], aa[:, 1, cb_], None, ALU.mult, None)]
            L_of[h] = (i, L, k_)
        L_of = {}

        def decay(h):
            i, L, k_ = L_of.pop(h)
            j, E, ef = emr.take()
            ek = []
            b, ps, fr = bank.take()
            mm(ps[:, 0:T], L[:, 0, 0, :], C["leo"], True, False, fr, k_)
            mm(ps[:, P:T], aa[:, 1, h:h + 1].to_broadcast([P, P]), LE, False, True)
            mm(ps[:, T:T + P], L[:, 0, 1, :], LE, True, True)
            a = act(E[:, 0:384], ps[:, 0:384], ACT.Exp, pe_done(), ef, pre)
            bank.give(b, a)
            ek.append(a)
            b, ps, fr = bank.take()
            mm(ps[:, 0:P], L[:, 1, 0, :], GE, True, True, fr)
            mm(ps[:, P:384], L[:, 1, 1, :], C["oge"], True, False)
            mm(ps[:, P:T], aa[:, 0, 32 + h:33 + h].to_broadcast([P, P]), GE, False, True)
            kd = pe_done()
            lmr.give(i, kd)
            a = act(E[:, 384:768], ps[:, 0:384], ACT.Exp, kd)
            bank.give(b, a)
            ek.append(a)
            E_of[h] = (j, E, ek)

        def weigh(h):
            j, E, ek = E_of[h]
            ci, cb, cks = cb_of[h // 4]
            mk = tt(E, E, cb, ALU.mult, ek, cks)
            if h % 4 == 3:
                cbr.give(ci, mk)
            E_of[h] = (j, E, mk)

        yk = []
        ybk = {}

        def ssm_out(h):
            j, E, mk = E_of.pop(h)
            p0 = 64 * (h % 2)
            if h % 2 == 0:
                ybk[0] = bank.take()
            b, ps, fr = ybk[0]
            o = ps[p0:p0 + 64, :]
            hs = slice(h * 64, h * 64 + 64)
            mm(o[:, 0:T], xF[:, 0, hs], E[:, 0:T], True, False, fr, mk, xs_k)
            mm(o[:, P:T], xF[:, 1, hs], E[:, T:384], False, False)
            mm(o[:, 0:P], xB[:, 0, hs], E[:, 384:512], False, False)
            mm(o[:, 0:T], xB[:, 1, hs], E[:, 512:768], False, True)
            kd = pe_done()
            emr.give(j, kd)
            if h % 2 == 1:
                f = h // 2
                a = stt(xcT[:, f, :], xcT[:, f, :], dd[:, f:f + 1], ps[:, 0:T], ALU.mult, ALU.add, kd, k2)
                bank.give(b, a)
                yk.append(tt(zT[:, f, :], xcT[:, f, :], zT[:, f, :], ALU.mult, a, zk))

        nrm, normed = {}, [[] for _ in range(4)]

        def norm_a(g):
            z2 = zT[:, 2 * g:2 * g + 2, :]
            nrm[g] = tt(xcT[:, 2 * g:2 * g + 2, :], z2, z2, ALU.mult, yk[-2:])

        def norm_b(g):
            b, ps, fr = bank.take()
            for c in range(2):
                mm(ps[:, 0:T], C["ones"], xcT[:, 2 * g + c, :], c == 0, c == 1, fr, nrm[g])
            v = xcT[:, 2 * g, :]
            a = act(v, ps[:, 0:T], ACT.Ln, pe_done(), k_eps, scale=1.0 / 256, bias=epst)
            bank.give(b, a)
            nrm[g] = act(v, v, ACT.Exp, a, scale=-0.5)

        def norm_c(g):
            for f in (2 * g, 2 * g + 1):
                normed[g // 2].append(stt(zT[:, f, :], zT[:, f, :], dd[:, 16 + f:17 + f], xcT[:, 2 * g, :], ALU.mult,
                                          ALU.mult, nrm[g]))
        epst = small[:, 180:181]
        k_eps = mset(epst, 1e-5)
        build_l(0)
        for i in range(36):
            if i < 32:
                if i % 4 == 0:
                    cb_group(i // 4)
                if i < 31:
                    build_l(i + 1)
                decay(i)
            if 1 <= i <= 32:
                weigh(i - 1)
            if 2 <= i < 34:
                ssm_out(i - 2)
            if i >= 5 and i % 4 == 1:
                norm_a((i - 5) // 4)
            if i >= 6 and i % 4 == 2 and (i - 6) // 4 < 8:
                norm_b((i - 6) // 4)
            if i >= 7 and i % 4 == 3 and (i - 7) // 4 < 8:
                norm_c((i - 7) // 4)
        bs = [bank.take() for _ in range(4)]
        kt = [None, None]
        for s in range(4):
            r, w, tok = slab("ssm_w_out", s * P * SLAB, 4, 1024)
            for t in range(2):
                for n in range(2):
                    b, ps, fr = bs[t * 2 + n]
                    for c in range(4):
                        mm(ps, zT[:, 4 * s + c, t * P:(t + 1) * P], w[:, c, n * 512:(n + 1) * 512],
                           s == 0 and c == 0, s == 3 and c == 3, fr, tok, normed[s])
                kt[t] = pe_done()
            ring.give(r, pe_done())
        xtok = layer_norm(lambda t: add_rows(t, bs, kt), gk)
        gk = next_gb("ln2_g", "ln2_b", 1, 1, Q.done("dve"))

        barrier(WRITERS)
        for name in LATE:
            C[name] = arena.get(consts[name])
        ctoks = [pdma(C[name], d["const_" + name]) for name in ("cm", "dmask")]
        arena.base = arena.pos
        ctab = C["rope2c"]
        stab = C["rope2s"]
        posf = small[:, 40:42]
        k = cp(posf, posi, kp)
        MOD = arena.get(6, D)
        mbase = arena.pos
        gb = arena.get(24)
        xbase = arena.pos
        hrows = arena.ap[:, xbase:xbase + 2 * D].rearrange("p (t f) -> p t f", t=2)
        arena.pos = xbase + 12 * T
        GN = arena.get(2, D)
        A = arena.get(2, 32)
        Bk = arena.get(2, 32)
        for t in range(2):
            k = ts(A[:, t, :], C["inv"], posf[:, t:t + 1], None, ALU.mult, None, k)
        MAGIC = 12582912.0
        k = ts(Bk, A, float(1.0 / (2 * np.pi)), MAGIC, ALU.mult, ALU.add, k)
        k = ts(Bk, Bk, MAGIC, None, ALU.subtract, None, k)
        for cst in (6.28125, 0.0019350051879882812, 3.019916050995584e-07):
            k = stt(A, Bk, -cst, A, ALU.mult, ALU.add, k)
        PI = 3.1415925
        k = ts(A, A, PI, -PI, ALU.min, ALU.max, k)
        sv = stab.rearrange("p (t x) -> p t x", t=2)
        cv = ctab.rearrange("p (t x) -> p t x", t=2)
        k5 = act(sv[:, :, 32:64], A, ACT.Sin, k)
        k6 = ts(sv[:, :, 0:32], sv[:, :, 32:64], -1.0, None, ALU.mult, None, k5)
        k = ts(A, A, float(np.pi / 2), None, ALU.add, None, k5)
        k = ts(Bk, A, float(np.pi), float(-2 * np.pi), ALU.is_gt, ALU.mult, k)
        k = tt(A, A, Bk, ALU.add, k)
        k = ts(A, A, PI, -PI, ALU.min, ALU.max, k)
        k7 = act(cv[:, :, 0:32], A, ACT.Sin, k)
        k8 = cp(cv[:, :, 32:64], cv[:, :, 0:32], k7)
        ropek = [k6, k7, k8]

        def rms(src, nf, o, tokw, w_):
            js = arena.get(nf)
            ks = []
            pk = None
            for t in range(2):
                pk = act(js, src(t), ACT.Square, tokw, pk, acc=o[:, t:t + 1])
                ks.append(pk)
            return rsqrt_small(o, o, 1.0 / nf, 1e-6, ks, w_)

        modk = {}
        gains = {}

        def spread(l, s, w_):
            b, ps, fr = bank.take()
            mm(ps, C["ident"][0:12, s:s + 1].to_broadcast([12, P]), modc[l][0:12, :], True, True, fr, modk_[l])
            a = cp(MOD[:, s // 2, (s % 2) * 512:(s % 2) * 512 + 512], ps, pe_done(), w_, e="act")
            bank.give(b, a)
            modk[s] = a

        def gain(i, g, gk):
            gains[i] = stt(MOD[:, i, :], MOD[:, i, :], 1.0, g, ALU.add, ALU.mult, modk[2 * i], modk[2 * i + 1], gk)

        def norm_mod(si, gi, rows, hh):
            rs = small[:, 60:62]
            ks = []
            for t in range(2):
                k = act(hh[:, t, :], X[:, t, :], ACT.Square, rows(t), acc=rs[:, t:t + 1])
                k = rsqrt_small(rs[:, t:t + 1], rs[:, t:t + 1], 1.0 / D, 1e-6, k)
                a = stt(hh[:, t, :], X[:, t, :], rs[:, t:t + 1], MOD[:, gi, :], ALU.mult, ALU.mult, k, gains[gi])
                ks.append(tt(hh[:, t, :], hh[:, t, :], MOD[:, si, :], ALU.add, a, modk[2 * si], modk[2 * si + 1]))
            return turn_rows(hh, ks), ks

        gnk = [pdma(GN[:, j, :], bcast(d[nm][0:1, :])) for j, nm in ((0, "norm1_g"), (1, "norm2_g"))]
        kgb = pdma(gb, d["gate_b"][0:P, :])
        filler.append(lambda: [spread(0, s, None) for s in range(6)])
        filler.append(lambda: [spread(0, s, None) for s in range(6, 12)] + [gain(1, GN[:, 0, :], gnk), gain(4, GN[:, 1, :], gnk)])
        rows_of = mlp(1, xtok)
        flush()
        ln_gk = gk
        htok, _ = norm_mod(0, 1, lambda t: ln_block(t, rows_of(t), ln_gk), hrows)

        for l in range(2):
            assert not filler
            arena.pos = xbase
            yT = [arena.get(4, T) for _ in range(3)]
            gT = arena.get(24, T)
            work = arena.pos
            gtk = {}
            gslab = {}

            def gate(q):
                if q % 4 == 0:
                    gslab[0] = slab("gate_w", (l * 6 + q // 4) * P * SLAB, 8, 512)
                r, w, tok = gslab[0]
                b, ps, fr = bank.take()
                for c in range(8):
                    mm(ps[:, 0:T], w[:, c, (q % 4) * P:(q % 4 + 1) * P], XT[:, c, :], c == 0, c == 7, fr, tok, htok)
                kd = pe_done()
                if q % 4 == 3:
                    ring.give(r, kd)
                a = act(gT[:, q, :], ps[:, 0:T], ACT.Exp, kd, ngb, bias=gb[:, q:q + 1], scale=-1.0)
                bank.give(b, a)

                def rest():
                    k = ts(gT[:, q, :], gT[:, q, :], 1.0, None, ALU.add, None, a)
                    gtk[q] = recip(gT[:, q, :], gT[:, q, :], k)
                after.append(rest)
            ngb = ts(gb, gb, -1.0, None, ALU.mult, None, kgb)
            if l:
                for s0 in (4, 8):
                    filler.append(lambda s0=s0: [spread(1, s, mod_free) for s in range(s0, s0 + 4)])
            for q in range(24):
                filler.append(lambda q=q: gate(q))
            rqk = arena.get(2, 512)
            rqT = arena.get(2, T)
            rkT = arena.get(2, T)
            rv = arena.get(2, 512)
            rg = arena.get(2, 512)
            tmp = arena.get(1024)
            ra_pos = arena.pos
            woff = l * P * (7 * 4096 - 8 * 60)
            ro[0] = []
            qk2 = [None, None]
            r, w, tok = slab("w_in2", woff, 8, 512)

            def ev(t, ps, k):
                reads, ks = rope(ps.rearrange("p (h x) -> p h x", h=8), 8, ctab[:, t * 64:t * 64 + 64],
                                 stab[:, t * 64:t * 64 + 64],
                                 [rqk[:, t, :].rearrange("p (h x) -> p h x", h=8)], tmp, ro[0], k, ropek)
                ro[0] = ks
                qk2[t] = ks
                return reads
            gemm_t(XT, w, tok, 512, ev, by_t=htok)
            ring.give(r, pe_done())
            rvk, rgk = [], []
            r, w, tok = slab("w_in2", woff + P * 4096, 8, 512)

            def ev(t, ps, k):
                a = copy_any(rv[:, t, :], ps, k)
                rvk.append(a)
                return a
            gemm_t(XT, w, tok, 512, ev)
            ring.give(r, pe_done())
            r, w, tok = slab("w_in2", woff + P * 8192, 8, 512)

            def ev(t, ps, k):
                a = act(rg[:, t, :], ps, ACT.Silu, k)
                rgk.append(a)
                return a
            gemm_t(XT, w, tok, 512, ev)
            ring.give(r, pe_done())
            tk = []
            for t in range(2):
                tk += transpose_to(rqT, lambda c, t=t: rqk[:, t, c * P:(c + 1) * P], 2, t, qk2[t])
                tk += transpose_to(rkT, lambda c, t=t: rqk[:, t, 256 + c * P:256 + (c + 1) * P], 2, t, qk2[t])
            smr = Rot([arena.get(384) for _ in range(2)])
            ob = [bank.take() for _ in range(2)]
            for h in range(4):
                p0 = 64 * (h % 2)
                b, ps, fr = bank.take()
                kh, qh = rkT[p0:p0 + 64, h // 2, :], rqT[p0:p0 + 64, h // 2, :]
                mm(ps[:, 0:T], kh[:, 0:P], qh, True, True, fr, tk)
                mm(ps[:, T:384], kh[:, P:T], qh[:, P:T], True, True)
                i, s_, sf = smr.take()
                a = tt(s_, ps[:, 0:384], C["dmask"][:, h * 384:(h + 1) * 384], ALU.mult, pe_done(), sf, ctoks)
                bank.give(b, a)
                step()
                hs = slice(h * P, h * P + P)
                mm(ob[0][1][:, hs], s_[:, 0:P], rv[:, 0, hs], True, True, ob[0][2], a, rvk)
                mm(ob[1][1][:, hs], s_[:, P:T], rv[:, 0, hs], True, False, ob[1][2])
                mm(ob[1][1][:, hs], s_[:, T:384], rv[:, 1, hs], False, True)
                smr.give(i, pe_done())
            kd = pe_done()
            step()
            st8 = small[:, 64:112].rearrange("p (a b) -> p a b", a=8)
            mv8 = small[:, 112:128].rearrange("p (a b) -> p a b", a=8)
            rs8 = small[:, 128:136]
            ks = []
            for t in range(2):
                for h in range(4):
                    q = t * 4 + h
                    o, i_ = st8[:, q, :], ob[t][1][:, h * P:(h + 1) * P]
                    k = Q.emit("dve", lambda e, o=o, i_=i_: e.bn_stats(o, i_), [kd])
                    o2, i2 = mv8[:, q, :], st8[:, q, :]
                    ks.append(Q.emit("dve", lambda e, o2=o2, i2=i2: e.bn_aggr(o2, i2), [k]))
            k = rsqrt_small(rs8, mv8[:, :, 1], 1.0, 1e-6, ks)
            yak, yin = [], []
            for t in range(2):
                lk = []
                for h in range(4):
                    q = t * 4 + h
                    lk.append(ts(rqk[:, t, h * P:(h + 1) * P], ob[t][1][:, h * P:(h + 1) * P], mv8[:, q, 0:1],
                                 rs8[:, q:q + 1], ALU.subtract, ALU.mult, k, tk))
                bank.give(ob[t][0], lk)
                yin.append(tt(rqk[:, t, :], rqk[:, t, :], rg[:, t, :], ALU.mult, lk, rgk))
            step(4)
            for t in range(2):
                yak += transpose_to(yT[0], lambda c, t=t: rqk[:, t, c * P:(c + 1) * P], 4, t, yin[t])
            barrier(WRITERS)
            arena.pos = work
            misc = arena.get(2, 452)
            fqT = arena.get(4, T)
            fkT = arena.get(4, T)
            fv = arena.get(2, 512)
            lf = arena.get(2, 4)
            fbb = arena.get(4)
            bufs = att_bufs()
            fmr = Rot([arena.get(384) for _ in range(2)])
            kfb = pdma(fbb, bcast(d["fox_fb"][l:l + 1, :]))
            fk_ = []
            FS = float(128 ** -0.5)
            r, w, tok = slab("w_in2", woff + P * 3 * 4096, 8, 512)

            def ev(fp, ps, k):
                a = act(fqT[:, 2 * fp:2 * fp + 2, :], ps, ACT.Copy, k, scale=FS)
                fk_.append(a)
                return a
            gemm_f(XT, w, tok, 4, ev)
            ring.give(r, pe_done())
            r, w, tok = slab("w_in2", woff + P * 4 * 4096, 8, 512)

            def ev(fp, ps, k):
                a = copy_any(fkT[:, 2 * fp:2 * fp + 2, :], ps, k)
                fk_.append(a)
                return a
            gemm_f(XT, w, tok, 4, ev)
            ring.give(r, pe_done())
            r, w, tok = slab("w_in2", woff + P * 5 * 4096, 8, 512)
            fvk, mk_ = [], []

            def ev(t, ps, k):
                a = copy_any(fv[:, t, :], ps, k)
                fvk.append(a)
                return a
            gemm_t(XT, w, tok, 512, ev)
            ring.give(r, pe_done())
            r, w, tok = slab("w_in2", woff + P * 6 * 4096, 8, 452)

            def ev(t, ps, k):
                a = copy_any(misc[:, t, :], ps, k)
                mk_.append(a)
                return a
            gemm_t(XT, w, tok, 452, ev)
            ring.give(r, pe_done())
            lt_ = small[:, 140:148].rearrange("p (t h) -> p t h", t=2)
            k = tt(lf, misc[:, :, 0:4], fbb.unsqueeze(1).to_broadcast([P, 2, 4]), ALU.add, mk_, kfb)
            k = ts(lt_, lf, -1.0, None, ALU.mult, None, k)
            k = tt(lt_, lt_, lf, ALU.min, k)
            k = act(lt_, lt_, ACT.Exp, k)
            k = act(lt_, lt_, ACT.Ln, k, bias=1.0)
            lfk = stt(lf, lf, 0.0, lt_, ALU.min, ALU.subtract, k)
            CB = [(0, 128), (128, 384)]
            CBL = [(0, 0, 0), (1, 0, 128), (1, 1, 256)]
            ytk = [yak, [], []]

            def causal_pv(br, v, vtok):
                def make(h):
                    def pv(pt, k):
                        b, ps, fr = bank.take()
                        hs = slice(h * P, h * P + P)
                        mm(ps[:, 0:T], v[:, 0, hs], pt[:, 0:T], True, False, fr, k, vtok)
                        mm(ps[:, P:T], v[:, 1, hs], pt[:, T + P:2 * T], False, True)
                        kd = pe_done()
                        a = copy_any(yT[br][:, h, :], ps[:, 0:T], kd)
                        ytk[br].append(a)
                        bank.give(b, a)
                        return kd
                    return pv
                return make

            mkpv = causal_pv(1, fv, fvk)
            step()

            def heads(h):
                i, F, ff = fmr.take()
                a = [ts(F[:, 0:P], C["gt"], lf[:, 0, h:h + 1], None, ALU.mult, None, ff, lfk),
                     ts(F[:, P:T], C["ones"], lf[:, 1, h:h + 1], None, ALU.mult, None),
                     ts(F[:, T:384], C["gt"], lf[:, 1, h:h + 1], None, ALU.mult, None)]

                def m(ps, fr):
                    mm(ps[:, 0:P], fqT[:, h, 0:P], fkT[:, h, 0:P], True, False, fr, fk_)
                    mm(ps[:, 0:P], LE, F[:, 0:P], False, True, a)
                    mm(ps[:, P:384], fqT[:, h, P:T], fkT[:, h, :], True, False)
                    mm(ps[:, P:T], C["ones"], F[:, 0:P], False, False)
                    mm(ps[:, P:384], LE, F[:, P:384], False, True)
                    fmr.give(i, pe_done())
                return dict(mm=m, pv=mkpv(h), width=384, scale=1.0, cols=CB, blocks=CBL, bias=C["cm"], btok=ctoks)
            attention(4, heads, *bufs, more=False)
            barrier()
            arena.pos = work + 904
            qnT = arena.get(4, T)
            knT = arena.get(4, T)
            vM = arena.get(2, 512)
            qpT = arena.get(2, T)
            kpT = arena.get(1, T)
            arena_keep = arena.pos
            lat = arena.get(2, 384)
            latT = arena.get(3, T)
            gq = arena.get(384)
            qpt = arena.get(2, T)
            kpt = arena.get(2, P)
            tmp = arena.get(512)
            kg1 = pdma(gq[:, 0:256], bcast(d["mla_q_g"][l:l + 1, :]))
            kg2 = pdma(gq[:, 256:384], bcast(d["mla_kv_g"][l:l + 1, :]))
            rs_q, rs_k = small[:, 160:162], small[:, 162:164]
            kq = rms(lambda t: misc[:, t, 4:260], 256, rs_q, [], [])
            kkv = rms(lambda t: misc[:, t, 260:388], 128, rs_k, [], [])
            step()
            lk = []
            for t in range(2):
                lk.append([stt(lat[:, t, 0:256], misc[:, t, 4:260], rs_q[:, t:t + 1], gq[:, 0:256], ALU.mult,
                               ALU.mult, kq, kg1),
                           stt(lat[:, t, 256:384], misc[:, t, 260:388], rs_k[:, t:t + 1], gq[:, 256:384], ALU.mult,
                               ALU.mult, kkv, kg2)])
            ltk = []
            kpk = [None, None]
            ro[0] = []
            for t in range(2):
                ltk += transpose_to(latT, lambda c, t=t: lat[:, t, c * P:(c + 1) * P], 3, t, lk[t])
                kv = kpt[:, t, :].rearrange("p (c x) -> p c x", c=2)
                reads, ks = rope(misc[:, t, 388:452].unsqueeze(1), 1, ctab[:, t * 64:t * 64 + 64],
                                 stab[:, t * 64:t * 64 + 64], [kv[:, 0:1, :], kv[:, 1:2, :]], tmp, ro[0])
                ro[0] = ks
                kpk[t] = ks
            r, w, tok = slab("wq_up", l * P * 1536, 2, 768)
            MS = float(192 ** -0.5)
            for h in range(0, 4, 2):
                b, ps, fr = bank.take()
                for j in range(2):
                    for c in range(2):
                        mm(ps[:, j * T:(j + 1) * T], w[:, c, (h + j) * 192:(h + j) * 192 + P], latT[:, c, :],
                           c == 0, c == 1, fr, tok, ltk)
                a = act(qnT[:, h:h + 2, :], ps.rearrange("p (a b) -> p a b", a=2), ACT.Copy, pe_done(), scale=MS)
                bank.give(b, a)
                fk_.append(a)
            wv = w.rearrange("p c (h x) -> p c h x", h=4)
            qpk = [None, None]
            for t in range(2):
                b, ps, fr = bank.take()
                for c in range(2):
                    mm(ps[:, 0:T].rearrange("p (h x) -> p h x", h=4), latT[:, c, t * P:(t + 1) * P],
                       wv[:, c, :, 128:192], c == 0, c == 1, fr, tok, ltk)
                reads, ks = rope(ps[:, 0:T].rearrange("p (h x) -> p h x", h=4), 4, ctab[:, t * 64:t * 64 + 64],
                                 stab[:, t * 64:t * 64 + 64],
                                 [qpt[:, t, :].rearrange("p (h x) -> p h x", h=4)], tmp, ro[0], pe_done())
                ks = [ts(qpt[:, t, :], qpt[:, t, :], MS, None, ALU.mult, None, ks)]
                ro[0] = ks
                qpk[t] = ks
                bank.give(b, reads)
            ring.give(r, pe_done())
            r, w, tok = slab("wkv_up", l * P * 1024, 1, 1024)
            for h in range(0, 4, 2):
                b, ps, fr = bank.take()
                for j in range(2):
                    mm(ps[:, j * T:(j + 1) * T], w[:, 0, (h + j) * 256:(h + j) * 256 + P], latT[:, 2, :],
                       True, True, fr, tok, ltk)
                a = copy_any(knT[:, h:h + 2, :], ps.rearrange("p (a b) -> p a b", a=2), pe_done())
                bank.give(b, a)
                fk_.append(a)
            wv = w.rearrange("p c (h x) -> p c h x", h=4)
            vmk = []
            for t in range(2):
                b, ps, fr = bank.take()
                mm(ps.rearrange("p (h x) -> p h x", h=4), latT[:, 2, t * P:(t + 1) * P], wv[:, 0, :, 128:256],
                   True, True, fr, tok, ltk)
                a = copy_any(vM[:, t, :], ps, pe_done())
                bank.give(b, a)
                vmk.append(a)
            ring.give(r, pe_done())
            for t in range(2):
                fk_ += transpose_to(qpT, lambda c, t=t: qpt[:, t, c * P:(c + 1) * P], 2, t, qpk[t])
                fk_ += transpose_to(kpT, lambda c, t=t: kpt[:, t, :], 1, t, kpk[t])
            mkpv = causal_pv(2, vM, vmk)
            step()
            barrier()
            arena.pos = arena_keep
            bufs = att_bufs()

            def heads(h):
                p0 = 64 * (h % 2)
                qp, kp_ = qpT[p0:p0 + 64, h // 2, :], kpT[p0:p0 + 64, 0, :]

                def m(ps, fr):
                    mm(ps[:, 0:P], qnT[:, h, 0:P], knT[:, h, 0:P], True, False, fr)
                    mm(ps[:, 0:P], qp[:, 0:P], kp_[:, 0:P], False, True)
                    mm(ps[:, P:384], qnT[:, h, P:T], knT[:, h, :], True, False)
                    mm(ps[:, P:384], qp[:, P:T], kp_, False, True)
                return dict(mm=m, pv=mkpv(h), width=384, scale=1.0, cols=CB, blocks=CBL, bias=C["cm"], btok=ctoks)
            attention(4, heads, *bufs, more=False)
            barrier()
            arena.pos = work
            flush()
            if l:
                gain(4, GB[:, 1, :], gbk)
            mg = arena.get(8, T)
            tb = Rot([arena.get(2, T) for _ in range(2)])
            mgk = {}
            for br in range(3):
                r, w, tok = slab("branch_w", (l * 3 + br) * P * SLAB, 4, 1024)

                def ev(fp, ps, k, br=br):
                    f0 = 2 * fp
                    m_ = mg[:, f0:f0 + 2, :]
                    g_ = gT[:, br * 8 + f0:br * 8 + f0 + 2, :]
                    gk_ = [gtk[br * 8 + f0], gtk[br * 8 + f0 + 1]]
                    if br == 0:
                        mgk[f0] = tt(m_, ps, g_, ALU.mult, k, gk_)
                        return mgk[f0]
                    i, t_, tf = tb.take()
                    a = tt(t_, ps, g_, ALU.mult, k, gk_, tf)
                    mgk[f0] = tt(m_, m_, t_, ALU.add, a, mgk[f0])
                    tb.give(i, mgk[f0])
                    return a
                gemm_f(yT[br], w, tok, 8, ev, 4, ytk[br])
                ring.give(r, pe_done())
            ot = Rot([arena.get(512) for _ in range(2)])
            rk = []
            extra = [arena.ap[:, xbase + j * SLAB:xbase + (j + 1) * SLAB] for j in range(2)]
            assert xbase + 2 * SLAB <= work
            for x_ in extra:
                ring.add(x_, all_done())

            sl = [slab("out_w", (l * 2 + n) * P * SLAB, 8, 512) for n in range(2)]
            ob = {}
            for t in range(2):
                for n in range(2):
                    b, ps, fr = bank.take()
                    for c in range(8):
                        mm(ps, mg[:, c, t * P:(t + 1) * P], sl[n][1][:, c, :], c == 0, c == 7, fr, sl[n][2],
                           list(mgk.values()))
                    ob[t, n] = (b, ps, pe_done())
            for n in range(2):
                ring.give(sl[n][0], pe_done())

            def gated_rows(t):
                out_ = []
                for n in range(2):
                    b, ps, k = ob[t, n]
                    i, o, of = ot.take()
                    a = tt(o, ps, MOD[:, 2, n * 512:(n + 1) * 512], ALU.mult, k, of, modk[4 + n])
                    bank.give(b, a)
                    x = X[:, t, n * 512:(n + 1) * 512]
                    a = tt(x, x, o, ALU.add, a)
                    ot.give(i, a)
                    out_.append(a)
                return out_

            H2 = MOD[:, 0:2, :]
            hv = H2.rearrange("p t (q c) -> p t q c", c=8)
            htok, hk_ = norm_mod(3, 4, gated_rows, H2)
            moe_start = barrier()
            hn_done = moe_start
            if l == 0:
                gbk = next_gb("norm1_g", "norm2_g", 1, 1, moe_start)
                kgb = pdma(gb, d["gate_b"][P:2 * P, :], moe_start)
            else:
                gbk = pdma(GB[:, 0, :], bcast(d["final_g"][0:1, :]), moe_start)
            av = MOD[:, 3:5, :]
            arena.pos = xbase + 2 * SLAB
            code = arena.get(2, 32)
            msk = arena.get(2, 32)
            ex = arena.get(2, 12)
            wc = arena.get(2, 32)
            rb_ = arena.get(36)
            lg = arena.get(2, 36)
            pr_ = arena.get(2, 8)
            m1 = arena.get(2, 8)
            m2 = arena.get(2, 8)
            tm = arena.get(2, 32)
            sel = arena.get(2, 8)
            gm = arena.get(2, 4)
            s4 = arena.get(2, 16)
            krb = pdma(rb_, bcast(d["router_b"][l:l + 1, :]))
            r, w, tok = slab("router_w", l * P * 288, 8, 36)
            lk = []

            def ev(t, ps, k):
                a = tt(lg[:, t, :], ps, rb_, ALU.add, k, krb)
                lk.append(a)
                return a
            gemm_t(XT, w, tok, 36, ev, by_t=htok)
            ring.give(r, pe_done())

            def bc2(x, n):
                return x.to_broadcast([P, 2, n])

            def first_max(x, n, mask, mx, w_):
                k = red(mx, x, ALU.max, w_)
                k = tt(mask, x, bc2(mx, n), ALU.is_equal, k)
                k = tt(mask, mask, C["desc"][:, 0:n].unsqueeze(1).to_broadcast([P, 2, n]), ALU.mult, k)
                k = red(s4[:, :, 15:16], mask, ALU.max, k)
                return tt(mask, mask, bc2(s4[:, :, 15:16], n), ALU.is_equal, k)

            def four(x):
                return x.rearrange("p t (g e) -> p t g e", g=4)

            def per_group(x):
                return x.unsqueeze(3).to_broadcast([P, 2, 4, 8])

            def per_expert(x):
                return x.unsqueeze(2).to_broadcast([P, 2, 4, 8])

            k = first_max(lg[:, :, 0:4], 4, gm, s4[:, :, 0:1], lk)
            k = tt(four(tm), four(lg[:, :, 4:36]), per_group(gm), ALU.mult, k)
            k = red(sel, tm.rearrange("p t (g e) -> p t e g", g=4), ALU.add, k)
            ksel = first_max(sel, 8, m1, s4[:, :, 1:2], k)
            k = stt(pr_, m1, -3e38, sel, ALU.mult, ALU.add, ksel)
            k = first_max(pr_, 8, m2, s4[:, :, 2:3], k)
            kb_ = tt(m1, m1, m2, ALU.add, k)
            mk = tt(four(msk), per_group(gm), per_expert(m1), ALU.mult, kb_)
            b, ps, fr = bank.take()
            mm(ps[:, 0:32], C["lt"], msk[:, 0, :], True, True, fr, mk)
            mm(ps[:, 32:64], C["ones"], msk[:, 0, :], True, False)
            mm(ps[:, 32:64], C["lt"], msk[:, 1, :], False, True)
            mm(ps[:, 64:96], C["ones"], msk[:, 0, :], True, False)
            mm(ps[:, 64:96], C["ones"], msk[:, 1, :], False, True)
            kd = pe_done()
            k = stt(code, ps[:, 0:64].rearrange("p (t e) -> p t e", t=2), 1.0, msk, ALU.add, ALU.mult, kd)
            ck_ = ts(code, code, -1.0, None, ALU.add, None, k)
            kf = red(small[:, 170:171], ps[:, 64:96], ALU.max, kd)
            bank.give(b, kf, k)
            flag_k = ts(flag[:, l:l + 1], small[:, 170:171], float(CAP), None, ALU.is_gt, None, kf)
            k = tt(ex[:, :, 0:4], lg[:, :, 0:4], bc2(s4[:, :, 0:1], 4), ALU.subtract, lk)
            k = tt(ex[:, :, 4:12], sel, bc2(s4[:, :, 1:2], 8), ALU.subtract, ksel)
            k = act(ex, ex, ACT.Exp, k)
            k1 = red(s4[:, :, 3:4], ex[:, :, 0:4], ALU.add, k)
            k2 = red(s4[:, :, 4:5], ex[:, :, 4:12], ALU.add, k)
            k = recip(s4[:, :, 5:7], s4[:, :, 3:5], k1, k2)
            k = tt(pr_, ex[:, :, 4:12], bc2(s4[:, :, 6:7], 8), ALU.mult, k)
            k = tt(pr_, pr_, m1, ALU.mult, k)
            k = red(s4[:, :, 7:8], pr_, ALU.add, k)
            k = recip(s4[:, :, 8:9], s4[:, :, 7:8], k)
            k = tt(pr_, pr_, bc2(s4[:, :, 8:9], 8), ALU.mult, k)
            k = tt(pr_, pr_, bc2(s4[:, :, 5:6], 8), ALU.mult, k)
            wk = tt(four(wc), per_group(gm), per_expert(pr_), ALU.mult, k)

            pselr = Rot([arena.get(2, P) for _ in range(2)])
            pwr = Rot([arena.get(2, P) for _ in range(1)])
            pwtr = Rot([arena.get(T) for _ in range(2)])
            xgr = Rot([arena.get(8, P) for _ in range(2)])
            sr_ = Rot([arena.get(512) for _ in range(2)])
            hr_ = Rot([arena.get(512) for _ in range(2)])
            htr = Rot([arena.get(4, P) for _ in range(2)])
            yr = Rot([arena.get(D) for _ in range(2)])
            G_, W_, Y_ = {}, {}, {}
            avk = {}

            def gather(i):
                q, pl, pf = pselr.take()
                k = tt(pl.rearrange("p t (e s) -> p t e s", e=2),
                       C["iota"].unsqueeze(1).unsqueeze(1).to_broadcast([P, 2, 2, CAP]),
                       code[:, :, 2 * i:2 * i + 2].unsqueeze(3).to_broadcast([P, 2, 2, CAP]), ALU.is_equal, ck_, pf)
                v, pw, wf = pwr.take()
                kw = tt(pw.rearrange("p t (e s) -> p t e s", e=2), pl.rearrange("p t (e s) -> p t e s", e=2),
                        wc[:, :, 2 * i:2 * i + 2].unsqueeze(3).to_broadcast([P, 2, 2, CAP]), ALU.mult, k, wk, wf)
                m, xg, xf = xgr.take()
                ks = []
                for c0 in (0, 4):
                    b, ps, fr = bank.take()
                    for c in range(c0, c0 + 4):
                        for t in range(2):
                            mm(ps[:, (c - c0) * P:(c - c0 + 1) * P], hv[:, t, :, c], pl[:, t, :], t == 0, t == 1,
                               fr, k, hk_)
                    a = cp(xg[:, c0:c0 + 4, :], ps.rearrange("p (a b) -> p a b", a=4), pe_done(), xf, e="act")
                    bank.give(b, a)
                    ks.append(a)
                pselr.give(q, pe_done(), kw)
                b, ps, fr = bank.take()
                for t in range(2):
                    tr(ps[:, t * P:(t + 1) * P], pw[:, t, :], fr, kw)
                kd = pe_done()
                pwr.give(v, kd)
                u, pt, pf2 = pwtr.take()
                a = cp(pt, ps[:, 0:T], kd, pf2)
                bank.give(b, a)
                G_[i] = (m, xg, ks)
                W_[i] = (u, pt, a)

            def inner(i):
                m, xg, ks = G_.pop(i)
                e0 = l * NE + 2 * i
                L1 = [slab("exp_w1", (e0 + j) * P * SLAB, 8, 512) for j in range(2)]
                L3 = [slab("exp_w3", (e0 + j) * P * SLAB, 8, 512) for j in range(2)]
                outs = []
                for L in (L1, L3):
                    b, ps, fr = bank.take()
                    for c in range(8):
                        for j in range(2):
                            mm(ps[64 * j:64 * j + 64, :], xg[:, c, 64 * j:64 * j + 64], L[j][1][:, c, :], c == 0,
                               c == 7, fr, ks, L[0][2], L[1][2] if j else None)
                    kd = pe_done()
                    ring.give(L[0][0], kd)
                    ring.give(L[1][0], kd)
                    outs.append((b, ps, kd))
                xgr.give(m, kd)
                (ba, pa, ka), (bb, pb, kb) = outs
                q, s_, sf = sr_.take()
                a = act(s_, pa, ACT.Silu, ka, sf)
                bank.give(ba, a)
                v, h_, hf = hr_.take()
                a2 = tt(h_, s_, pb, ALU.mult, a, kb, hf)
                bank.give(bb, a2)
                sr_.give(q, a2)
                return v, h_, a2

            def turn_h(H_):
                v, h_, hk2 = H_
                b, ps, fr = bank.take()
                for f in range(4):
                    tr(ps[:, f * P:(f + 1) * P], h_[:, f:512:4], fr, hk2)
                kd = pe_done()
                hr_.give(v, kd)
                q, ht, hf = htr.take()
                a = cp(ht, ps.rearrange("p (a b) -> p a b", a=4), kd, hf)
                bank.give(b, a)
                return q, ht, a

            def outer(i, HT_):
                q, ht, hk2 = HT_
                e0 = l * NE + 2 * i
                L2 = [slab("exp_w2", (e0 + j) * P * SLAB, 4, 1024) for j in range(2)]
                bs = [bank.take() for _ in range(2)]
                for f in range(4):
                    for j in range(2):
                        for n in range(2):
                            mm(bs[n][1][64 * j:64 * j + 64, :], ht[:, f, 64 * j:64 * j + 64],
                               L2[j][1][:, f, n * 512:(n + 1) * 512], f == 0, f == 3, bs[n][2], hk2, L2[0][2],
                               L2[1][2] if j else None)
                kd = pe_done()
                ring.give(L2[0][0], kd)
                ring.give(L2[1][0], kd)
                htr.give(q, kd)
                v, y, yf = yr.take()
                ks = []
                for n in range(2):
                    a = cp(y[:, n * 512:(n + 1) * 512], bs[n][1], kd, yf, e="act")
                    bank.give(bs[n][0], a)
                    ks.append(a)
                Y_[i] = (v, y, ks)

            def combine(i):
                v, y, ks = Y_.pop(i)
                u, pt, kp_ = W_.pop(i)
                for t in range(2):
                    for n in range(2):
                        b, ps, fr = bank.take()
                        mm(ps, pt[:, t * P:(t + 1) * P], y[:, n * 512:(n + 1) * 512], True, True, fr, ks, kp_)
                        o = av[:, t, n * 512:(n + 1) * 512]
                        if i == 0:
                            a = cp(o, ps, pe_done(), hn_done)
                        else:
                            a = tt(o, o, ps, ALU.add, pe_done(), avk[t, n])
                        avk[t, n] = a
                        bank.give(b, a)
                yr.give(v, pe_done())
                pwtr.give(u, pe_done())

            gather(0)
            for i in range(NE // 2):
                H_ = inner(i)
                if i >= 1:
                    combine(i - 1)
                if i + 1 < NE // 2:
                    gather(i + 1)
                HT_ = turn_h(H_)
                outer(i, HT_)
            combine(NE // 2 - 1)
            ring.cut(NRING)
            barrier()
            moe_end = all_done()
            flag_wait[0] = flag_k
            general_experts(l, av, wc, arena_hid=(sr_.bufs, xgr.bufs), main=moe_end, extra=extra)
            end = barrier()

            def expert_rows(t):
                a = tt(av[:, t, :], av[:, t, :], MOD[:, 5, :], ALU.mult, end)
                return tt(X[:, t, :], X[:, t, :], av[:, t, :], ALU.add, a)
            if l == 0:
                for s in range(4):
                    spread(1, s, end)
                gain(1, GB[:, 0, :], gbk)
                htok, mod_free = norm_mod(0, 1, expert_rows, hrows)

        rs = small[:, 60:62]
        fk = []
        for t in range(2):
            k = act(hrows[:, t, :], X[:, t, :], ACT.Square, expert_rows(t), acc=rs[:, t:t + 1])
            k = rsqrt_small(rs[:, t:t + 1], rs[:, t:t + 1], 1.0 / D, 1e-6, k)
            fk.append(stt(X[:, t, :], X[:, t, :], rs[:, t:t + 1], GB[:, 0, :], ALU.mult, ALU.mult, k, gbk))

        block = ctx.enter_context(nc.Block())

        def run(queue, eng, name):
            for n, rec in enumerate(queue):
                if rec[0] == "wait":
                    eng.wait_ge(rec[1], rec[2])
                elif rec[0] == "branch":
                    reg = eng.alloc_register(f"{name}_flag{n}")
                    eng.reg_load(reg, rec[1])
                    with eng.If_ne(reg, 0):
                        run(rec[2], eng, name)
                else:
                    ins = rec[1](eng)
                    if rec[2] is not None:
                        ins.then_inc(rec[2], rec[3])

        @block.sync
        def _(eng):
            run(Q.q["sp"], eng, "sp")
            for t in range(2):
                eng.wait_ge(fk[t][1], fk[t][2])
                eng.dma_start(out[t * P:(t + 1) * P, :], X[:, t, :]).then_inc(osem, 16)
            eng.wait_ge(osem, 32)

        @block.gpsimd
        def _(eng):
            run(Q.q["pool"], eng, "pool")

        @block.scalar
        def _(eng):
            run(Q.q["act"], eng, "act")

        @block.vector
        def _(eng):
            run(Q.q["dve"], eng, "dve")

        @block.tensor
        def _(eng):
            run(Q.q["pe"], eng, "pe")


def constants():
    i = np.arange(P)[:, None]
    j = np.arange(P)[None, :]
    f = np.float32
    one = np.ones((P, P), f)
    c = {}
    c["ident"] = np.eye(P, dtype=f)
    c["ones"] = None
    c["half"] = None
    c["gt"] = (i > j).astype(f)
    c["lt"] = (i < j).astype(f)
    c["leo"] = np.concatenate([(i <= j).astype(f), one], 1)
    c["oge"] = np.concatenate([one, (i >= j).astype(f)], 1)
    k = np.arange(T)[None, :]
    c["maska"] = np.concatenate([np.where(np.abs(i + t * P - k) <= 128, 0.0, NEG) for t in range(2)], 1).astype(f)
    tri = np.where(j <= i, 0.0, NEG)
    c["cm"] = np.concatenate([tri, np.zeros((P, P)), tri], 1).astype(f)
    inv = 10000.0 ** (-np.arange(32, dtype=np.float64) / 32)
    c["inv"] = np.broadcast_to(inv.astype(f)[None], (P, 32)).copy()
    ang = (np.arange(T, dtype=f)[:, None] * inv.astype(f)[None, :]).astype(f).astype(np.float64)
    co, si = np.cos(ang), np.sin(ang)
    ct = np.concatenate([co, co], 1).reshape(2, P, 64).transpose(1, 0, 2).reshape(P, 128)
    st = np.concatenate([-si, si], 1).reshape(2, P, 64).transpose(1, 0, 2).reshape(P, 128)
    c["ropec"], c["ropes"] = ct.astype(f), st.astype(f)
    dm = []
    for h in range(4):
        lg = np.log1p(-np.exp2(-5.0 - h))
        q = np.arange(T)[None, :]
        m0 = np.where(q >= i, np.exp(lg * np.maximum(q - i, 0)), 0.0)
        q1 = np.arange(P)[None, :]
        m1 = np.where(q1 >= i, np.exp(lg * np.maximum(q1 - i, 0)), 0.0)
        dm.append(np.concatenate([m0, m1], 1) * 0.125)
    c["dmask"] = np.concatenate(dm, 1).astype(f)
    c["iota"] = np.broadcast_to(np.arange(CAP, dtype=f)[None], (P, CAP)).copy()
    c["e12"] = np.zeros((P, 24), f)
    c["e12"][:, 11] = 1.0
    c["desc"] = np.broadcast_to((8 - np.arange(8)).astype(f)[None], (P, 8)).copy()
    return c


CONST_WIDTH = {"ident": 128, "ones": 128, "half": 8, "gt": 128, "lt": 128, "leo": 256, "oge": 256, "maska": 512,
               "cm": 384, "inv": 32, "ropec": 128, "ropes": 128, "dmask": 1536, "desc": 8, "e12": 24, "iota": CAP, "rope2c": 128,
               "rope2s": 128}


def pc(w, cuts):
    k, n = w.shape
    v = w.reshape(P, k // P, n)
    out, a = [], 0
    for m in cuts:
        out.append(v[:, :, a:a + m].reshape(-1))
        a += m
    assert a == n
    return np.concatenate(out)


def cpw(w, cuts):
    k, n = w.shape
    return pc(np.ascontiguousarray(w.reshape(k // P, P, n).transpose(1, 0, 2)).reshape(k, n), cuts)


def cpk(w, kc):
    k, n = w.shape
    return np.ascontiguousarray(w.reshape(k // (kc * P), kc, P, n).transpose(0, 2, 1, 3)).reshape(-1)


def kernel(**inputs):
    import numpy as _np
    import concourse.bacc as _bacc
    from concourse import mybir as _mybir
    from concourse.bass_utils import run_bass_kernel_spmd as _run

    g = {k: _np.asarray(v) for k, v in inputs.items()}
    a = {}
    a["x"] = g["x"].reshape(T, D)
    a["attn_w_in"] = pc(g["attn_w_in"][0], [512, 256, 512, 512, 512])
    a["attn_sink"] = g["attn_sink"]
    q = _np.arange(T)
    r_, c_ = q // 64, q % 64
    cs = _np.clip(c_ - 8, 0, 48)
    ok = (c_[None, :] >= cs[:, None]) & (c_[None, :] < cs[:, None] + 16)
    dr = r_[None, :] - r_[:, None] + 7
    dc = _np.clip(c_[None, :] - c_[:, None] + 15, 0, 30)
    idx = _np.where(ok, dr * 31 + dc, 15 * 31)
    rp = _np.concatenate([g["attn_rpb"][0].reshape(8, 465), _np.full((8, 1), NEG, _np.float32)], 1)
    bias = rp[:, idx.reshape(-1)].reshape(8, 2, P, T)
    a["attn_bias"] = _np.ascontiguousarray(bias.transpose(2, 0, 1, 3)).reshape(-1)
    a["attn_w_out"] = cpk(g["attn_w_out"][0], 4)
    a["ssm_w_in"] = pc(g["ssm_w_in"][0][:, 0:6144], [512] * 12)
    a["ssm_w_dt"] = pc(g["ssm_w_in"][0][:, 6144:], [64])
    cw = g["ssm_conv_w"][0].reshape(5, 32, P).transpose(2, 1, 0)
    cb = g["ssm_conv_b"][0].reshape(32, P).T[:, :, None]
    a["ssm_conv"] = _np.concatenate([cw, cb], 2).reshape(P, 192)
    dsk = _np.repeat(g["ssm_D"][0], 64).reshape(16, P).T
    a["ssm_dn"] = _np.concatenate([dsk, g["ssm_norm_w"][0].reshape(16, P).T], 1)
    a["ssm_dt_bias"] = g["ssm_dt_bias"]
    a["ssm_A_log"] = g["ssm_A_log"].reshape(1, 64)
    a["ssm_w_out"] = cpk(g["ssm_w_out"][0], 4)
    a["mlp_w1"] = _np.concatenate([pc(g["mlp_w1"][l], [512] * 8) for l in range(2)])
    a["mlp_w2"] = _np.concatenate([cpk(g["mlp_w2"][l], 4) for l in range(2)])
    for n in ("ln1_g", "ln1_b", "ln2_g", "ln2_b"):
        a[n] = g[n]
    a["c"] = g["c_2"].reshape(-1)
    a["positions"] = g["positions_2"].reshape(2, P).T
    a["ada_w"] = _np.concatenate([pc(g["ada_w_2"][l], [512] * 12) for l in range(2)])
    a["ada_b"] = g["ada_b_2"].reshape(24, 512)
    a["norm1_g"], a["norm2_g"], a["final_g"] = g["norm1_g_2"], g["norm2_g_2"], g["final_g_2"].reshape(1, D)
    a["w_in2"] = _np.concatenate([pc(g["w_in_2"][l], [512] * 6 + [452]) for l in range(2)])
    a["fox_fb"] = g["fox_fb_2"]
    a["mla_q_g"], a["mla_kv_g"] = g["mla_q_norm_g_2"], g["mla_kv_norm_g_2"]
    a["wq_up"] = _np.concatenate([cpw(g["mla_wq_up_2"][l], [768]) for l in range(2)])
    a["wkv_up"] = _np.concatenate([cpw(g["mla_wkv_up_2"][l], [1024]) for l in range(2)])
    a["gate_w"] = _np.concatenate([pc(g["gate_w_2"][l], [512] * 6) for l in range(2)])
    a["gate_b"] = _np.concatenate([g["gate_b_2"][l].reshape(24, P).T for l in range(2)])
    a["branch_w"] = _np.concatenate([cpk(g["branch_w_2"][l, b], 4) for l in range(2) for b in range(3)])
    a["out_w"] = _np.concatenate([cpw(g["out_w_2"][l], [512, 512]) for l in range(2)])
    a["router_w"] = _np.concatenate(
        [pc(_np.concatenate([g["router_grp_w_2"][l], g["router_exp_w_2"][l]], 1), [36]) for l in range(2)])
    a["router_b"] = _np.concatenate([g["router_grp_b_2"], g["router_exp_b_2"]], 1)
    a["exp_w1"] = g["exp_w1_2"].reshape(-1)
    a["exp_w3"] = g["exp_w3_2"].reshape(-1)
    a["exp_w2"] = g["exp_w2_2"].reshape(-1)
    for n, v in constants().items():
        if v is not None:
            a["const_" + n] = v

    nc = _bacc.Bacc("TRN2", target_bir_lowering=False, num_devices=1)
    arrays, args = {}, {}
    for name, v in a.items():
        v = _np.ascontiguousarray(v)
        arrays[f"in_{name}"] = v
        args[name] = nc.dram_tensor(f"in_{name}", v.shape, _mybir.dt.from_np(v.dtype), kind="ExternalInput").ap()
    out = nc.dram_tensor("out_0", (T, D), _mybir.dt.float32, kind="ExternalOutput").ap()
    build(nc, args, out, CONST_WIDTH)
    r = _run(nc, [arrays], core_ids=[0])
    return r.results[0]["out_0"].reshape(1, T, D)
```
